# Optimizing a Trainium2 kernel written in Bass

```python
import jax, jax.numpy as jnp
from jax import lax
import numpy as np

D_MODEL = 1024
BATCH = 1
SEQ = 256
DEPTH = 2
DEC_BATCH = 8
DEC_SEQ = 8
PAST_LEN = 256
PAGE_SIZE = 128

MIX_WIDTH = D_MODEL
N_MIXERS = 4
GROUP_WIDTH = MIX_WIDTH // N_MIXERS
HEAD_DIM = 64
ATT_HEADS = GROUP_WIDTH // HEAD_DIM
MOBA_BLOCK = 256
MOBA_TOP_K = 3
QUERY_BLOCK = 128
POOL_WINDOWS = (2, 4, 8, 16)
POOL_GROUP = GROUP_WIDTH // len(POOL_WINDOWS)
POOL_HIST = max(POOL_WINDOWS) - 1
CONV_WIDTH = 31
CONV_HIST = CONV_WIDTH - 1
GMLP_CHUNK = 128
GMLP_HEADS = 4
GMLP_HEAD_DIM = GROUP_WIDTH // GMLP_HEADS
IN_COLS = 3 * GROUP_WIDTH + GROUP_WIDTH + 2 * GROUP_WIDTH + 2 * GROUP_WIDTH
FFN_DIM = ((8 * D_MODEL // 3 + 127) // 128) * 128
RMS_EPS = 1e-6
LN_EPS = 1e-5

kernel_name = 'hymba_moba_pool_conv_gmlp_step'

def rmsnorm(x, gain):
    xf = x.astype(jnp.float32)
    y = xf * lax.rsqrt(jnp.mean(xf * xf, axis=-1, keepdims=True) + RMS_EPS)
    return (y * gain.astype(jnp.float32)).astype(x.dtype)

def layernorm(x, gain, bias):
    xf = x.astype(jnp.float32)
    mu = jnp.mean(xf, axis=-1, keepdims=True)
    var = jnp.mean(jnp.square(xf - mu), axis=-1, keepdims=True)
    y = (xf - mu) * lax.rsqrt(var + LN_EPS)
    return (y * gain.astype(jnp.float32) + bias.astype(jnp.float32)).astype(x.dtype)

def swiglu(x, w_gate, w_up, w_down):
    return (jax.nn.silu(x @ w_gate) * (x @ w_up)) @ w_down

def alibi_slopes(n_heads):
    return jnp.exp2(-8.0 * jnp.arange(1, n_heads + 1, dtype=jnp.float32) / n_heads)

def moba_attention(q, k_all, v_all, pos0):
    B, T, H, Dh = q.shape
    L = k_all.shape[1]
    n_blk = -(-L // MOBA_BLOCK)
    pad = n_blk * MOBA_BLOCK - L
    kb = jnp.pad(k_all, ((0, 0), (0, pad), (0, 0), (0, 0))).reshape(B, n_blk, MOBA_BLOCK, H, Dh).transpose(0, 3, 1, 2, 4)
    vb = jnp.pad(v_all, ((0, 0), (0, pad), (0, 0), (0, 0))).reshape(B, n_blk, MOBA_BLOCK, H, Dh).transpose(0, 3, 1, 2, 4)
    k_mean = jnp.mean(kb.astype(jnp.float32), axis=3)
    slopes = alibi_slopes(H)
    scale = Dh ** -0.5
    bi = jnp.arange(B)[:, None, None]
    hi = jnp.arange(H)[None, None, :]
    blk_ids = jnp.arange(n_blk, dtype=jnp.int32)
    offs = jnp.arange(MOBA_BLOCK, dtype=jnp.int32)
    n_slots = MOBA_TOP_K + 1

    def attend(args):
        q_c, pos_c = args
        tc = q_c.shape[1]
        own = pos_c // MOBA_BLOCK
        gate = jnp.einsum('bthd,bhnd->bthn', q_c.astype(jnp.float32), k_mean)
        past = (blk_ids[None, :] < own[:, None])[None, :, None, :]
        gate = jnp.where(past, gate, -jnp.inf)
        if n_blk < MOBA_TOP_K:
            gate = jnp.pad(gate, ((0, 0), (0, 0), (0, 0), (0, MOBA_TOP_K - n_blk)), constant_values=-jnp.inf)
        top_val, top_idx = lax.top_k(gate, MOBA_TOP_K)
        sel_ok = jnp.isfinite(top_val)
        top_idx = jnp.minimum(top_idx, n_blk - 1)
        own_idx = jnp.broadcast_to(own[None, :, None], (B, tc, H))
        slots = [top_idx[..., s] for s in range(MOBA_TOP_K)] + [own_idx]
        scores = []
        for s in range(n_slots):
            idx = slots[s]
            k_sel = kb[bi, hi, idx]
            sc = jnp.einsum('bthd,bthjd->bthj', q_c, k_sel, preferred_element_type=jnp.float32) * scale
            key_pos = idx[..., None] * MOBA_BLOCK + offs
            sc = sc - slopes[:, None] * (pos_c[None, :, None, None] - key_pos).astype(jnp.float32)
            if s < MOBA_TOP_K:
                valid = sel_ok[..., s, None]
            else:
                valid = key_pos <= pos_c[None, :, None, None]
            scores.append(jnp.where(valid, sc, -jnp.inf))
        probs = jax.nn.softmax(jnp.concatenate(scores, axis=-1), axis=-1)
        probs = probs.astype(v_all.dtype).reshape(B, tc, H, n_slots, MOBA_BLOCK)
        out = jnp.einsum('bthj,bthjd->bthd', probs[..., 0, :], vb[bi, hi, slots[0]], preferred_element_type=jnp.float32)
        for s in range(1, n_slots):
            out = out + jnp.einsum('bthj,bthjd->bthd', probs[..., s, :], vb[bi, hi, slots[s]], preferred_element_type=jnp.float32)
        return out.astype(q_c.dtype)

    tc = QUERY_BLOCK if T % QUERY_BLOCK == 0 else T
    nq = T // tc
    pos = pos0 + jnp.arange(T, dtype=jnp.int32)
    qs = q.reshape(B, nq, tc, H, Dh).transpose(1, 0, 2, 3, 4)
    out = lax.map(attend, (qs, pos.reshape(nq, tc)))
    return out.transpose(1, 0, 2, 3, 4).reshape(B, T, H * Dh)

def pool_mixer(u_hist, u_new, pool_w, pool_scale):
    B, T, C = u_new.shape
    n_hist = u_hist.shape[1]
    u_cat = jnp.concatenate([u_hist, u_new], axis=1)
    u = u_cat.astype(jnp.float32)
    csum = jnp.concatenate([jnp.zeros((B, 1, C), jnp.float32), jnp.cumsum(u, axis=1)], axis=1)
    win = jnp.repeat(jnp.array(POOL_WINDOWS, dtype=jnp.int32), C // len(POOL_WINDOWS))
    idx = n_hist + jnp.arange(T, dtype=jnp.int32)
    start = jnp.maximum(idx[:, None] + 1 - win[None, :], 0)
    prev = jnp.take_along_axis(csum, jnp.broadcast_to(start[None], (B, T, C)), axis=1)
    count = jnp.minimum(idx[:, None] + 1, win[None, :]).astype(jnp.float32)
    m = (csum[:, n_hist + 1:] - prev) / count - u[:, n_hist:]
    m = m.astype(u_new.dtype).reshape(B, T, len(POOL_WINDOWS), C // len(POOL_WINDOWS))
    out = jnp.einsum('btgc,gcd->btgd', m, pool_w).reshape(B, T, C) * pool_scale
    return out, u_cat[:, -POOL_HIST:]

def conv_module(a_hist, c_in, conv_w, conv_b, ln_g, ln_b, conv_pw):
    a, g = jnp.split(c_in, 2, axis=-1)
    a = a * jax.nn.sigmoid(g)
    full = jnp.concatenate([a_hist, a], axis=1)
    C = a.shape[-1]
    y = lax.conv_general_dilated(full, conv_w[:, None, :], window_strides=(1,), padding='VALID',
                                 dimension_numbers=('NWC', 'WIO', 'NWC'), feature_group_count=C) + conv_b
    y = jax.nn.silu(layernorm(y, ln_g, ln_b))
    return y @ conv_pw, full[:, -CONV_HIST:]

def spatial_gating(d_in, gate_gain, spatial_w, spatial_b):
    B, T, _ = d_in.shape
    u, v = jnp.split(jax.nn.gelu(d_in), 2, axis=-1)
    v = rmsnorm(v, gate_gain)
    n_chunk = -(-T // GMLP_CHUNK)
    vp = jnp.pad(v, ((0, 0), (0, n_chunk * GMLP_CHUNK - T), (0, 0)))
    vp = vp.reshape(B, n_chunk, GMLP_CHUNK, GMLP_HEADS, GMLP_HEAD_DIM)
    w_causal = spatial_w * jnp.tril(jnp.ones((GMLP_CHUNK, GMLP_CHUNK), spatial_w.dtype))
    s = jnp.einsum('gts,bcsgd->bctgd', w_causal, vp) + spatial_b.T[None, None, :, :, None]
    s = s.reshape(B, n_chunk * GMLP_CHUNK, GROUP_WIDTH)[:, :T]
    return u * s, v

def hybrid_layer(x, pos0, k_past, v_past, pool_hist, conv_hist,
                 ffn1_norm, ffn1_w_gate, ffn1_w_up, ffn1_w_down, mix_norm, w_in, q_norm, k_norm,
                 pool_w, pool_scale, conv_w, conv_b, conv_ln_g, conv_ln_b, conv_pw,
                 gate_norm, spatial_w, spatial_b, w_out, ffn2_norm, ffn2_w_gate, ffn2_w_up, ffn2_w_down):
    B, T, _ = x.shape
    G = GROUP_WIDTH
    x = x + 0.5 * swiglu(rmsnorm(x, ffn1_norm), ffn1_w_gate, ffn1_w_up, ffn1_w_down)
    z = rmsnorm(x, mix_norm) @ w_in
    q, k, v, p_in, c_in, d_in = jnp.split(z, [G, 2 * G, 3 * G, 4 * G, 6 * G], axis=-1)
    q = rmsnorm(q.reshape(B, T, ATT_HEADS, HEAD_DIM), q_norm)
    k = rmsnorm(k.reshape(B, T, ATT_HEADS, HEAD_DIM), k_norm)
    v = v.reshape(B, T, ATT_HEADS, HEAD_DIM)
    att = moba_attention(q, jnp.concatenate([k_past, k], axis=1), jnp.concatenate([v_past, v], axis=1), pos0)
    pool, pool_state = pool_mixer(pool_hist, p_in, pool_w, pool_scale)
    conv, conv_state = conv_module(conv_hist, c_in, conv_w, conv_b, conv_ln_g, conv_ln_b, conv_pw)
    gmlp, gate_v = spatial_gating(d_in, gate_norm, spatial_w, spatial_b)
    x = x + jnp.concatenate([att, pool, conv, gmlp], axis=-1) @ w_out
    x = x + 0.5 * swiglu(rmsnorm(x, ffn2_norm), ffn2_w_gate, ffn2_w_up, ffn2_w_down)
    return x, k, v, pool_state, conv_state, gate_v

def setup_inputs(seed: int = 0) -> dict:
    key = jax.random.key(seed)
    keys = iter(jax.random.split(key, 32))

    def nrm(shape, scale):
        return scale * jax.random.normal(next(keys), shape, jnp.float32)

    n_pages = PAST_LEN // PAGE_SIZE
    n_used = DEC_BATCH * n_pages
    n_pool = (n_used * 5) // 4
    G = GROUP_WIDTH
    page_table = jax.random.permutation(next(keys), n_pool)[:n_used].reshape(DEC_BATCH, n_pages).astype(jnp.int32)
    return {
        'x_prompt': nrm((BATCH, SEQ, D_MODEL), 1.0),
        'x_sample': nrm((DEC_BATCH, DEC_SEQ, D_MODEL), 1.0),
        'cache_k': nrm((DEPTH, n_pool, PAGE_SIZE, ATT_HEADS, HEAD_DIM), 1.0),
        'cache_v': nrm((DEPTH, n_pool, PAGE_SIZE, ATT_HEADS, HEAD_DIM), 1.0),
        'state_pool': nrm((DEPTH, DEC_BATCH, POOL_HIST, G), 1.0),
        'state_conv': nrm((DEPTH, DEC_BATCH, CONV_HIST, G), 0.5),
        'page_table': page_table,
        'ffn1_norm': 1.0 + nrm((DEPTH, D_MODEL), 0.05),
        'ffn1_w_gate': nrm((DEPTH, D_MODEL, FFN_DIM), D_MODEL ** -0.5),
        'ffn1_w_up': nrm((DEPTH, D_MODEL, FFN_DIM), D_MODEL ** -0.5),
        'ffn1_w_down': nrm((DEPTH, FFN_DIM, D_MODEL), FFN_DIM ** -0.5),
        'mix_norm': 1.0 + nrm((DEPTH, D_MODEL), 0.05),
        'w_in': nrm((DEPTH, D_MODEL, IN_COLS), D_MODEL ** -0.5),
        'q_norm': 1.0 + nrm((DEPTH, HEAD_DIM), 0.05),
        'k_norm': 1.0 + nrm((DEPTH, HEAD_DIM), 0.05),
        'pool_w': nrm((DEPTH, len(POOL_WINDOWS), POOL_GROUP, POOL_GROUP), POOL_GROUP ** -0.5),
        'pool_scale': 1.0 + nrm((DEPTH, G), 0.05),
        'conv_w': nrm((DEPTH, CONV_WIDTH, G), CONV_WIDTH ** -0.5),
        'conv_b': nrm((DEPTH, G), 0.02),
        'conv_ln_g': 1.0 + nrm((DEPTH, G), 0.05),
        'conv_ln_b': nrm((DEPTH, G), 0.02),
        'conv_pw': nrm((DEPTH, G, G), G ** -0.5),
        'gate_norm': 1.0 + nrm((DEPTH, G), 0.05),
        'spatial_w': nrm((DEPTH, GMLP_HEADS, GMLP_CHUNK, GMLP_CHUNK), 0.5 * GMLP_CHUNK ** -0.5),
        'spatial_b': 1.0 + nrm((DEPTH, GMLP_HEADS, GMLP_CHUNK), 0.1),
        'w_out': nrm((DEPTH, D_MODEL, D_MODEL), D_MODEL ** -0.5),
        'ffn2_norm': 1.0 + nrm((DEPTH, D_MODEL), 0.05),
        'ffn2_w_gate': nrm((DEPTH, D_MODEL, FFN_DIM), D_MODEL ** -0.5),
        'ffn2_w_up': nrm((DEPTH, D_MODEL, FFN_DIM), D_MODEL ** -0.5),
        'ffn2_w_down': nrm((DEPTH, FFN_DIM, D_MODEL), FFN_DIM ** -0.5),
    }

def reference(x_prompt, x_sample, cache_k, cache_v, state_pool, state_conv, page_table,
              ffn1_norm, ffn1_w_gate, ffn1_w_up, ffn1_w_down, mix_norm, w_in, q_norm, k_norm,
              pool_w, pool_scale, conv_w, conv_b, conv_ln_g, conv_ln_b, conv_pw,
              gate_norm, spatial_w, spatial_b, w_out, ffn2_norm, ffn2_w_gate, ffn2_w_up, ffn2_w_down):
    B = x_prompt.shape[0]
    DB = x_sample.shape[0]
    n_pages = PAST_LEN // PAGE_SIZE
    hp, hs = x_prompt, x_sample
    kp_l, vp_l, ks_l, vs_l, pp_l, ps_l, cp_l, cs_l, gs_l = [], [], [], [], [], [], [], [], []
    for l in range(DEPTH):
        lw = (ffn1_norm[l], ffn1_w_gate[l], ffn1_w_up[l], ffn1_w_down[l], mix_norm[l], w_in[l], q_norm[l], k_norm[l],
              pool_w[l], pool_scale[l], conv_w[l], conv_b[l], conv_ln_g[l], conv_ln_b[l], conv_pw[l],
              gate_norm[l], spatial_w[l], spatial_b[l], w_out[l], ffn2_norm[l], ffn2_w_gate[l], ffn2_w_up[l], ffn2_w_down[l])
        no_kv = jnp.zeros((B, 0, ATT_HEADS, HEAD_DIM), hp.dtype)
        hp, kp, vp, pp, cp, _ = hybrid_layer(hp, 0, no_kv, no_kv,
                                             jnp.zeros((B, 0, GROUP_WIDTH), hp.dtype),
                                             jnp.zeros((B, CONV_HIST, GROUP_WIDTH), hp.dtype), *lw)
        k_past = cache_k[l][page_table].reshape(DB, n_pages * PAGE_SIZE, ATT_HEADS, HEAD_DIM)
        v_past = cache_v[l][page_table].reshape(DB, n_pages * PAGE_SIZE, ATT_HEADS, HEAD_DIM)
        hs, ks, vs, ps, cs, gs = hybrid_layer(hs, PAST_LEN, k_past, v_past, state_pool[l], state_conv[l], *lw)
        kp_l.append(kp); vp_l.append(vp); ks_l.append(ks); vs_l.append(vs)
        pp_l.append(pp); ps_l.append(ps); cp_l.append(cp); cs_l.append(cs); gs_l.append(gs)
    y_prompt, y_sample = hp, hs
    k_prompt, v_prompt = jnp.stack(kp_l), jnp.stack(vp_l)
    k_sample, v_sample = jnp.stack(ks_l), jnp.stack(vs_l)
    pool_prompt, pool_sample = jnp.stack(pp_l), jnp.stack(ps_l)
    conv_prompt, conv_sample = jnp.stack(cp_l), jnp.stack(cs_l)
    gate_v_sample = jnp.stack(gs_l)
    return (y_prompt, y_sample, k_prompt, v_prompt, k_sample, v_sample, pool_prompt, pool_sample, conv_prompt, conv_sample, gate_v_sample)


_drawn_inputs = setup_inputs


def setup_inputs(seed=0):
    import zlib

    import numpy as np

    out = dict(_drawn_inputs(seed))
    spreads = {}
    factors = {'q_norm': 8.0,
     'conv_b': 3.846,
     'conv_ln_g': 2.894,
     'conv_ln_b': 8.0,
     'pool_scale': 2.754,
     'ffn2_norm': 2.935}
    for name, (base, spread) in spreads.items():
        noise = np.random.default_rng([zlib.crc32(name.encode()), seed]).standard_normal(out[name].shape)
        drawn = base * np.exp(spread * noise) if base else spread * noise
        out[name] = __import__('jax').numpy.asarray(drawn.astype(out[name].dtype))
    for name, factor in factors.items():
        out[name] = (out[name] * factor).astype(out[name].dtype)
    return out
```

```python
from contextlib import ExitStack

import concourse.bass as bass
from concourse import mybir

F32 = mybir.dt.float32
F32R = mybir.dt.float32r
I32 = mybir.dt.int32
ALU = mybir.AluOpType
ACT = mybir.ActivationFunctionType
AX = mybir.AxisListType

P = 128
DEPTH, D_MODEL, FFN = 2, 1024, 2816
SEQ, DEC_B, DEC_T = 256, 8, 8
NS = DEC_B * DEC_T
TOK = SEQ + NS
PAST, PAGE = 256, 128
PAGES = PAST // PAGE
HEADS, HEAD = 4, 64
KEYS = PAST + DEC_T
POOL_HIST, CONV_W, CONV_HIST = 15, 31, 30
RMS_EPS, LN_EPS = 1e-6, 1e-5
SCALE = HEAD ** -0.5
DT = D_MODEL // P
FT = FFN // P
GT = 2

IT_G, IT_D, IT_I, IT_O = FT // 2, DT, 4, 2
BASE_G1 = 0
BASE_D1 = BASE_G1 + IT_G
BASE_I = BASE_D1 + IT_D
BASE_O = BASE_I + IT_I
BASE_G2 = BASE_O + IT_O
BASE_D2 = BASE_G2 + IT_G
ITS = BASE_D2 + IT_D
W8_G1, W8_I, W8_O, W8_G2, W8_ROWS = 0, IT_G, IT_G + IT_I, IT_G + IT_I + IT_O, 2 * IT_G + IT_I + IT_O
W11_ROWS = 2 * IT_D
N8, N11 = 16 * P, 11 * P
HALVES8 = ((0, 8), (0, 8), (8, 8), (8, 8))
HALVES11 = ((0, 6), (0, 6), (6, 5), (6, 5))
T_G1 = 0
T_D1 = T_G1 + 4 * IT_G
T_I = T_D1 + DT
T_O = T_I + 16
T_G2 = T_O + DT
T_D2 = T_G2 + 4 * IT_G
TILES = T_D2 + DT

V_QG, V_KG, V_PS, V_CB, V_LG, V_LB, V_GG, V_CW = 0, 1, 2, 4, 6, 8, 10, 12
NV = V_CW + CONV_W * GT
CONSTS = (("ones", P), ("blk", P), ("ident", P), ("dist", 3 * P), ("alibi", KEYS), ("newm", 2 * NS),
          ("bmask", NS), ("e8", NS), ("gsel", GT * P), ("tril", P), ("inv", GT * TOK))
NC_ = sum(n for _, n in CONSTS)
SMALLS = 8
STATES = 11


class Signal:

    def __init__(self, sem, per_layer, head=0):
        self.sem, self.per, self.head = sem, per_layer, head

    def at(self, layer, k):
        return layer * self.per + (k + self.head)


def hybrid_decoder(nc, xT, w8, w11, gains, vecs, consts, pool_w, conv_pw, sp_wT, sp_b,
                   cache_kT, cache_v, conv_hist, pool_hist, pages,
                   yT, kT, vT, poolT, pool_sT, convT, conv_sT, gateT):
    ctx = ExitStack()
    with ctx:
        place = [16512]

        def sb(name, shape, dt=F32, at=None):
            n = 4
            for s in shape[1:]:
                n *= s
            offset = place[0] if at is None else at[0]
            t = nc.alloc_sbuf_tensor_at(name, shape, dt, offset=offset)
            end = offset + (n + 31) // 32 * 32
            if at is None:
                place[0] = end
                assert end <= 229344, (name, end)
            else:
                at[0] = end
                assert end <= at[1], (name, end, at[1])
            return t

        raw_a = sb("raw_a", [P, N8])
        raw_b = sb("raw_b", [P, N8])
        w_hi = sb("w_hi", [P, 4, 8 * P], F32R)
        w_lo = sb("w_lo", [P, 4, 8 * P], F32R)
        x = sb("x", [P, DT, TOK])
        mix_hi = sb("mix_hi", [P, DT, TOK], F32R)
        mix_lo = sb("mix_lo", [P, DT, TOK], F32R)
        norm_region = [place[0], None]
        xg_hi = sb("xg_hi", [P, DT, TOK], F32R)
        xg_lo = sb("xg_lo", [P, DT, TOK], F32R)
        norm_region[1] = place[0]
        ffn_region = [place[0], None]
        h_hi = sb("h_hi", [P, FT, TOK], F32R)
        h_lo = sb("h_lo", [P, FT, TOK], F32R)
        ffn_region[1] = place[0]
        cst = sb("cst", [P, NC_])
        gain = sb("gain", [P, (3 * DEPTH + 1) * DT])
        vec = sb("vec", [P, DEPTH * NV])
        page_row = sb("page_row", [1, DEC_B * PAGES], I32)
        w_pool = sb("w_pool", [P, GT, P])
        w_pw = sb("w_pw", [P, GT, GT * P])
        w_sp = sb("w_sp", [P, HEADS, P])
        w_spm = sb("w_spm", [P, HEADS, P])
        b_sp = sb("b_sp", [HEADS, P])
        bias_sp = sb("bias_sp", [HEADS, TOK])
        w_sps = sb("w_sps", [NS, HEADS, DEC_B, DEC_T])
        conv_in = sb("conv_in", [P, GT, CONV_HIST + SEQ + DEC_B * (CONV_HIST + DEC_T)])
        pool_in = sb("pool_in", [P, GT, POOL_HIST + SEQ + DEC_B * (POOL_HIST + DEC_T)])
        rms = sb("rms", [P, TOK])
        root = sb("root", [P, TOK])
        sumsq = sb("sumsq", [P, TOK])
        square = sb("square", [P, 2, TOK])
        tmp = sb("tmp", [P, 8, TOK])
        q_pad = sb("q_pad", [P, GT, DEC_B, 32])
        stat = sb("stat", [P, 64])
        prob = sb("prob", [P, HEADS, 3 * P])
        prob_s = sb("prob_s", [P, 2, KEYS])

        k_all = sb("k_all", [P, GT, DEC_B, KEYS], at=ffn_region)
        v_past = sb("v_past", [P, DEC_B * PAGES, GT * P], at=ffn_region)
        qk = sb("qk", [P, 4, TOK], at=ffn_region)
        conv_y = sb("conv_y", [P, GT, TOK], at=ffn_region)
        z_v = sb("z_v", [P, GT, TOK], at=ffn_region)
        z_u = sb("z_u", [P, GT, TOK], at=ffn_region)
        z_w = sb("z_w", [P, GT, TOK], at=ffn_region)
        v_tok = sb("v_tok", [P, 2, GT * P], at=ffn_region)
        v_tok_s = sb("v_tok_s", [NS, GT * P], at=ffn_region)
        w_tok = sb("w_tok", [P, 2, GT * P], at=ffn_region)
        w_tok_s = sb("w_tok_s", [NS, GT * P], at=ffn_region)
        prob_t = sb("prob_t", [P, HEADS, 3 * P], at=norm_region)
        prob_st = sb("prob_st", [P, 2, PAST], at=norm_region)
        prob_new = sb("prob_new", [P, 2, DEC_B, DEC_T], at=norm_region)
        prob_nt = sb("prob_nt", [NS, 2, P], at=norm_region)
        out_s = sb("out_s", [P, 2, GT * P], at=norm_region)
        att_s = sb("att_s", [P, GT, NS], at=norm_region)
        win1 = sb("win1", [P, GT, POOL_HIST + SEQ + DEC_B * (POOL_HIST + DEC_T)], at=norm_region)
        win2 = sb("win2", [P, GT, POOL_HIST + SEQ + DEC_B * (POOL_HIST + DEC_T)], at=norm_region)
        pool_m = tmp[:, 6:8, :]
        z_a = tmp[:, 0:2, :]
        z_g = tmp[:, 2:4, :]
        qk_root = tmp[:, 4:8, :]
        gm_sq = tmp[:, 0:2, :]
        gm_root = tmp[:, 2, :]
        gated = tmp[:, 4:6, :]
        conv_sq = tmp[:, 0:2, :]
        conv_root = tmp[:, 3, :]

        at, views = 0, {}
        for name, n in CONSTS:
            views[name] = cst[:, at:at + n]
            at += n
        ident = views["ident"]

        bank = [ctx.enter_context(nc.psum_tensor(f"bank{i}", [P, 512], F32)) for i in range(8)]

        def sig(name, per_layer, head=0):
            return Signal(ctx.enter_context(nc.semaphore(name)), per_layer, head)

        consts_in = sig("consts_in", 0)
        x_in = sig("x_in", 0)
        raw_a_in = sig("raw_a_in", 16 * ITS)
        raw_b_in = sig("raw_b_in", 16 * ITS)
        small_in = sig("small_in", 16 * SMALLS)
        kv_in = sig("kv_in", 16 * 2 * DEC_B * PAGES)
        states_out = sig("states_out", 16 * STATES, 16)
        y_out = sig("y_out", 0)
        passed = sig("passed", 0)
        split_hi = sig("split_hi", 4 * ITS)
        split = sig("split", 4 * ITS, 4)
        slots = sig("slots", 4 * ITS, 4)
        taken = sig("taken", TILES, 4)
        xg_hi_ok = sig("xg_hi_ok", 3 * DT, DT)
        xg_lo_ok = sig("xg_lo_ok", 3 * DT, DT)
        squared = sig("squared", 3 * DT, DT)
        summed = sig("summed", 3 * (DT + 1), DT + 1)
        norm_sum = sig("norm_sum", 3)
        norm_root = sig("norm_root", 3)
        norm_ok = sig("norm_ok", 3)
        silu_ok = sig("silu_ok", 2 * FT)
        h_ok = sig("h_ok", 2 * FT)
        h_hi_ok = sig("h_hi_ok", 2 * FT)
        h_lo_ok = sig("h_lo_ok", 2 * FT)
        zeros_ok = sig("zeros_ok", 0)
        glu_sig = sig("glu_sig", 2)
        glu_ok = sig("glu_ok", 4)
        taps = sig("taps", 4 * CONV_W)
        qk_sq = sig("qk_sq", 4)
        qk_sum = sig("qk_sum", 4)
        qk_rt = sig("qk_rt", 4)
        qk_inv = sig("qk_inv", 4)
        qk_ok = sig("qk_ok", 4)
        pads = sig("pads", 6)
        sp_ok = sig("sp_ok", 4)
        sp_rep = sig("sp_rep", 1)
        v_tr = sig("v_tr", 2)
        v_copied = sig("v_copied", 2)
        p_scores = sig("p_scores", 4)
        p_biased = sig("p_biased", 4)
        p_max = sig("p_max", 3)
        p_exp = sig("p_exp", 8)
        p_norm = sig("p_norm", 3)
        p_tr = sig("p_tr", 4)
        p_copied = sig("p_copied", 4)
        p_att = sig("p_att", 2)
        p_att_hi = sig("p_att_hi", 2)
        s_scores = sig("s_scores", 2)
        s_biased = sig("s_biased", 2)
        s_max = sig("s_max", 2)
        s_exp = sig("s_exp", 2)
        s_norm = sig("s_norm", 3)
        s_tr = sig("s_tr", 2)
        s_copied = sig("s_copied", 4)
        s_out = sig("s_out", 2)
        s_out_ok = sig("s_out_ok", 2)
        s_out_tr = sig("s_out_tr", 1)
        s_att = sig("s_att", 4)
        s_att_hi = sig("s_att_hi", 1)
        gelu_ok = sig("gelu_ok", 4)
        gm_sq_ok = sig("gm_sq_ok", 2)
        gm_sum = sig("gm_sum", 1)
        gm_rt = sig("gm_rt", 1)
        gm_v = sig("gm_v", 3)
        gm_tr = sig("gm_tr", 2)
        gm_copied = sig("gm_copied", 2)
        gm_mm = sig("gm_mm", 2)
        gm_ok = sig("gm_ok", 2)
        gm_hi = sig("gm_hi", 2)
        pool_step = sig("pool_step", 11)
        pool_mm = sig("pool_mm", 2)
        pool_hi = sig("pool_hi", 2)
        cv_mean = sig("cv_mean", 1)
        cv_cent = sig("cv_cent", 2)
        cv_sq = sig("cv_sq", 2)
        cv_var = sig("cv_var", 1)
        cv_rt = sig("cv_rt", 1)
        cv_ln = sig("cv_ln", 3)
        cv_act = sig("cv_act", 2)
        cv_pw = sig("cv_pw", 2)
        cv_hi = sig("cv_hi", 2)
        mix_ok = sig("mix_ok", 9)
        MIX_ORDER = ((6, 1), (7, 2), (2, 3), (3, 4), (0, 7), (1, 7), (4, 8), (5, 9))

        def split_tokens(ap2d, width, hist):
            prompt = ap2d[:, 0:hist + SEQ]
            rows = ap2d[:, hist + SEQ:hist + SEQ + DEC_B * width].rearrange("p (b t) -> p b t", b=DEC_B)
            return prompt, rows

        def batch(ap2d):
            return ap2d.rearrange("p (b t) -> p b t", b=DEC_B)

        def hold(engine, sem, value):
            engine.wait_ge(sem, value)
            engine.sem_inc(passed.sem, 1)

        block = ctx.enter_context(nc.Block())

        @block.sync
        def _(sp):
            sp.dma_start(cst[:, :], consts).then_inc(consts_in.sem, 16)
            sp.dma_start(gain[:, :], gains).then_inc(consts_in.sem, 16)
            sp.dma_start(vec[:, :], vecs).then_inc(consts_in.sem, 16)
            sp.dma_start(page_row[:, :], pages).then_inc(consts_in.sem, 16)
            sp.dma_start(x[:, :, :], xT).then_inc(x_in.sem, 16)

            def load(L, base, i, weights, row, n):
                for buf, part, done, landed in ((raw_a, 0, 3, raw_a_in), (raw_b, 1, 4, raw_b_in)):
                    sp.wait_ge(split.sem, L * split.per + (base + i) * 4 + done)
                    src = weights[bass.ds(row, 1), part, :, :].rearrange("a p n -> (a p) n")
                    sp.dma_start(buf[:, 0:n], src).then_inc(landed.sem, 16)

            with sp.Fori(0, DEPTH) as L:
                with sp.Fori(0, IT_G) as i:
                    load(L, BASE_G1, i, w8, L * W8_ROWS + W8_G1 + i, N8)
                with sp.Fori(0, IT_D) as i:
                    load(L, BASE_D1, i, w11, L * W11_ROWS + i, N11)
                with sp.Fori(0, 2) as i:
                    load(L, BASE_I, i, w8, L * W8_ROWS + W8_I + i, N8)
                hold(sp, states_out.sem, states_out.at(L, 0))
                hold(sp, slots.sem, slots.at(L, 4 * BASE_I))
                one = bass.ds(L, 1)
                _, conv_rows = split_tokens(conv_in[:, 0, :], CONV_HIST + DEC_T, CONV_HIST)
                for c in range(GT):
                    _, conv_rows = split_tokens(conv_in[:, c, :], CONV_HIST + DEC_T, CONV_HIST)
                    sp.dma_start(conv_rows[:, :, 0:CONV_HIST],
                                 conv_hist[one, c, :, :, :].rearrange("a p b t -> (a p) b t")).then_inc(small_in.sem, 16)
                    _, pool_rows = split_tokens(pool_in[:, c, :], POOL_HIST + DEC_T, POOL_HIST)
                    sp.dma_start(pool_rows[:, :, 0:POOL_HIST],
                                 pool_hist[one, c, :, :, :].rearrange("a p b t -> (a p) b t")).then_inc(small_in.sem, 16)
                for dst, src in ((w_pool, pool_w), (w_pw, conv_pw), (w_sp, sp_wT)):
                    sp.dma_start(dst[:, :, :], src[one, :, :, :].rearrange("a p c n -> (a p) c n")).then_inc(small_in.sem, 16)
                sp.dma_start(b_sp[:, :], sp_b[one, :, :].rearrange("a g t -> (a g) t")).then_inc(small_in.sem, 16)
                with sp.Fori(0, DEC_B) as b:
                    for n in range(PAGES):
                        page = sp.value_load(page_row[0:1, bass.ds(b * PAGES + n, 1)],
                                             min_val=0, max_val=cache_v.shape[1] - 1)
                        at_page = bass.ds(page, 1)
                        sp.dma_start(k_all[:, :, bass.ds(b, 1), n * PAGE:(n + 1) * PAGE].rearrange("p c b t -> p c (b t)"),
                                     cache_kT[one, at_page, :, :, :].rearrange("l a p c t -> (l a p) c t")).then_inc(kv_in.sem, 16)
                        sp.dma_start(v_past[:, bass.ds(b * PAGES + n, 1), :].rearrange("p b t -> p (b t)"),
                                     cache_v[one, at_page, :, :].rearrange("l a p n -> (l a p) n")).then_inc(kv_in.sem, 16)
                with sp.Fori(2, IT_I) as i:
                    load(L, BASE_I, i, w8, L * W8_ROWS + W8_I + i, N8)
                with sp.Fori(0, IT_O) as i:
                    load(L, BASE_O, i, w8, L * W8_ROWS + W8_O + i, N8)
                with sp.Fori(0, IT_G) as i:
                    load(L, BASE_G2, i, w8, L * W8_ROWS + W8_G2 + i, N8)
                with sp.Fori(0, IT_D) as i:
                    load(L, BASE_D2, i, w11, L * W11_ROWS + IT_D + i, N11)
            sp.wait_ge(taken.sem, taken.at(DEPTH, 0))
            sp.dma_start(yT, x[:, :, :]).then_inc(y_out.sem, 16)
            sp.wait_ge(y_out.sem, 16)
            sp.wait_ge(states_out.sem, states_out.at(DEPTH, 0))

        @block.gpsimd
        def _(pool):
            pool.sem_inc(split.sem, 4)

            def split_iteration(L, base, i, halves):
                for j in range(4):
                    buf, landed = ((raw_a, raw_a_in), (raw_b, raw_b_in))[j % 2]
                    first, count = halves[j]
                    src = buf[:, first * P:(first + count) * P]
                    u = L * (4 * ITS) + (base + i) * 4 + j
                    if j < 2:
                        pool.wait_ge(landed.sem, L * landed.per + (base + i) * 16 + 16)
                    hold(pool, slots.sem, u + 1)
                    pool.tensor_scalar(w_hi[:, j, 0:count * P], src, 1.0, 1.0, ALU.mult, ALU.mult).then_inc(split_hi.sem, 1)
                    pool.wait_ge(split_hi.sem, u + 1)
                    pool.tensor_tensor(w_lo[:, j, 0:count * P], src, w_hi[:, j, 0:count * P].bitcast(F32),
                                       ALU.subtract).then_inc(split.sem, 1)

            def window_sums(L):
                width = POOL_HIST + SEQ + DEC_B * (POOL_HIST + DEC_T)
                pool.wait_ge(slots.sem, slots.at(L, 4 * BASE_O))
                pool.wait_ge(taken.sem, taken.at(L, T_I + 12))
                pool.wait_ge(small_in.sem, small_in.at(L, 16 * SMALLS))
                steps = [0]

                def done(ins):
                    ins.then_inc(pool_step.sem, 1)
                    steps[0] += 1
                    hold(pool, pool_step.sem, pool_step.at(L, steps[0]))

                def add(dst, src, lanes, c, shift, lead):
                    done(pool.tensor_tensor(dst[lanes, c, lead:width], src[lanes, c, lead:width],
                                            src[lanes, c, lead - shift:width - shift], ALU.add))

                low, high, every = slice(0, 64), slice(64, P), slice(0, P)
                add(win1, pool_in, every, 0, 1, 1)
                add(win1, pool_in, every, 1, 1, 1)
                add(win2, pool_in, low, 0, 1, 1)
                add(win2, win1, high, 0, 2, 3)
                add(win2, win1, every, 1, 2, 3)
                add(win1, win2, every, 1, 4, 7)
                add(win2, win1, high, 1, 8, 15)
                done(pool.tensor_copy(win2[low, 1, 15:width], win1[low, 1, 15:width]))
                pool.wait_ge(qk_ok.sem, qk_ok.at(L, 4))
                inv = views["inv"].rearrange("p (c t) -> p c t", c=GT)
                for c in range(GT):
                    means, mean_rows = split_tokens(win2[:, c, :], POOL_HIST + DEC_T, POOL_HIST)
                    if c == 0:
                        done(pool.tensor_tensor(pool_m[:, :, 0:SEQ], win2[:, :, POOL_HIST:POOL_HIST + SEQ],
                                                inv[:, :, 0:SEQ], ALU.mult))
                    pool.tensor_tensor(batch(pool_m[:, c, SEQ:TOK]), mean_rows[:, :, POOL_HIST:],
                                       batch(inv[:, c, SEQ:TOK]), ALU.mult)
                done(pool.tensor_tensor(pool_m[:, :, 0:SEQ], pool_m[:, :, 0:SEQ],
                                        pool_in[:, :, POOL_HIST:POOL_HIST + SEQ], ALU.subtract))
                for c in range(GT):
                    _, rows = split_tokens(pool_in[:, c, :], POOL_HIST + DEC_T, POOL_HIST)
                    last = pool.tensor_tensor(batch(pool_m[:, c, SEQ:TOK]), batch(pool_m[:, c, SEQ:TOK]),
                                              rows[:, :, POOL_HIST:], ALU.subtract)
                last.then_inc(pool_step.sem, 1)
                assert steps[0] + 1 == pool_step.per

            with pool.Fori(0, DEPTH) as L:
                with pool.Fori(0, IT_G) as i:
                    split_iteration(L, BASE_G1, i, HALVES8)
                with pool.Fori(0, IT_D) as i:
                    split_iteration(L, BASE_D1, i, HALVES11)
                with pool.Fori(0, IT_I) as i:
                    split_iteration(L, BASE_I, i, HALVES8)
                split_iteration(L, BASE_O, 0, HALVES8)
                window_sums(L)
                split_iteration(L, BASE_O, 1, HALVES8)
                with pool.Fori(0, IT_G) as i:
                    split_iteration(L, BASE_G2, i, HALVES8)
                with pool.Fori(0, IT_D) as i:
                    split_iteration(L, BASE_D2, i, HALVES11)

        @block.tensor
        def _(pe):
            pe.sem_inc(slots.sem, 4)
            pe.wait_ge(consts_in.sem, 64)

            def use_slot(L, base, i, j, out, k_tiles, in_hi, in_lo, first, last, before_k=None):
                pe.wait_ge(split.sem, L * split.per + (base + i) * 4 + (j + 1 + split.head))
                for n, k in enumerate(k_tiles):
                    if before_k:
                        before_k(n, k)
                    hi, lo = w_hi[:, j, n * P:(n + 1) * P], w_lo[:, j, n * P:(n + 1) * P]
                    pe.matmul(out, hi, in_hi[:, k, :], start=first and n == 0, stop=False)
                    pe.matmul(out, hi, in_lo[:, k, :], start=False, stop=False)
                    end = n == len(k_tiles) - 1
                    mm = pe.matmul(out, lo, in_hi[:, k, :], start=False, stop=last and end)
                mm.then_inc(slots.sem, 1)

            def bank_free(L, tile):
                pe.wait_ge(taken.sem, L * taken.per + tile + 1)

            def sum_squares(L, n):
                pe.wait_ge(summed.sem, L * summed.per + (n + 1) * (DT + 1))
                pe.matmul(bank[6][:, 0:TOK], views["ones"], sumsq[:, :], start=True, stop=True).then_inc(norm_sum.sem, 1)

            def columns(L, base, tile0, norm, i, first=False):
                for j in range(4):
                    bank_free(L, i * 4 + (tile0 + j))
                    ready = (lambda n, k: pe.wait_ge(xg_lo_ok.sem, L * xg_lo_ok.per + norm * DT + k + 1)) if first and j == 0 else None
                    use_slot(L, base, i, j, bank[j][:, 0:TOK], range(8), xg_hi, xg_lo, True, True, ready)
                    if first and j == 0:
                        sum_squares(L, norm)

            def down(L, base, tile0, ffn):
                with pe.Fori(0, IT_D // 2) as i2:
                    for e in range(2):
                        i = i2 * 2 + e
                        pe.wait_ge(taken.sem, L * taken.per + i + (tile0 - 2 + 1 + 4))
                        for j, ks in enumerate((range(0, 6), range(11, 17), range(6, 11), range(17, 22))):
                            pe.wait_ge(h_lo_ok.sem, h_lo_ok.at(L, ffn * FT + ks[-1] + 1))
                            use_slot(L, base, i, j, bank[4 + e][:, 0:TOK], ks, h_hi, h_lo, j == 0, j == 3)

            def gate_up(L, base, tile0, norm):
                columns(L, base, tile0, norm, 0, first=True)
                with pe.Fori(1, IT_G) as i:
                    columns(L, base, tile0, norm, i)

            def qk_sums(L):
                for t in range(4):
                    pe.wait_ge(qk_sq.sem, qk_sq.at(L, t + 1))
                    pe.matmul(bank[4 + t][:, 0:TOK], views["blk"], qk_root[:, t, :], start=True, stop=True).then_inc(qk_sum.sem, 1)

            def prompt_scores(L):
                pe.wait_ge(qk_ok.sem, qk_ok.at(L, 4))
                for h in range(HEADS):
                    c, lanes = h // 2, slice(64 * (h % 2), 64 * (h % 2) + 64)
                    for t in range(2):
                        mm = pe.matmul(bank[4 + h][:, t * P:t * P + (t + 1) * P], qk[lanes, 2 * c, t * P:(t + 1) * P],
                                       qk[lanes, 2 * c + 1, 0:(t + 1) * P], start=True, stop=True)
                    mm.then_inc(p_scores.sem, 1)

            def value_rows(L):
                pe.wait_ge(taken.sem, taken.at(L, T_O))
                for c in range(GT):
                    for t in range(2):
                        mm = pe.transpose(bank[0][:, t * 2 * P + c * P:t * 2 * P + (c + 1) * P], z_v[:, c, t * P:(t + 1) * P], ident)
                mm.then_inc(v_tr.sem, 1)
                pe.wait_ge(sp_ok.sem, sp_ok.at(L, 3))
                pe.matmul(bank[1][0:NS, 256:288].rearrange("p (g t) -> p g t", g=HEADS), views["e8"][0:8, :],
                          w_spm[0:8, :, 0:DEC_T], start=True, stop=True).then_inc(sp_rep.sem, 1)
                for c in range(GT):
                    mm = pe.transpose(bank[1][0:NS, c * P:(c + 1) * P], z_v[:, c, SEQ:TOK], ident)
                mm.then_inc(v_tr.sem, 1)

            def batch_scores(L):
                pe.wait_ge(pads.sem, pads.at(L, 6))
                pe.wait_ge(kv_in.sem, kv_in.at(L, kv_in.per))
                for g in range(2):
                    for b4 in range(4):
                        b = 4 * g + b4
                        for c in range(GT):
                            mm = pe.matmul(bank[2 + g][32 * b4:32 * b4 + 32, 0:KEYS], q_pad[:, c, b, :], k_all[:, c, b, :],
                                           start=c == 0, stop=c == 1)
                    mm.then_inc(s_scores.sem, 1)

            def gate_square_sum(L):
                pe.wait_ge(gm_sq_ok.sem, gm_sq_ok.at(L, 2))
                pe.wait_ge(v_copied.sem, v_copied.at(L, 1))
                for c in range(GT):
                    mm = pe.matmul(bank[0][:, 0:TOK], views["ones"], gm_sq[:, c, :], start=c == 0, stop=c == 1)
                mm.then_inc(gm_sum.sem, 1)

            def prompt_attention_transposes(L):
                pe.wait_ge(p_norm.sem, p_norm.at(L, 3))
                for h in range(HEADS):
                    for n in range(3):
                        mm = pe.transpose(bank[4 + h][:, n * P:(n + 1) * P], prob[:, h, n * P:(n + 1) * P], ident)
                    mm.then_inc(p_tr.sem, 1)

            def gate_value_rows(L):
                pe.wait_ge(gm_v.sem, gm_v.at(L, 3))
                pe.wait_ge(sp_ok.sem, sp_ok.at(L, 4))
                pe.wait_ge(v_copied.sem, v_copied.at(L, 2))
                for c in range(GT):
                    for t in range(2):
                        mm = pe.transpose(bank[1][:, t * 2 * P + c * P:t * 2 * P + (c + 1) * P], z_w[:, c, t * P:(t + 1) * P], ident)
                mm.then_inc(gm_tr.sem, 1)
                for c in range(GT):
                    mm = pe.transpose(bank[0][0:NS, c * P:(c + 1) * P], z_w[:, c, SEQ:TOK], ident)
                mm.then_inc(gm_tr.sem, 1)

            def prompt_attention(L):
                pe.wait_ge(p_copied.sem, p_copied.at(L, 4))
                pe.wait_ge(v_copied.sem, v_copied.at(L, 1))
                for c in range(GT):
                    for h2 in range(2):
                        h, lanes = 2 * c + h2, slice(64 * h2, 64 * h2 + 64)
                        for t in range(2):
                            for kt in range(t + 1):
                                mm = pe.matmul(bank[4 + c][lanes, t * P:(t + 1) * P], v_tok[:, kt, h * 64:(h + 1) * 64],
                                               prob_t[:, h, (t + kt) * P:(t + kt + 1) * P], start=kt == 0, stop=kt == t)
                    mm.then_inc(p_att.sem, 1)

            def spatial_gates(L):
                pe.wait_ge(gm_copied.sem, gm_copied.at(L, 2))
                sel = views["gsel"].rearrange("p (c n) -> p c n", c=GT)
                for c in range(GT):
                    pe.matmul(bank[c][:, 0:TOK], sel[0:HEADS, c, :], bias_sp[:, :], start=True, stop=False, skip_group_check=True)
                    for h2 in range(2):
                        g, lanes = 2 * c + h2, slice(64 * h2, 64 * h2 + 64)
                        for t in range(2):
                            pe.matmul(bank[c][lanes, t * P:(t + 1) * P], w_tok[:, t, g * 64:(g + 1) * 64], w_spm[:, g, :],
                                      start=False, stop=False, skip_group_check=True)
                        mm = pe.matmul(bank[c][lanes, SEQ:TOK], w_tok_s[:, g * 64:(g + 1) * 64],
                                       w_sps[:, g, :, :].rearrange("p b t -> p (b t)"),
                                       start=False, stop=h2 == 1, skip_group_check=True)
                    mm.then_inc(gm_mm.sem, 1)

            def batch_attention(L):
                pe.wait_ge(s_norm.sem, s_norm.at(L, 3))
                for g in range(2):
                    for n in range(PAGES):
                        pe.transpose(bank[2 + g][:, n * P:(n + 1) * P], prob_s[:, g, n * P:(n + 1) * P], ident)
                    pe.transpose(bank[2 + g][0:NS, PAST:PAST + P], prob_new[:, g, :, :].rearrange("p b t -> p (b t)"),
                                 ident).then_inc(s_tr.sem, 1)
                for g in range(2):
                    pe.wait_ge(s_copied.sem, s_copied.at(L, 2 * g + 2))
                    pe.matmul(bank[6 + g][:, 0:GT * P], prob_nt[:, g, :], v_tok_s[:, :], start=True, stop=False, skip_group_check=True)
                    for b4 in range(4):
                        for n in range(PAGES):
                            mm = pe.matmul(bank[6 + g][32 * b4:32 * b4 + 32, 0:GT * P],
                                           prob_st[:, g, n * P + 32 * b4:n * P + 32 * b4 + 32],
                                           v_past[:, (4 * g + b4) * PAGES + n, :], start=False,
                                           stop=b4 == 3 and n == PAGES - 1, skip_group_check=True)
                    mm.then_inc(s_out.sem, 1)
                pe.wait_ge(s_out_ok.sem, s_out_ok.at(L, 2))
                for c in range(GT):
                    for g in range(2):
                        mm = pe.transpose(bank[2][:, (2 * c + g) * P:(2 * c + g + 1) * P], out_s[:, g, c * P:(c + 1) * P], ident)
                mm.then_inc(s_out_tr.sem, 1)

            def pool_map(L):
                pe.wait_ge(pool_step.sem, pool_step.at(L, pool_step.per))
                for c in range(GT):
                    pe.matmul(bank[(3, 7)[c]][:, 0:TOK], w_pool[:, c, :], pool_m[:, c, :], start=True, stop=True).then_inc(pool_mm.sem, 1)

            def conv_norm_map(L):
                pe.wait_ge(taps.sem, taps.at(L, taps.per))
                for c in range(GT):
                    mm = pe.matmul(bank[6][:, 0:TOK], views["ones"], conv_y[:, c, :], start=c == 0, stop=c == 1)
                mm.then_inc(cv_mean.sem, 1)
                pe.wait_ge(cv_sq.sem, cv_sq.at(L, 2))
                for c in range(GT):
                    mm = pe.matmul(bank[6][:, 0:TOK], views["ones"], conv_sq[:, c, :], start=c == 0, stop=c == 1)
                mm.then_inc(cv_var.sem, 1)
                pe.wait_ge(mix_ok.sem, mix_ok.at(L, 6))
                pe.wait_ge(cv_act.sem, cv_act.at(L, 2))
                for m in range(GT):
                    for c in range(GT):
                        mm = pe.matmul(bank[4 + m][:, 0:TOK], w_pw[:, c, m * P:(m + 1) * P], conv_y[:, c, :], start=c == 0, stop=c == 1)
                    mm.then_inc(cv_pw.sem, 1)

            with pe.Fori(0, DEPTH) as L:
                gate_up(L, BASE_G1, T_G1, 0)
                down(L, BASE_D1, T_D1, 0)
                columns(L, BASE_I, T_I, 1, 0, first=True)
                columns(L, BASE_I, T_I, 1, 1)
                columns(L, BASE_I, T_I, 1, 2)
                qk_sums(L)
                columns(L, BASE_I, T_I, 1, 3)
                pe.wait_ge(small_in.sem, small_in.at(L, small_in.per))
                prompt_scores(L)
                value_rows(L)
                batch_scores(L)
                gate_square_sum(L)
                prompt_attention_transposes(L)
                gate_value_rows(L)
                prompt_attention(L)
                spatial_gates(L)
                batch_attention(L)
                pool_map(L)
                conv_norm_map(L)
                with pe.Fori(0, IT_O) as i:
                    for j in range(4):
                        bank_free(L, i * 4 + (T_O + j))
                        counts = dict(MIX_ORDER)
                        ready = (lambda n, k: pe.wait_ge(mix_ok.sem, mix_ok.at(L, counts[k]))) if j == 0 else None
                        use_slot(L, BASE_O, i, j, bank[j][:, 0:TOK], [k for k, _ in MIX_ORDER], mix_hi, mix_lo, True, True, ready)
                gate_up(L, BASE_G2, T_G2, 2)
                down(L, BASE_D2, T_D2, 1)

        @block.scalar
        def _(act):
            act.sem_inc(states_out.sem, 16)
            act.wait_ge(consts_in.sem, 64)

            def root_of_norm(L, n):
                act.wait_ge(norm_sum.sem, norm_sum.at(L, n + 1))
                act.activation(root[:, :], bank[6][:, 0:TOK], ACT.Sqrt, bias=eps_rms, scale=1.0 / D_MODEL).then_inc(norm_root.sem, 1)

            def norm_input(gain_col, d, e, xg_col):
                act.activation(xg_hi[:, bass.ds(d, 1), :].rearrange("p a t -> p (a t)"), x[:, bass.ds(d, 1), :].rearrange("p a t -> p (a t)"),
                               ACT.Identity, scale=gain[:, bass.ds(gain_col, 1)]).then_inc(xg_hi_ok.sem, 1)
                hold(act, summed.sem, xg_col)
                act.activation(square[:, e, :], x[:, bass.ds(d, 1), :].rearrange("p a t -> p (a t)"), ACT.Square).then_inc(squared.sem, 1)

            def gate_up(L, base, tile0, ffn):
                with act.Fori(0, IT_G) as i:
                    for m in range(2):
                        act.wait_ge(taken.sem, L * taken.per + i * 4 + (tile0 + 2 * m + 1 + taken.head))
                        act.activation(tmp[:, 2 + m, :], tmp[:, m, :], ACT.Silu).then_inc(silu_ok.sem, 1)
                        hold(act, h_ok.sem, L * h_ok.per + i * 2 + (ffn * FT + m + 1))
                        act.activation(h_hi[:, bass.ds(i * 2 + m, 1), :].rearrange("p a t -> p (a t)"), tmp[:, 6 + m, :],
                                       ACT.Copy).then_inc(h_hi_ok.sem, 1)

            def residual(L, tile0, norm, count):
                with act.Fori(0, DT // 2) as i:
                    for e in range(2):
                        d = i * 2 + e
                        hold(act, taken.sem, L * taken.per + d + (tile0 + 1 + taken.head))
                        norm_input(L * (3 * DT) + d + norm * DT, d, e, L * summed.per + d + norm * (DT + 1))

            eps_rms, eps_ln = stat[:, 60:61], stat[:, 61:62]
            act.wait_ge(zeros_ok.sem, 1)
            act.wait_ge(x_in.sem, 16)
            with act.Fori(0, DT // 2) as i:
                for e in range(2):
                    d = i * 2 + e
                    norm_input(d, d, e, d + 1)

            with act.Fori(0, DEPTH) as L:
                root_of_norm(L, 0)
                gate_up(L, BASE_G1, T_G1, 0)
                residual(L, T_D1, 1, None)
                root_of_norm(L, 1)
                for c in range(GT):
                    act.wait_ge(taken.sem, taken.at(L, T_I + 2 * c + 2))
                    act.activation(z_g[:, c, :], z_g[:, c, :], ACT.Sigmoid).then_inc(glu_sig.sem, 1)
                for t in range(4):
                    act.wait_ge(taken.sem, taken.at(L, T_I + 4 + t + 1))
                    act.activation(qk_root[:, t, :], qk[:, t, :], ACT.Square).then_inc(qk_sq.sem, 1)
                for t in range(4):
                    act.wait_ge(qk_sum.sem, qk_sum.at(L, t + 1))
                    act.activation(qk_root[:, t, :], bank[4 + t][:, 0:TOK], ACT.Sqrt, bias=eps_rms, scale=1.0 / HEAD).then_inc(qk_rt.sem, 1)
                for n, z in enumerate((z_u[:, 0, :], z_w[:, 0, :], z_u[:, 1, :], z_w[:, 1, :])):
                    act.wait_ge(taken.sem, taken.at(L, T_I + 12 + n + 1))
                    act.activation(z, z, ACT.Gelu_apprx_tanh).then_inc(gelu_ok.sem, 1)
                for c in range(GT):
                    act.wait_ge(gelu_ok.sem, gelu_ok.at(L, 2 * c + 2))
                    act.activation(gm_sq[:, c, :], z_w[:, c, :], ACT.Square).then_inc(gm_sq_ok.sem, 1)
                act.wait_ge(v_tr.sem, v_tr.at(L, 1))
                act.activation(v_tok[:, :, :].rearrange("p t n -> p (t n)"), bank[0][:, :], ACT.Copy).then_inc(v_copied.sem, 1)
                act.wait_ge(v_tr.sem, v_tr.at(L, 2))
                act.activation(v_tok_s[:, :], bank[1][0:NS, 0:GT * P], ACT.Copy).then_inc(v_copied.sem, 1)
                act.wait_ge(p_max.sem, p_max.at(L, 3))
                for t in range(2):
                    for h in range(HEADS):
                        cols = slice(t * P, t * P + (t + 1) * P)
                        act.activation(prob[:, h, cols], prob[:, h, cols], ACT.Exp, bias=stat[:, 8 + 4 * t + h:9 + 4 * t + h],
                                       scale=SCALE, accum_out=stat[:, 16 + 4 * t + h:17 + 4 * t + h]).then_inc(p_exp.sem, 1)
                act.wait_ge(s_max.sem, s_max.at(L, 2))
                for g in range(2):
                    act.activation(prob_s[:, g, :], prob_s[:, g, :], ACT.Exp, bias=stat[:, 34 + g:35 + g], scale=SCALE,
                                   accum_out=stat[:, 36 + g:37 + g]).then_inc(s_exp.sem, 1)
                act.wait_ge(gm_sum.sem, gm_sum.at(L, 1))
                act.activation(gm_root[:, :], bank[0][:, 0:TOK], ACT.Sqrt, bias=eps_rms, scale=1.0 / (GT * P)).then_inc(gm_rt.sem, 1)
                for h in range(HEADS):
                    act.wait_ge(p_tr.sem, p_tr.at(L, h + 1))
                    act.activation(prob_t[:, h, :], bank[4 + h][:, 0:3 * P], ACT.Copy).then_inc(p_copied.sem, 1)
                act.wait_ge(gm_tr.sem, gm_tr.at(L, 1))
                act.activation(w_tok[:, :, :].rearrange("p t n -> p (t n)"), bank[1][:, :], ACT.Copy).then_inc(gm_copied.sem, 1)
                act.wait_ge(gm_tr.sem, gm_tr.at(L, 2))
                act.activation(w_tok_s[:, :], bank[0][0:NS, 0:GT * P], ACT.Copy).then_inc(gm_copied.sem, 1)
                for c in range(GT):
                    act.wait_ge(p_att.sem, p_att.at(L, c + 1))
                    act.activation(mix_hi[:, c, 0:SEQ], bank[4 + c][:, 0:SEQ], ACT.Copy).then_inc(p_att_hi.sem, 1)
                for g in range(2):
                    act.wait_ge(s_tr.sem, s_tr.at(L, g + 1))
                    act.activation(prob_st[:, g, :], bank[2 + g][:, 0:PAST], ACT.Copy).then_inc(s_copied.sem, 1)
                    act.activation(prob_nt[:, g, :], bank[2 + g][0:NS, PAST:PAST + P], ACT.Copy).then_inc(s_copied.sem, 1)
                for g in range(2):
                    act.wait_ge(s_out.sem, s_out.at(L, g + 1))
                    act.activation(out_s[:, g, :], bank[6 + g][:, 0:GT * P], ACT.Copy).then_inc(s_out_ok.sem, 1)
                for c in range(GT):
                    act.wait_ge(gm_ok.sem, gm_ok.at(L, c + 1))
                    act.activation(mix_hi[:, 6 + c, :], gated[:, c, :], ACT.Copy).then_inc(gm_hi.sem, 1)
                for c in range(GT):
                    hold(act, pool_mm.sem, pool_mm.at(L, c + 1))
                    act.activation(mix_hi[:, 2 + c, :], bank[(3, 7)[c]][:, 0:TOK], ACT.Identity,
                                   scale=vec[:, bass.ds(L * NV + (V_PS + c), 1)]).then_inc(pool_hi.sem, 1)
                act.wait_ge(s_att.sem, s_att.at(L, 4))
                act.activation(mix_hi[:, 0:2, SEQ:TOK], att_s[:, :, :], ACT.Copy).then_inc(s_att_hi.sem, 1)
                for c in range(GT):
                    act.wait_ge(cv_cent.sem, cv_cent.at(L, c + 1))
                    act.activation(conv_sq[:, c, :], conv_y[:, c, :], ACT.Square).then_inc(cv_sq.sem, 1)
                act.wait_ge(cv_var.sem, cv_var.at(L, 1))
                act.activation(conv_root[:, :], bank[6][:, 0:TOK], ACT.Sqrt, bias=eps_ln, scale=1.0 / (GT * P)).then_inc(cv_rt.sem, 1)
                for c in range(GT):
                    hold(act, cv_ln.sem, cv_ln.at(L, c + 2))
                    act.activation(conv_y[:, c, :], conv_y[:, c, :], ACT.Silu, scale=vec[:, bass.ds(L * NV + (V_LG + c), 1)],
                                   bias=vec[:, bass.ds(L * NV + (V_LB + c), 1)]).then_inc(cv_act.sem, 1)
                for c in range(GT):
                    act.wait_ge(cv_pw.sem, cv_pw.at(L, c + 1))
                    act.activation(mix_hi[:, 4 + c, :], bank[4 + c][:, 0:TOK], ACT.Copy).then_inc(cv_hi.sem, 1)
                layer = bass.ds(L, 1)
                act.wait_ge(mix_ok.sem, mix_ok.at(L, 7))
                act.dma_start(kT[layer, :, :, :].rearrange("l c p t -> p (l c) t"), qk[:, 1:4:2, :]).then_inc(states_out.sem, 16)
                act.dma_start(vT[layer, :, :, :].rearrange("l c p t -> p (l c) t"), z_v[:, :, :]).then_inc(states_out.sem, 16)
                act.dma_start(poolT[layer, :, :, :].rearrange("l c p t -> p (l c) t"), pool_in[:, :, SEQ:SEQ + POOL_HIST]).then_inc(states_out.sem, 16)
                act.dma_start(convT[layer, :, :, :].rearrange("l c p t -> p (l c) t"), conv_in[:, :, SEQ:SEQ + CONV_HIST]).then_inc(states_out.sem, 16)
                act.dma_start(gateT[layer, :, :, :].rearrange("l c p t -> p (l c) t"), z_w[:, :, SEQ:TOK]).then_inc(states_out.sem, 16)
                for c in range(GT):
                    _, rows = split_tokens(pool_in[:, c, :], POOL_HIST + DEC_T, POOL_HIST)
                    act.dma_start(pool_sT[layer, c, :, :, :].rearrange("l p b t -> (l p) b t"), rows[:, :, DEC_T:]).then_inc(states_out.sem, 16)
                    _, rows = split_tokens(conv_in[:, c, :], CONV_HIST + DEC_T, CONV_HIST)
                    for half in range(2):
                        act.dma_start(conv_sT[layer, c, :, 4 * half:4 * half + 4, :].rearrange("l p b t -> (l p) b t"),
                                      rows[:, 4 * half:4 * half + 4, DEC_T:]).then_inc(states_out.sem, 16)
                residual(L, T_O, 2, None)
                root_of_norm(L, 2)
                act.wait_ge(states_out.sem, states_out.at(L, states_out.per))
                gate_up(L, BASE_G2, T_G2, 1)
                residual(L, T_D2, 3, None)

        @block.vector
        def _(dve):
            dve.sem_inc(taken.sem, 4)
            for n, (ap, value) in enumerate(((stat[:, 60:61], RMS_EPS), (stat[:, 61:62], LN_EPS), (q_pad[:, :, :, :], 0.0),
                                             (conv_in[:, :, 0:CONV_HIST], 0.0), (pool_in[:, :, 0:POOL_HIST], 0.0))):
                last = dve.memset(ap, value)
            last.then_inc(zeros_ok.sem, 1)
            dve.memset(sumsq[:, :], 0.0).then_inc(summed.sem, 1)
            dve.wait_ge(consts_in.sem, 64)
            dve.wait_ge(x_in.sem, 16)

            def norm_input(gain_col, d, e, tile_count, sum_count):
                one = x[:, bass.ds(d, 1), :].rearrange("p a t -> p (a t)")
                dve.wait_ge(xg_hi_ok.sem, tile_count + 1)
                dve.scalar_tensor_tensor(out=xg_lo[:, bass.ds(d, 1), :].rearrange("p a t -> p (a t)"), in0=one,
                                         scalar=gain[:, bass.ds(gain_col, 1)],
                                         in1=xg_hi[:, bass.ds(d, 1), :].bitcast(F32).rearrange("p a t -> p (a t)"),
                                         op0=ALU.mult, op1=ALU.subtract).then_inc(xg_lo_ok.sem, 1)
                dve.wait_ge(squared.sem, tile_count + 1)
                dve.wait_ge(summed.sem, sum_count + 1)
                dve.tensor_tensor(sumsq[:, :], sumsq[:, :], square[:, e, :], ALU.add).then_inc(summed.sem, 1)

            def invert_norm(L, n):
                dve.wait_ge(norm_root.sem, norm_root.at(L, n + 1))
                dve.reciprocal(rms[:, :], root[:, :]).then_inc(norm_ok.sem, 1)
                dve.memset(sumsq[:, :], 0.0).then_inc(summed.sem, 1)
                hold(dve, norm_ok.sem, norm_ok.at(L, n + 1))

            def gate_up(L, base, tile0, ffn):
                with dve.Fori(0, IT_G) as i:
                    for m in range(2):
                        f = L * (2 * FT) + i * 2 + (ffn * FT + m + 1)
                        tiles = L * TILES + i * 4 + (tile0 + 2 * m + taken.head)
                        done = L * slots.per + i * 4 + (4 * base + 2 * m + slots.head)
                        dve.wait_ge(slots.sem, done + 1)
                        dve.tensor_tensor(tmp[:, m, :], bank[2 * m][:, 0:TOK], rms[:, :], ALU.mult).then_inc(taken.sem, 1)
                        dve.wait_ge(slots.sem, done + 2)
                        dve.tensor_tensor(tmp[:, 4 + m, :], bank[2 * m + 1][:, 0:TOK], rms[:, :], ALU.mult).then_inc(taken.sem, 1)
                        dve.wait_ge(silu_ok.sem, f)
                        dve.wait_ge(taken.sem, tiles + 2)
                        dve.tensor_tensor(tmp[:, 6 + m, :], tmp[:, 2 + m, :], tmp[:, 4 + m, :], ALU.mult).then_inc(h_ok.sem, 1)
                        dve.wait_ge(h_hi_ok.sem, f)
                        dve.tensor_tensor(h_lo[:, bass.ds(i * 2 + m, 1), :].rearrange("p a t -> p (a t)"), tmp[:, 6 + m, :],
                                          h_hi[:, bass.ds(i * 2 + m, 1), :].bitcast(F32).rearrange("p a t -> p (a t)"),
                                          ALU.subtract).then_inc(h_lo_ok.sem, 1)

            def residual(L, base, tile0, norm, factor, tiles_an_iteration, banks):
                n_banks = len(banks)
                with dve.Fori(0, DT // n_banks) as i:
                    for e in range(n_banks):
                        d = i * n_banks + e
                        slots_a_tile = 4 // tiles_an_iteration
                        dve.wait_ge(slots.sem, L * slots.per + d * slots_a_tile + (4 * base + slots_a_tile + slots.head))
                        one = x[:, bass.ds(d, 1), :].rearrange("p a t -> p (a t)")
                        dve.scalar_tensor_tensor(out=one, in0=bank[banks[e]][:, 0:TOK], scalar=factor, in1=one,
                                                 op0=ALU.mult, op1=ALU.add).then_inc(taken.sem, 1)
                        norm_input(L * (3 * DT) + d + norm * DT, d, e % 2, L * (3 * DT) + d + norm * DT,
                                   L * summed.per + d + norm * (DT + 1))

            with dve.Fori(0, DT // 2) as i:
                for e in range(2):
                    d = i * 2 + e
                    norm_input(d, d, e, d, d)

            def take(L, t, dst, b=None):
                dve.wait_ge(slots.sem, slots.at(L, 4 * BASE_I + t + 1))
                dve.tensor_tensor(dst, bank[t % 4][:, 0:TOK], rms[:, :], ALU.mult).then_inc(taken.sem, 1)

            def conv_taps(L, k0, k1):
                def views_at(c, k):
                    prompt = conv_in[:, c, bass.ds(k, SEQ)]
                    _, rows = split_tokens(conv_in[:, c, :], CONV_HIST + DEC_T, CONV_HIST)
                    return ((prompt, conv_y[:, c, 0:SEQ]), (rows[:, :, bass.ds(k, DEC_T)], batch(conv_y[:, c, SEQ:TOK])))

                if k0 == 0:
                    dve.wait_ge(glu_ok.sem, glu_ok.at(L, 4))
                    dve.wait_ge(small_in.sem, small_in.at(L, small_in.per))
                    for c in range(GT):
                        for src, dst in views_at(c, 0):
                            dve.tensor_scalar(dst, src, vec[:, bass.ds(L * NV + (V_CW + c), 1)],
                                              vec[:, bass.ds(L * NV + (V_CB + c), 1)], ALU.mult, ALU.add).then_inc(taps.sem, 1)
                    k0 = 1
                with dve.Fori(k0, k1) as k:
                    for c in range(GT):
                        for n, (src, dst) in enumerate(views_at(c, k)):
                            dve.wait_ge(taps.sem, L * taps.per + k * 4 + (2 * c + n - 3))
                            dve.scalar_tensor_tensor(out=dst, in0=src, scalar=vec[:, bass.ds(L * NV + k * GT + (V_CW + c), 1)],
                                                     in1=dst, op0=ALU.mult, op1=ALU.add).then_inc(taps.sem, 1)

            with dve.Fori(0, DEPTH) as L:
                invert_norm(L, 0)
                gate_up(L, BASE_G1, T_G1, 0)
                residual(L, BASE_D1, T_D1, 1, 0.5, 1, (4, 5))
                invert_norm(L, 1)
                dve.wait_ge(states_out.sem, states_out.at(L, 0))
                for c in range(GT):
                    take(L, 2 * c, z_a[:, c, :])
                    take(L, 2 * c + 1, z_g[:, c, :])
                for c in range(GT):
                    dve.wait_ge(glu_sig.sem, glu_sig.at(L, c + 1))
                    dve.tensor_tensor(conv_in[:, c, CONV_HIST:CONV_HIST + SEQ], z_a[:, c, 0:SEQ], z_g[:, c, 0:SEQ], ALU.mult).then_inc(glu_ok.sem, 1)
                    _, rows = split_tokens(conv_in[:, c, :], CONV_HIST + DEC_T, CONV_HIST)
                    dve.tensor_tensor(rows[:, :, CONV_HIST:], batch(z_a[:, c, SEQ:TOK]), batch(z_g[:, c, SEQ:TOK]), ALU.mult).then_inc(glu_ok.sem, 1)
                dve.wait_ge(small_in.sem, small_in.at(L, small_in.per))
                dve.tensor_tensor(w_spm[:, :, :], w_sp[:, :, :], views["tril"].rearrange("p (g t) -> p g t", g=1).to_broadcast([P, HEADS, P]),
                                  ALU.mult).then_inc(sp_ok.sem, 1)
                dve.tensor_copy(bias_sp[:, 0:SEQ].rearrange("p (n t) -> p n t", n=2),
                                b_sp[:, :].rearrange("p (n t) -> p n t", n=1).to_broadcast([HEADS, 2, P])).then_inc(sp_ok.sem, 1)
                dve.tensor_copy(batch(bias_sp[:, SEQ:TOK]),
                                b_sp[:, 0:DEC_T].rearrange("p (n t) -> p n t", n=1).to_broadcast([HEADS, DEC_B, DEC_T])).then_inc(sp_ok.sem, 1)
                conv_taps(L, 0, 8)
                for t in range(4):
                    take(L, 4 + t, qk[:, t, :])
                conv_taps(L, 8, 17)
                for c in range(GT):
                    dve.wait_ge(slots.sem, slots.at(L, 4 * BASE_I + 8 + 2 * c + 1))
                    dve.tensor_tensor(pool_in[:, c, POOL_HIST:POOL_HIST + SEQ], bank[2 * c][:, 0:SEQ], rms[:, 0:SEQ], ALU.mult)
                    _, rows = split_tokens(pool_in[:, c, :], POOL_HIST + DEC_T, POOL_HIST)
                    dve.tensor_tensor(rows[:, :, POOL_HIST:], batch(bank[2 * c][:, SEQ:TOK]), batch(rms[:, SEQ:TOK]), ALU.mult).then_inc(taken.sem, 1)
                    take(L, 8 + 2 * c + 1, z_v[:, c, :])
                for t in range(4):
                    dve.wait_ge(qk_rt.sem, qk_rt.at(L, t + 1))
                    dve.reciprocal(qk_root[:, t, :], qk_root[:, t, :]).then_inc(qk_inv.sem, 1)
                    dve.wait_ge(qk_inv.sem, qk_inv.at(L, t + 1))
                    dve.scalar_tensor_tensor(out=qk[:, t, :], in0=qk[:, t, :], scalar=vec[:, bass.ds(L * NV + (V_QG, V_KG)[t % 2], 1)],
                                             in1=qk_root[:, t, :], op0=ALU.mult, op1=ALU.mult).then_inc(qk_ok.sem, 1)
                dve.wait_ge(qk_ok.sem, qk_ok.at(L, 4))
                for c in range(GT):
                    for h2 in range(2):
                        lanes, h = slice(64 * h2, 64 * h2 + 64), 2 * c + h2
                        dve.tensor_copy(q_pad[lanes, c, :, h * DEC_T:(h + 1) * DEC_T], batch(qk[lanes, 2 * c, SEQ:TOK])).then_inc(pads.sem, 1)
                    dve.tensor_copy(k_all[:, c, :, PAST:KEYS], batch(qk[:, 2 * c + 1, SEQ:TOK])).then_inc(pads.sem, 1)
                for c in range(GT):
                    take(L, 12 + 2 * c, z_u[:, c, :])
                    take(L, 12 + 2 * c + 1, z_w[:, c, :])
                for h in range(HEADS):
                    dve.wait_ge(p_scores.sem, p_scores.at(L, h + 1))
                    dve.scalar_tensor_tensor(out=prob[:, h, :], in0=views["dist"], scalar=2.0 ** (-8.0 * (h + 1) / HEADS) / SCALE,
                                             in1=bank[4 + h][:, 0:3 * P], op0=ALU.mult, op1=ALU.add).then_inc(p_biased.sem, 1)
                dve.wait_ge(p_biased.sem, p_biased.at(L, 4))
                dve.tensor_reduce(stat[:, 0:4], prob[:, :, 0:P], AX.X, ALU.max).then_inc(p_max.sem, 1)
                dve.tensor_reduce(stat[:, 4:8], prob[:, :, P:3 * P], AX.X, ALU.max).then_inc(p_max.sem, 1)
                dve.wait_ge(p_max.sem, p_max.at(L, 2))
                dve.tensor_scalar(stat[:, 8:16], stat[:, 0:8], -SCALE, None, ALU.mult).then_inc(p_max.sem, 1)
                for g in range(2):
                    dve.wait_ge(s_scores.sem, s_scores.at(L, g + 1))
                    dve.tensor_tensor(prob_s[:, g, :], bank[2 + g][:, 0:KEYS], views["alibi"], ALU.add).then_inc(s_biased.sem, 1)
                dve.wait_ge(s_biased.sem, s_biased.at(L, 2))
                dve.tensor_reduce(stat[:, 32:34], prob_s[:, :, :], AX.X, ALU.max).then_inc(s_max.sem, 1)
                dve.wait_ge(s_max.sem, s_max.at(L, 1))
                dve.tensor_scalar(stat[:, 34:36], stat[:, 32:34], -SCALE, None, ALU.mult).then_inc(s_max.sem, 1)
                dve.wait_ge(sp_rep.sem, sp_rep.at(L, 1))
                dve.wait_ge(v_copied.sem, v_copied.at(L, 2))
                dve.tensor_tensor(w_sps[:, :, :, :],
                                  bank[1][0:NS, 256:288].rearrange("p (g b t) -> p g b t", g=HEADS, b=1).to_broadcast([NS, HEADS, DEC_B, DEC_T]),
                                  views["bmask"][0:NS, :].rearrange("p (g b t) -> p g b t", g=1, b=DEC_B).to_broadcast([NS, HEADS, DEC_B, DEC_T]),
                                  ALU.mult).then_inc(sp_ok.sem, 1)
                dve.wait_ge(p_exp.sem, p_exp.at(L, 8))
                dve.reciprocal(stat[:, 24:32], stat[:, 16:24]).then_inc(p_norm.sem, 1)
                dve.wait_ge(p_norm.sem, p_norm.at(L, 1))
                for t in range(2):
                    cols, n = slice(t * P, t * P + (t + 1) * P), (t + 1) * P
                    inv = stat[:, 24 + 4 * t:28 + 4 * t].rearrange("p (h n) -> p h n", n=1).to_broadcast([P, HEADS, n])
                    dve.tensor_tensor(prob[:, :, cols], prob[:, :, cols], inv, ALU.mult).then_inc(p_norm.sem, 1)
                dve.wait_ge(s_exp.sem, s_exp.at(L, 2))
                dve.reciprocal(stat[:, 38:40], stat[:, 36:38]).then_inc(s_norm.sem, 1)
                dve.wait_ge(s_norm.sem, s_norm.at(L, 1))
                dve.tensor_tensor(prob_s[:, :, :], prob_s[:, :, :],
                                  stat[:, 38:40].rearrange("p (g n) -> p g n", n=1).to_broadcast([P, 2, KEYS]), ALU.mult).then_inc(s_norm.sem, 1)
                dve.wait_ge(s_norm.sem, s_norm.at(L, 2))
                dve.tensor_tensor(prob_new[:, :, :, :],
                                  prob_s[:, :, PAST:KEYS].rearrange("p g (b t) -> p g b t", b=1).to_broadcast([P, 2, DEC_B, DEC_T]),
                                  views["newm"].rearrange("p (g b t) -> p g b t", g=2, b=DEC_B), ALU.mult).then_inc(s_norm.sem, 1)
                dve.wait_ge(gm_rt.sem, gm_rt.at(L, 1))
                dve.reciprocal(gm_root[:, :], gm_root[:, :]).then_inc(gm_v.sem, 1)
                dve.wait_ge(gm_v.sem, gm_v.at(L, 1))
                for c in range(GT):
                    dve.scalar_tensor_tensor(out=z_w[:, c, :], in0=z_w[:, c, :], scalar=vec[:, bass.ds(L * NV + (V_GG + c), 1)],
                                             in1=gm_root[:, :], op0=ALU.mult, op1=ALU.mult).then_inc(gm_v.sem, 1)
                conv_taps(L, 17, CONV_W)

                def low_part(c, out_lo, src, out_hi):
                    dve.tensor_tensor(out_lo, src, out_hi.bitcast(F32), ALU.subtract).then_inc(mix_ok.sem, 1)

                for c in range(GT):
                    dve.wait_ge(gm_mm.sem, gm_mm.at(L, c + 1))
                    dve.tensor_tensor(gated[:, c, :], z_u[:, c, :], bank[c][:, 0:TOK], ALU.mult).then_inc(gm_ok.sem, 1)
                for c in range(GT):
                    dve.wait_ge(gm_hi.sem, gm_hi.at(L, c + 1))
                    low_part(c, mix_lo[:, 6 + c, :], gated[:, c, :], mix_hi[:, 6 + c, :])
                for c in range(GT):
                    dve.wait_ge(pool_hi.sem, pool_hi.at(L, c + 1))
                    dve.scalar_tensor_tensor(out=mix_lo[:, 2 + c, :], in0=bank[(3, 7)[c]][:, 0:TOK],
                                             scalar=vec[:, bass.ds(L * NV + (V_PS + c), 1)], in1=mix_hi[:, 2 + c, :].bitcast(F32),
                                             op0=ALU.mult, op1=ALU.subtract).then_inc(mix_ok.sem, 1)
                for c in range(GT):
                    dve.wait_ge(p_att_hi.sem, p_att_hi.at(L, c + 1))
                    low_part(c, mix_lo[:, c, 0:SEQ], bank[4 + c][:, 0:SEQ], mix_hi[:, c, 0:SEQ])
                dve.wait_ge(s_out_tr.sem, s_out_tr.at(L, 1))
                for c in range(GT):
                    for h2 in range(2):
                        lanes, h = slice(64 * h2, 64 * h2 + 64), 2 * c + h2
                        src = bank[2][lanes, 2 * c * P:2 * (c + 1) * P].rearrange("p (b n) -> p b n", b=DEC_B)[:, :, h * DEC_T:(h + 1) * DEC_T]
                        dve.tensor_copy(batch(att_s[lanes, c, :]), src).then_inc(s_att.sem, 1)
                dve.wait_ge(s_att_hi.sem, s_att_hi.at(L, 1))
                low_part(0, mix_lo[:, 0:2, SEQ:TOK], att_s[:, :, :], mix_hi[:, 0:2, SEQ:TOK])
                dve.wait_ge(cv_mean.sem, cv_mean.at(L, 1))
                for c in range(GT):
                    dve.scalar_tensor_tensor(out=conv_y[:, c, :], in0=bank[6][:, 0:TOK], scalar=-1.0 / (GT * P), in1=conv_y[:, c, :],
                                             op0=ALU.mult, op1=ALU.add).then_inc(cv_cent.sem, 1)
                dve.wait_ge(cv_rt.sem, cv_rt.at(L, 1))
                dve.reciprocal(conv_root[:, :], conv_root[:, :]).then_inc(cv_ln.sem, 1)
                dve.wait_ge(cv_ln.sem, cv_ln.at(L, 1))
                for c in range(GT):
                    dve.tensor_tensor(conv_y[:, c, :], conv_y[:, c, :], conv_root[:, :], ALU.mult).then_inc(cv_ln.sem, 1)
                for c in range(GT):
                    dve.wait_ge(cv_hi.sem, cv_hi.at(L, c + 1))
                    low_part(c, mix_lo[:, 4 + c, :], bank[4 + c][:, 0:TOK], mix_hi[:, 4 + c, :])
                residual(L, BASE_O, T_O, 2, 1.0, 4, (0, 1, 2, 3))
                invert_norm(L, 2)
                hold(dve, states_out.sem, states_out.at(L, states_out.per))
                gate_up(L, BASE_G2, T_G2, 1)
                residual(L, BASE_D2, T_D2, 3, 0.5, 1, (4, 5))


def _constants(np):
    BIG = -1.0e30
    c = {}
    c["ones"] = np.ones((P, P))
    c["blk"] = np.kron(np.eye(2), np.ones((64, 64)))
    c["ident"] = np.eye(P)
    q = np.arange(P)[:, None]
    first = np.where(q >= np.arange(P), np.arange(P) - q, BIG)
    second = np.where(q + P >= np.arange(2 * P), np.arange(2 * P) - (q + P), BIG)
    c["dist"] = np.concatenate([first, second], 1)
    row = np.arange(P)
    slope = 2.0 ** (-8.0 * ((row // 8) % 4 + 1) / HEADS) / SCALE
    pos = PAST + row % 8
    key = np.arange(KEYS)
    c["alibi"] = np.where(key <= pos[:, None], slope[:, None] * (key - pos[:, None]), BIG)
    b = np.arange(NS) // 8
    c["newm"] = np.concatenate([b[None, :] == (4 * g + row // 32)[:, None] for g in range(2)], 1)
    c["bmask"] = np.zeros((P, NS))
    c["bmask"][:NS] = b[:, None] == b[None, :]
    c["e8"] = np.zeros((P, NS))
    c["e8"][:8] = np.arange(8)[:, None] == (np.arange(NS) % 8)[None, :]
    gsel = np.zeros((P, GT, P))
    for g in range(HEADS):
        gsel[g, g // 2, 64 * (g % 2):64 * (g % 2) + 64] = 1
    c["gsel"] = gsel.reshape(P, -1)
    c["tril"] = np.arange(P)[:, None] <= np.arange(P)[None, :]
    inv = np.zeros((P, GT, TOK))
    for g, w in enumerate((2, 4, 8, 16)):
        lanes = slice(64 * (g % 2), 64 * (g % 2) + 64)
        inv[lanes, g // 2, :SEQ] = 1.0 / np.minimum(np.arange(SEQ) + 1, w)
        inv[lanes, g // 2, SEQ:] = 1.0 / w
    c["inv"] = inv.reshape(P, -1)
    return np.concatenate([np.asarray(c[n], np.float32) for n, _ in CONSTS], 1)


def kernel(**inputs):
    import numpy as np
    import concourse.bacc as bacc
    from concourse.bass_utils import run_bass_kernel_spmd as run

    a = {k: np.asarray(v) for k, v in inputs.items()}
    n_pool = a["cache_k"].shape[1]

    def cols(w):
        d, r, n = w.shape
        return w.reshape(d, r // P, P, n // P, P).transpose(0, 3, 2, 1, 4)

    def halves(first, second):
        both = np.stack([first, second], 2)
        d, it, ab, half = both.shape[:4]
        return both.transpose(0, 1, 2, 4, 3, 5, 6).reshape(d, it, ab, P, -1)

    def gate_up(g, u):
        g, u = cols(g), cols(u)
        pair = lambda w: w.reshape(DEPTH, FT // 2, 2, P, DT, P)
        return halves(pair(g), pair(u))

    def down(w):
        w = cols(w)
        return np.stack([w[:, :, :, :11], w[:, :, :, 11:]], 2).reshape(DEPTH, DT, 2, P, 11 * P)

    w_in = cols(a["w_in"])
    order_a = [8, 9, 0, 1, 6, 7, 12, 13]
    order_b = [10, 11, 2, 3, 4, 5, 14, 15]
    i8 = halves(w_in[:, order_a].reshape(DEPTH, 4, 2, P, DT, P), w_in[:, order_b].reshape(DEPTH, 4, 2, P, DT, P))
    w_out = cols(a["w_out"])[:, :, :, [6, 7, 2, 3, 0, 1, 4, 5]].reshape(DEPTH, 2, 2, 2, P, DT, P)
    o8 = halves(w_out[:, :, :, 0], w_out[:, :, :, 1])
    w8 = np.concatenate([gate_up(a["ffn1_w_gate"], a["ffn1_w_up"]), i8, o8, gate_up(a["ffn2_w_gate"], a["ffn2_w_up"])], 1)
    w11 = np.concatenate([down(a["ffn1_w_down"]), down(a["ffn2_w_down"])], 1)

    gains = np.stack([a["ffn1_norm"], a["mix_norm"], a["ffn2_norm"]], 1).reshape(3 * DEPTH, DT, P)
    gains = np.concatenate([gains, gains[:1]]).transpose(2, 0, 1).reshape(P, -1)
    two = lambda v: v.reshape(DEPTH, GT, P).transpose(2, 0, 1)
    twice = lambda v: np.concatenate([v, v], 1).T[:, :, None]
    conv_w = a["conv_w"].reshape(DEPTH, CONV_W * GT, P).transpose(2, 0, 1)
    vecs = np.concatenate([twice(a["q_norm"]), twice(a["k_norm"]), two(a["pool_scale"]), two(a["conv_b"]), two(a["conv_ln_g"]),
                           two(a["conv_ln_b"]), two(a["gate_norm"]), conv_w], 2).reshape(P, -1)
    pool_w = np.zeros((DEPTH, P, GT, P), np.float32)
    for g in range(4):
        lanes = slice(64 * (g % 2), 64 * (g % 2) + 64)
        pool_w[:, lanes, g // 2, lanes] = a["pool_w"][:, g]
    tok = np.concatenate([a["x_prompt"].reshape(SEQ, D_MODEL), a["x_sample"].reshape(NS, D_MODEL)])
    arrays = {
        "xT": tok.reshape(TOK, DT, P).transpose(2, 1, 0),
        "w8": w8.reshape(DEPTH * W8_ROWS, 2, P, N8),
        "w11": w11.reshape(DEPTH * W11_ROWS, 2, P, N11),
        "gains": gains,
        "vecs": vecs,
        "consts": _constants(np),
        "pool_w": pool_w,
        "conv_pw": a["conv_pw"].reshape(DEPTH, GT, P, GT * P).transpose(0, 2, 1, 3),
        "sp_wT": a["spatial_w"].transpose(0, 3, 1, 2),
        "sp_b": a["spatial_b"],
        "cache_kT": a["cache_k"].reshape(DEPTH, n_pool, PAGE, GT, P).transpose(0, 1, 4, 3, 2),
        "cache_v": a["cache_v"].reshape(DEPTH, n_pool, PAGE, GT * P),
        "conv_hist": a["state_conv"].reshape(DEPTH, DEC_B, CONV_HIST, GT, P).transpose(0, 3, 4, 1, 2),
        "pool_hist": a["state_pool"].reshape(DEPTH, DEC_B, POOL_HIST, GT, P).transpose(0, 3, 4, 1, 2),
        "pages": a["page_table"].reshape(1, DEC_B * PAGES),
    }
    outs = {"yT": [P, DT, TOK], "kT": [DEPTH, GT, P, TOK], "vT": [DEPTH, GT, P, TOK],
            "poolT": [DEPTH, GT, P, POOL_HIST], "pool_sT": [DEPTH, GT, P, DEC_B, POOL_HIST],
            "convT": [DEPTH, GT, P, CONV_HIST], "conv_sT": [DEPTH, GT, P, DEC_B, CONV_HIST],
            "gateT": [DEPTH, GT, P, NS]}
    nc = bacc.Bacc("TRN2", target_bir_lowering=False, num_devices=1)
    args, feed = [], {}
    for name, v in arrays.items():
        v = np.ascontiguousarray(v)
        feed[f"in_{name}"] = v
        args.append(nc.dram_tensor(f"in_{name}", v.shape, mybir.dt.from_np(v.dtype), kind="ExternalInput").ap())
    for name, shape in outs.items():
        args.append(nc.dram_tensor(f"out_{name}", shape, F32, kind="ExternalOutput").ap())
    hybrid_decoder(nc, *args)
    r = run(nc, [feed], core_ids=[0]).results[0]
    o = {name: np.asarray(r[f"out_{name}"]) for name in outs}

    y = o["yT"].transpose(2, 1, 0).reshape(TOK, D_MODEL)
    width = GT * P

    def rows(t):
        return np.ascontiguousarray(t.transpose(0, 3, 1, 2)).reshape(DEPTH, -1, width)

    def state(t):
        return np.ascontiguousarray(t.transpose(0, 3, 4, 1, 2)).reshape(DEPTH, DEC_B, -1, width)

    k, v = rows(o["kT"]), rows(o["vT"])
    prompt = lambda t: t[:, :SEQ].reshape(DEPTH, 1, SEQ, HEADS, HEAD)
    sample = lambda t: t[:, SEQ:].reshape(DEPTH, DEC_B, DEC_T, HEADS, HEAD)
    return (y[:SEQ].reshape(1, SEQ, D_MODEL), y[SEQ:].reshape(DEC_B, DEC_T, D_MODEL),
            prompt(k), prompt(v), sample(k), sample(v),
            rows(o["poolT"]).reshape(DEPTH, 1, POOL_HIST, width), state(o["pool_sT"]),
            rows(o["convT"]).reshape(DEPTH, 1, CONV_HIST, width), state(o["conv_sT"]),
            rows(o["gateT"]).reshape(DEPTH, DEC_B, DEC_T, width))
```

```python
from contextlib import ExitStack

import concourse.bass as bass
from concourse import mybir

F32 = mybir.dt.float32
F32R = mybir.dt.float32r
I32 = mybir.dt.int32
ALU = mybir.AluOpType
ACT = mybir.ActivationFunctionType
AX = mybir.AxisListType

P = 128
DEPTH, D_MODEL, FFN = 2, 1024, 2816
SEQ, DEC_B, DEC_T = 256, 8, 8
NS = DEC_B * DEC_T
TOK = SEQ + NS
PAST, PAGE = 256, 128
PAGES = PAST // PAGE
HEADS, HEAD = 4, 64
KEYS = PAST + DEC_T
POOL_HIST, CONV_W, CONV_HIST = 15, 31, 30
RMS_EPS, LN_EPS = 1e-6, 1e-5
SCALE = HEAD ** -0.5
DT = D_MODEL // P
FT = FFN // P
GT = 2

IT_G, IT_D, IT_I, IT_O = FT // 2, DT, 4, 2
BASE_G1 = 0
BASE_D1 = BASE_G1 + IT_G
BASE_I = BASE_D1 + IT_D
BASE_O = BASE_I + IT_I
BASE_G2 = BASE_O + IT_O
BASE_D2 = BASE_G2 + IT_G
ITS = BASE_D2 + IT_D
W8_G1, W8_I, W8_O, W8_G2, W8_ROWS = 0, IT_G, IT_G + IT_I, IT_G + IT_I + IT_O, 2 * IT_G + IT_I + IT_O
W11_ROWS = 2 * IT_D
N8, N11 = 16 * P, 11 * P
HALVES8 = ((0, 8), (0, 8), (8, 8), (8, 8))
HALVES11 = ((0, 6), (0, 6), (6, 5), (6, 5))
T_G1 = 0
T_D1 = T_G1 + 4 * IT_G
T_I = T_D1 + DT
T_O = T_I + 16
T_G2 = T_O + DT
T_D2 = T_G2 + 4 * IT_G
TILES = T_D2 + DT

V_QG, V_KG, V_PS, V_CB, V_LG, V_LB, V_GG, V_CW = 0, 1, 2, 4, 6, 8, 10, 12
NV = V_CW + CONV_W * GT
CONSTS = (("ones", P), ("ident", P), ("dist", 3 * P), ("alibi", KEYS), ("newm", 2 * NS), ("bmask", NS),
          ("e8", NS), ("gsel", GT * P), ("tril", P), ("hsum", 4 * 8), ("hrep", 4 * P),
          ("first", GT * (POOL_HIST + 1)), ("window", GT))
NC_ = sum(n for _, n in CONSTS)
SMALLS = 8
STATES = 11


class Signal:

    def __init__(self, sem, per_layer, head=0):
        self.sem, self.per, self.head = sem, per_layer, head

    def at(self, layer, k):
        return layer * self.per + (k + self.head)


def hybrid_decoder(nc, xT, w8, w11, gains, vecs, consts, pool_w, conv_pw, sp_wT, sp_b,
                   cache_kT, cache_v, conv_hist, pool_hist, pages,
                   yT, kT, vT, poolT, pool_sT, convT, conv_sT, gateT):
    ctx = ExitStack()
    with ctx:
        place = [16512]

        def sb(name, shape, dt=F32, at=None):
            n = 4
            for s in shape[1:]:
                n *= s
            offset = place[0] if at is None else at[0]
            t = nc.alloc_sbuf_tensor_at(name, shape, dt, offset=offset)
            end = offset + (n + 31) // 32 * 32
            if at is None:
                place[0] = end
                assert end <= 229344, (name, end)
            else:
                at[0] = end
                assert end <= at[1], (name, end, at[1])
            return t

        raw_a = sb("raw_a", [P, N8])
        raw_b = sb("raw_b", [P, N8])
        w_hi = sb("w_hi", [P, 4, 8 * P], F32R)
        w_lo = sb("w_lo", [P, 4, 8 * P], F32R)
        x = sb("x", [P, DT, TOK])
        mix_place = place[0]
        mix_hi = sb("mix_hi", [P, DT, TOK], F32R)
        mix_lo = sb("mix_lo", [P, DT, TOK], F32R)
        norm_region = [place[0], None]
        xg_hi = sb("xg_hi", [P, DT, TOK], F32R)
        xg_lo = sb("xg_lo", [P, DT, TOK], F32R)
        norm_region[1] = place[0]
        ffn_region = [place[0], None]
        h_hi = sb("h_hi", [P, FT, TOK], F32R)
        h_lo = sb("h_lo", [P, FT, TOK], F32R)
        ffn_region[1] = place[0]
        cst = sb("cst", [P, NC_])
        gain = sb("gain", [P, (3 * DEPTH + 1) * DT])
        vec = sb("vec", [P, DEPTH * NV])
        page_row = sb("page_row", [1, DEC_B * PAGES], I32)
        w_pool = sb("w_pool", [P, GT, P])
        w_pw = sb("w_pw", [P, GT, GT * P])
        w_sp = sb("w_sp", [P, HEADS, P])
        b_sp = sb("b_sp", [HEADS, P])
        bias_sp = sb("bias_sp", [HEADS, TOK])
        w_sps = sb("w_sps", [NS, HEADS, DEC_B, DEC_T])
        conv_in = sb("conv_in", [P, GT, CONV_HIST + SEQ + DEC_B * (CONV_HIST + DEC_T)])
        pool_in = sb("pool_in", [P, GT, POOL_HIST + SEQ + DEC_B * (POOL_HIST + DEC_T)])
        conv_y = sb("conv_y", [P, GT, TOK])
        rms = sb("rms", [P, TOK])
        root = sb("root", [P, TOK])
        sumsq = sb("sumsq", [P, TOK])
        square = sb("square", [P, 2, TOK])
        tmp = sb("tmp", [P, 8, TOK])
        q_pad = sb("q_pad", [P, GT, DEC_B, 32])
        stat = sb("stat", [P, 64])
        prob = sb("prob", [P, HEADS, 3 * P])
        prob_s = sb("prob_s", [P, 2, KEYS])

        k_all = sb("k_all", [P, GT, DEC_B, KEYS], at=ffn_region)
        v_past = sb("v_past", [P, DEC_B * PAGES, GT * P], at=ffn_region)
        qk = sb("qk", [P, 4, TOK], at=ffn_region)
        z_v = sb("z_v", [P, GT, TOK], at=ffn_region)
        z_u = sb("z_u", [P, GT, TOK], at=ffn_region)
        z_w = sb("z_w", [P, GT, TOK], at=ffn_region)
        v_tok = sb("v_tok", [P, 2, GT * P], at=ffn_region)
        v_tok_s = sb("v_tok_s", [NS, GT * P], at=ffn_region)
        w_tok = sb("w_tok", [P, 2, GT * P], at=ffn_region)
        w_tok_s = sb("w_tok_s", [NS, GT * P], at=ffn_region)
        prob_t = sb("prob_t", [P, HEADS, 3 * P], at=norm_region)
        prob_st = sb("prob_st", [P, 2, PAST], at=norm_region)
        prob_new = sb("prob_new", [P, 2, DEC_B, DEC_T], at=norm_region)
        prob_nt = sb("prob_nt", [NS, 2, P], at=norm_region)
        out_s = sb("out_s", [P, 2, GT * P], at=norm_region)
        att_s = sb("att_s", [P, GT, NS], at=norm_region)
        win1 = sb("win1", [P, GT, POOL_HIST + SEQ + DEC_B * (POOL_HIST + DEC_T)],
                  at=[mix_place + 2 * TOK * 4, mix_place + 5 * TOK * 4])
        win2 = sb("win2", [P, GT, POOL_HIST + SEQ + DEC_B * (POOL_HIST + DEC_T)],
                  at=[mix_place + (DT + 2) * TOK * 4, mix_place + (DT + 5) * TOK * 4])
        pool_m = tmp[:, 6:8, :]
        z_a = tmp[:, 0:2, :]
        z_g = tmp[:, 2:4, :]
        qk_square = tmp[:, 4:8, :]
        qk_root = tmp[0:8, 2, :]
        gm_sq = tmp[:, 0:2, :]
        gm_root = tmp[:, 2, :]
        gated = tmp[:, 4:6, :]
        conv_sq = tmp[:, 0:2, :]
        conv_root = tmp[:, 3, :]

        at, views = 0, {}
        for name, n in CONSTS:
            views[name] = cst[:, at:at + n]
            at += n
        ident = views["ident"]

        bank = [ctx.enter_context(nc.psum_tensor(f"bank{i}", [P, 512], F32)) for i in range(8)]

        def sig(name, per_layer, head=0):
            return Signal(ctx.enter_context(nc.semaphore(name)), per_layer, head)

        gain_in = sig("gain_in", 0)
        consts_in = sig("consts_in", 0)
        x_in = sig("x_in", 0)
        raw_a_in = sig("raw_a_in", 16 * ITS)
        raw_b_in = sig("raw_b_in", 16 * ITS)
        small_in = sig("small_in", 16 * SMALLS)
        kv_in = sig("kv_in", 16 * 2 * DEC_B * PAGES)
        states_out = sig("states_out", 16 * STATES, 16)
        y_out = sig("y_out", 0)
        passed = sig("passed", 0)
        split_hi = sig("split_hi", 4 * ITS)
        split = sig("split", 4 * ITS, 4)
        slots = sig("slots", 4 * ITS, 4)
        taken = sig("taken", TILES, 4)
        xg_hi_ok = sig("xg_hi_ok", 3 * DT, DT)
        xg_lo_ok = sig("xg_lo_ok", 3 * DT, DT)
        squared = sig("squared", 3 * DT, DT)
        summed = sig("summed", 3 * (DT + 1), DT + 1)
        norm_sum = sig("norm_sum", 3)
        norm_root = sig("norm_root", 3)
        norm_ok = sig("norm_ok", 3)
        silu_ok = sig("silu_ok", 2 * FT)
        h_ok = sig("h_ok", 2 * FT)
        h_hi_ok = sig("h_hi_ok", 2 * FT)
        h_lo_ok = sig("h_lo_ok", 2 * FT)
        zeros_ok = sig("zeros_ok", 0)
        glu_sig = sig("glu_sig", 2)
        glu_ok = sig("glu_ok", 4)
        taps = sig("taps", 2 * CONV_W)
        batch_taps = sig("batch_taps", 2 * CONV_W)
        qk_sq = sig("qk_sq", 4)
        qk_sum = sig("qk_sum", 1)
        qk_rt = sig("qk_rt", 1)
        qk_inv = sig("qk_inv", 1)
        qk_rep = sig("qk_rep", 4)
        qk_ok = sig("qk_ok", 4)
        pads = sig("pads", 6)
        sp_ok = sig("sp_ok", 4)
        sp_rep = sig("sp_rep", 1)
        v_tr = sig("v_tr", 2)
        v_copied = sig("v_copied", 2)
        p_scores = sig("p_scores", 4)
        p_biased = sig("p_biased", 4)
        p_max = sig("p_max", 3)
        p_exp = sig("p_exp", 8)
        p_norm = sig("p_norm", 3)
        p_tr = sig("p_tr", 4)
        p_copied = sig("p_copied", 4)
        p_att = sig("p_att", 2)
        p_att_hi = sig("p_att_hi", 2)
        s_scores = sig("s_scores", 2)
        s_biased = sig("s_biased", 2)
        s_max = sig("s_max", 2)
        s_exp = sig("s_exp", 2)
        s_norm = sig("s_norm", 3)
        s_tr = sig("s_tr", 2)
        s_copied = sig("s_copied", 4)
        s_out = sig("s_out", 2)
        s_out_ok = sig("s_out_ok", 2)
        s_out_tr = sig("s_out_tr", 1)
        s_att = sig("s_att", 4)
        s_att_hi = sig("s_att_hi", 1)
        gelu_ok = sig("gelu_ok", 4)
        gm_sq_ok = sig("gm_sq_ok", 2)
        gm_sum = sig("gm_sum", 1)
        gm_rt = sig("gm_rt", 1)
        gm_v = sig("gm_v", 3)
        gm_tr = sig("gm_tr", 2)
        gm_copied = sig("gm_copied", 2)
        gm_mm = sig("gm_mm", 2)
        gm_ok = sig("gm_ok", 2)
        gm_hi = sig("gm_hi", 2)
        pool_step = sig("pool_step", 12)
        pool_mm = sig("pool_mm", 2)
        pool_hi = sig("pool_hi", 2)
        cv_mean = sig("cv_mean", 1)
        cv_cent = sig("cv_cent", 2)
        cv_sq = sig("cv_sq", 2)
        cv_var = sig("cv_var", 1)
        cv_rt = sig("cv_rt", 1)
        cv_ln = sig("cv_ln", 3)
        cv_act = sig("cv_act", 2)
        cv_pw = sig("cv_pw", 2)
        cv_hi = sig("cv_hi", 2)
        mix_ok = sig("mix_ok", 9)
        MIX_ORDER = ((6, 3), (7, 4), (2, 5), (3, 6), (4, 7), (5, 8), (0, 9), (1, 9))

        def split_tokens(ap2d, width, hist):
            prompt = ap2d[:, 0:hist + SEQ]
            rows = ap2d[:, hist + SEQ:hist + SEQ + DEC_B * width].rearrange("p (b t) -> p b t", b=DEC_B)
            return prompt, rows

        def batch(ap2d):
            return ap2d.rearrange("p (b t) -> p b t", b=DEC_B)

        def hold(engine, sem, value):
            engine.wait_ge(sem, value)
            engine.sem_inc(passed.sem, 1)

        block = ctx.enter_context(nc.Block())

        @block.sync
        def _(sp):
            sp.dma_start(gain[:, :], gains).then_inc(gain_in.sem, 16)
            for n in range(2):
                half = slice(n * DT // 2, (n + 1) * DT // 2)
                sp.dma_start(x[:, half, :], xT[:, half, :]).then_inc(x_in.sem, 16)

            def load(L, base, i, weights, row, n):
                for buf, part, done, landed in ((raw_a, 0, 3, raw_a_in), (raw_b, 1, 4, raw_b_in)):
                    sp.wait_ge(split.sem, L * split.per + (base + i) * 4 + done)
                    src = weights[bass.ds(row, 1), part, :, :].rearrange("a p n -> (a p) n")
                    sp.dma_start(buf[:, 0:n], src).then_inc(landed.sem, 16)

            def load_small(L):
                hold(sp, states_out.sem, states_out.at(L, 0))
                one = bass.ds(L, 1)
                for c in range(GT):
                    _, conv_rows = split_tokens(conv_in[:, c, :], CONV_HIST + DEC_T, CONV_HIST)
                    sp.dma_start(conv_rows[:, :, 0:CONV_HIST],
                                 conv_hist[one, c, :, :, :].rearrange("a p b t -> (a p) b t")).then_inc(small_in.sem, 16)
                    _, pool_rows = split_tokens(pool_in[:, c, :], POOL_HIST + DEC_T, POOL_HIST)
                    sp.dma_start(pool_rows[:, :, 0:POOL_HIST],
                                 pool_hist[one, c, :, :, :].rearrange("a p b t -> (a p) b t")).then_inc(small_in.sem, 16)
                for dst, src in ((w_pool, pool_w), (w_pw, conv_pw), (w_sp, sp_wT)):
                    sp.dma_start(dst[:, :, :], src[one, :, :, :].rearrange("a p c n -> (a p) c n")).then_inc(small_in.sem, 16)
                sp.dma_start(b_sp[:, :], sp_b[one, :, :].rearrange("a g t -> (a g) t")).then_inc(small_in.sem, 16)

            def load_past(L, b0, b1):
                one = bass.ds(L, 1)
                with sp.Fori(b0, b1) as b:
                    for n in range(PAGES):
                        page = sp.value_load(page_row[0:1, bass.ds(b * PAGES + n, 1)],
                                             min_val=0, max_val=cache_v.shape[1] - 1)
                        at_page = bass.ds(page, 1)
                        sp.dma_start(k_all[:, :, bass.ds(b, 1), n * PAGE:(n + 1) * PAGE].rearrange("p c b t -> p c (b t)"),
                                     cache_kT[one, at_page, :, :, :].rearrange("l a p c t -> (l a p) c t")).then_inc(kv_in.sem, 16)
                        sp.dma_start(v_past[:, bass.ds(b * PAGES + n, 1), :].rearrange("p b t -> p (b t)"),
                                     cache_v[one, at_page, :, :].rearrange("l a p n -> (l a p) n")).then_inc(kv_in.sem, 16)

            def store_states(L):
                layer = bass.ds(L, 1)
                sp.wait_ge(mix_ok.sem, mix_ok.at(L, mix_ok.per))
                sp.dma_start(kT[layer, :, :, :].rearrange("l c p t -> p (l c) t"), qk[:, 1:4:2, :]).then_inc(states_out.sem, 16)
                sp.dma_start(vT[layer, :, :, :].rearrange("l c p t -> p (l c) t"), z_v[:, :, :]).then_inc(states_out.sem, 16)
                sp.dma_start(poolT[layer, :, :, :].rearrange("l c p t -> p (l c) t"), pool_in[:, :, SEQ:SEQ + POOL_HIST]).then_inc(states_out.sem, 16)
                sp.dma_start(convT[layer, :, :, :].rearrange("l c p t -> p (l c) t"), conv_in[:, :, SEQ:SEQ + CONV_HIST]).then_inc(states_out.sem, 16)
                sp.dma_start(gateT[layer, :, :, :].rearrange("l c p t -> p (l c) t"), z_w[:, :, SEQ:TOK]).then_inc(states_out.sem, 16)
                for c in range(GT):
                    _, rows = split_tokens(pool_in[:, c, :], POOL_HIST + DEC_T, POOL_HIST)
                    sp.dma_start(pool_sT[layer, c, :, :, :].rearrange("l p b t -> (l p) b t"), rows[:, :, DEC_T:]).then_inc(states_out.sem, 16)
                    _, rows = split_tokens(conv_in[:, c, :], CONV_HIST + DEC_T, CONV_HIST)
                    for half in range(2):
                        sp.dma_start(conv_sT[layer, c, :, 4 * half:4 * half + 4, :].rearrange("l p b t -> (l p) b t"),
                                     rows[:, 4 * half:4 * half + 4, DEC_T:]).then_inc(states_out.sem, 16)

            sp.dma_start(cst[:, :], consts).then_inc(consts_in.sem, 16)
            sp.dma_start(vec[:, :], vecs).then_inc(consts_in.sem, 16)
            sp.dma_start(page_row[:, :], pages).then_inc(consts_in.sem, 16)
            with sp.Fori(0, DEPTH) as L:
                with sp.Fori(0, IT_G) as i:
                    load(L, BASE_G1, i, w8, L * W8_ROWS + W8_G1 + i, N8)
                load_small(L)
                with sp.Fori(0, IT_D) as i:
                    load(L, BASE_D1, i, w11, L * W11_ROWS + i, N11)
                with sp.Fori(0, 2) as i:
                    load(L, BASE_I, i, w8, L * W8_ROWS + W8_I + i, N8)
                hold(sp, slots.sem, slots.at(L, 4 * BASE_I))
                for n in range(2):
                    load_past(L, n * DEC_B // 2, (n + 1) * DEC_B // 2)
                    load(L, BASE_I, 2 + n, w8, L * W8_ROWS + (W8_I + 2 + n), N8)
                with sp.Fori(0, IT_O) as i:
                    load(L, BASE_O, i, w8, L * W8_ROWS + W8_O + i, N8)
                store_states(L)
                with sp.Fori(0, IT_G) as i:
                    load(L, BASE_G2, i, w8, L * W8_ROWS + W8_G2 + i, N8)
                with sp.Fori(0, IT_D) as i:
                    load(L, BASE_D2, i, w11, L * W11_ROWS + IT_D + i, N11)
            sp.wait_ge(taken.sem, taken.at(DEPTH, 0))
            sp.dma_start(yT, x[:, :, :]).then_inc(y_out.sem, 16)
            sp.wait_ge(y_out.sem, 16)
            sp.wait_ge(states_out.sem, states_out.at(DEPTH, 0))

        @block.gpsimd
        def _(pool):
            pool.sem_inc(split.sem, 4)

            def split_iteration(L, base, i, halves):
                for j in range(4):
                    buf = (raw_a, raw_b)[j % 2]
                    first, count = halves[j]
                    pool.wait_ge(split_hi.sem, L * split_hi.per + (base + i) * 4 + j + 1)
                    pool.tensor_tensor(w_lo[:, j, 0:count * P], buf[:, first * P:(first + count) * P],
                                       w_hi[:, j, 0:count * P].bitcast(F32), ALU.subtract).then_inc(split.sem, 1)

            def window_sums(L):
                width = POOL_HIST + SEQ + DEC_B * (POOL_HIST + DEC_T)
                pool.wait_ge(taken.sem, taken.at(L, T_I + 11))
                pool.wait_ge(small_in.sem, small_in.at(L, 16 * SMALLS))
                steps = [0]

                def done(ins):
                    ins.then_inc(pool_step.sem, 1)
                    steps[0] += 1
                    hold(pool, pool_step.sem, pool_step.at(L, steps[0]))

                def add(dst, src, lanes, c, shift, lead):
                    done(pool.tensor_tensor(dst[lanes, c, lead:width], src[lanes, c, lead:width],
                                            src[lanes, c, lead - shift:width - shift], ALU.add))

                low, high, every = slice(0, 64), slice(64, P), slice(0, P)
                add(win1, pool_in, every, 0, 1, 1)
                add(win1, pool_in, every, 1, 1, 1)
                add(win2, pool_in, low, 0, 1, 1)
                add(win2, win1, high, 0, 2, 3)
                add(win2, win1, every, 1, 2, 3)
                add(win1, win2, every, 1, 4, 7)
                add(win2, win1, high, 1, 8, 15)
                done(pool.tensor_copy(win2[low, 1, 15:width], win1[low, 1, 15:width]))
                hold(pool, qk_ok.sem, qk_ok.at(L, 4))
                first = views["first"].rearrange("p (c t) -> p c t", c=GT)
                for c in range(GT):
                    _, mean_rows = split_tokens(win2[:, c, :], POOL_HIST + DEC_T, POOL_HIST)
                    scale = views["window"][:, c:c + 1]
                    pool.tensor_scalar(pool_m[:, c, 0:SEQ], win2[:, c, POOL_HIST:POOL_HIST + SEQ], scale, 1.0, ALU.mult, ALU.mult)
                    last = pool.tensor_scalar(batch(pool_m[:, c, SEQ:TOK]), mean_rows[:, :, POOL_HIST:], scale, 1.0, ALU.mult, ALU.mult)
                done(last)
                done(pool.tensor_tensor(pool_m[:, :, 0:POOL_HIST + 1], win2[:, :, POOL_HIST:2 * POOL_HIST + 1], first, ALU.mult))
                done(pool.tensor_tensor(pool_m[:, :, 0:SEQ], pool_m[:, :, 0:SEQ],
                                        pool_in[:, :, POOL_HIST:POOL_HIST + SEQ], ALU.subtract))
                for c in range(GT):
                    _, rows = split_tokens(pool_in[:, c, :], POOL_HIST + DEC_T, POOL_HIST)
                    last = pool.tensor_tensor(batch(pool_m[:, c, SEQ:TOK]), batch(pool_m[:, c, SEQ:TOK]),
                                              rows[:, :, POOL_HIST:], ALU.subtract)
                last.then_inc(pool_step.sem, 1)
                assert steps[0] + 1 == pool_step.per

            with pool.Fori(0, DEPTH) as L:
                with pool.Fori(0, IT_G) as i:
                    split_iteration(L, BASE_G1, i, HALVES8)
                with pool.Fori(0, IT_D) as i:
                    split_iteration(L, BASE_D1, i, HALVES11)
                with pool.Fori(0, IT_I) as i:
                    split_iteration(L, BASE_I, i, HALVES8)
                window_sums(L)
                with pool.Fori(0, IT_O) as i:
                    split_iteration(L, BASE_O, i, HALVES8)
                with pool.Fori(0, IT_G) as i:
                    split_iteration(L, BASE_G2, i, HALVES8)
                with pool.Fori(0, IT_D) as i:
                    split_iteration(L, BASE_D2, i, HALVES11)

        @block.tensor
        def _(pe):
            pe.sem_inc(slots.sem, 4)
            pe.wait_ge(consts_in.sem, 48)

            def use_slot(L, base, i, j, out, k_tiles, in_hi, in_lo, first, last, before_k=None):
                pe.wait_ge(split.sem, L * split.per + (base + i) * 4 + (j + 1 + split.head))
                for n, k in enumerate(k_tiles):
                    if before_k:
                        before_k(n, k)
                    hi, lo = w_hi[:, j, n * P:(n + 1) * P], w_lo[:, j, n * P:(n + 1) * P]
                    pe.matmul(out, hi, in_hi[:, k, :], start=first and n == 0, stop=False)
                    pe.matmul(out, hi, in_lo[:, k, :], start=False, stop=False)
                    end = n == len(k_tiles) - 1
                    mm = pe.matmul(out, lo, in_hi[:, k, :], start=False, stop=last and end)
                mm.then_inc(slots.sem, 1)

            def bank_free(L, tile):
                pe.wait_ge(taken.sem, L * taken.per + tile + 1)

            def sum_squares(L, n):
                pe.wait_ge(summed.sem, L * summed.per + (n + 1) * (DT + 1))
                pe.matmul(bank[6][:, 0:TOK], views["ones"], sumsq[:, :], start=True, stop=True).then_inc(norm_sum.sem, 1)

            def column(L, base, tile0, norm, i, j, first=False):
                bank_free(L, i * 4 + (tile0 + j))
                ready = (lambda n, k: pe.wait_ge(xg_lo_ok.sem, L * xg_lo_ok.per + norm * DT + k + 1)) if first and j == 0 else None
                use_slot(L, base, i, j, bank[j][:, 0:TOK], range(8), xg_hi, xg_lo, True, True, ready)
                if first and j == 0:
                    sum_squares(L, norm)

            def columns(L, base, tile0, norm, i, first=False):
                for j in range(4):
                    column(L, base, tile0, norm, i, j, first)

            def down(L, base, tile0, ffn):
                with pe.Fori(0, IT_D // 2) as i2:
                    for e in range(2):
                        i = i2 * 2 + e
                        pe.wait_ge(taken.sem, L * taken.per + i + (tile0 - 2 + 1 + 4))
                        for j, ks in enumerate((range(0, 6), range(11, 17), range(6, 11), range(17, 22))):
                            pe.wait_ge(h_lo_ok.sem, h_lo_ok.at(L, ffn * FT + ks[-1] + 1))
                            use_slot(L, base, i, j, bank[4 + e][:, 0:TOK], ks, h_hi, h_lo, j == 0, j == 3)

            def gate_up(L, base, tile0, norm):
                columns(L, base, tile0, norm, 0, first=True)
                with pe.Fori(1, IT_G) as i:
                    columns(L, base, tile0, norm, i)

            def qk_sums(L):
                pe.wait_ge(qk_sq.sem, qk_sq.at(L, 4))
                hsum = views["hsum"].rearrange("p (t n) -> p t n", t=4)
                for t in range(4):
                    mm = pe.matmul(bank[4][0:8, 0:TOK], hsum[:, t, :], qk_square[:, t, :], start=t == 0, stop=t == 3)
                mm.then_inc(qk_sum.sem, 1)

            def qk_spread(L):
                pe.wait_ge(qk_inv.sem, qk_inv.at(L, 1))
                hrep = views["hrep"].rearrange("p (t n) -> p t n", t=4)
                for t in range(4):
                    pe.matmul(bank[4 + t][:, 0:TOK], hrep[0:8, t, :], qk_root, start=True, stop=True).then_inc(qk_rep.sem, 1)

            def prompt_scores(L):
                pe.wait_ge(qk_ok.sem, qk_ok.at(L, 4))
                for h in range(HEADS):
                    c, lanes = h // 2, slice(64 * (h % 2), 64 * (h % 2) + 64)
                    for t in range(2):
                        mm = pe.matmul(bank[4 + h][:, t * P:t * P + (t + 1) * P], qk[lanes, 2 * c, t * P:(t + 1) * P],
                                       qk[lanes, 2 * c + 1, 0:(t + 1) * P], start=True, stop=True)
                    mm.then_inc(p_scores.sem, 1)

            def value_rows(L):
                pe.wait_ge(taken.sem, taken.at(L, T_O))
                for c in range(GT):
                    for t in range(2):
                        mm = pe.transpose(bank[0][:, t * 2 * P + c * P:t * 2 * P + (c + 1) * P], z_v[:, c, t * P:(t + 1) * P], ident)
                mm.then_inc(v_tr.sem, 1)
                pe.wait_ge(sp_ok.sem, sp_ok.at(L, 3))
                pe.matmul(bank[1][0:NS, 256:288].rearrange("p (g t) -> p g t", g=HEADS), views["e8"][0:8, :],
                          w_sp[0:8, :, 0:DEC_T], start=True, stop=True).then_inc(sp_rep.sem, 1)
                for c in range(GT):
                    mm = pe.transpose(bank[1][0:NS, c * P:(c + 1) * P], z_v[:, c, SEQ:TOK], ident)
                mm.then_inc(v_tr.sem, 1)

            def batch_scores(L):
                pe.wait_ge(pads.sem, pads.at(L, 6))
                pe.wait_ge(kv_in.sem, kv_in.at(L, kv_in.per))
                for g in range(2):
                    pe.wait_ge(p_biased.sem, p_biased.at(L, g + 1))
                    for b4 in range(4):
                        b = 4 * g + b4
                        for c in range(GT):
                            mm = pe.matmul(bank[4 + g][32 * b4:32 * b4 + 32, 0:KEYS], q_pad[:, c, b, :], k_all[:, c, b, :],
                                           start=c == 0, stop=c == 1)
                    mm.then_inc(s_scores.sem, 1)

            def gate_square_sum(L):
                pe.wait_ge(gm_sq_ok.sem, gm_sq_ok.at(L, 2))
                pe.wait_ge(p_biased.sem, p_biased.at(L, 3))
                for c in range(GT):
                    mm = pe.matmul(bank[6][:, 0:TOK], views["ones"], gm_sq[:, c, :], start=c == 0, stop=c == 1)
                mm.then_inc(gm_sum.sem, 1)

            def conv_mean(L):
                pe.wait_ge(taps.sem, taps.at(L, taps.per))
                pe.wait_ge(batch_taps.sem, batch_taps.at(L, batch_taps.per))
                pe.wait_ge(p_biased.sem, p_biased.at(L, 4))
                for c in range(GT):
                    mm = pe.matmul(bank[7][:, 0:TOK], views["ones"], conv_y[:, c, :], start=c == 0, stop=c == 1)
                mm.then_inc(cv_mean.sem, 1)

            def conv_variance(L):
                pe.wait_ge(cv_sq.sem, cv_sq.at(L, 2))
                for c in range(GT):
                    mm = pe.matmul(bank[7][:, 0:TOK], views["ones"], conv_sq[:, c, :], start=c == 0, stop=c == 1)
                mm.then_inc(cv_var.sem, 1)

            def prompt_attention_transposes(L):
                pe.wait_ge(p_norm.sem, p_norm.at(L, 3))
                for h in range(HEADS):
                    before = ((s_biased, 1), (s_biased, 2), (gm_rt, 1), (cv_rt, 1))[h]
                    pe.wait_ge(before[0].sem, before[0].at(L, before[1]))
                    for n in range(3):
                        mm = pe.transpose(bank[4 + h][:, n * P:(n + 1) * P], prob[:, h, n * P:(n + 1) * P], ident)
                    mm.then_inc(p_tr.sem, 1)

            def gate_value_rows(L):
                pe.wait_ge(gm_v.sem, gm_v.at(L, 3))
                for c in range(GT):
                    for t in range(2):
                        mm = pe.transpose(bank[2][:, t * 2 * P + c * P:t * 2 * P + (c + 1) * P], z_w[:, c, t * P:(t + 1) * P], ident)
                mm.then_inc(gm_tr.sem, 1)
                for c in range(GT):
                    mm = pe.transpose(bank[3][0:NS, c * P:(c + 1) * P], z_w[:, c, SEQ:TOK], ident)
                mm.then_inc(gm_tr.sem, 1)

            def prompt_attention(L):
                pe.wait_ge(p_copied.sem, p_copied.at(L, 4))
                pe.wait_ge(v_copied.sem, v_copied.at(L, 1))
                for c in range(GT):
                    for h2 in range(2):
                        h, lanes = 2 * c + h2, slice(64 * h2, 64 * h2 + 64)
                        for t in range(2):
                            for kt in range(t + 1):
                                mm = pe.matmul(bank[4 + c][lanes, t * P:(t + 1) * P], v_tok[:, kt, h * 64:(h + 1) * 64],
                                               prob_t[:, h, (t + kt) * P:(t + kt + 1) * P], start=kt == 0, stop=kt == t)
                    mm.then_inc(p_att.sem, 1)

            def spatial_gates(L):
                pe.wait_ge(sp_ok.sem, sp_ok.at(L, 4))
                pe.wait_ge(v_copied.sem, v_copied.at(L, 2))
                pe.wait_ge(gm_copied.sem, gm_copied.at(L, 2))
                sel = views["gsel"].rearrange("p (c n) -> p c n", c=GT)
                for c in range(GT):
                    pe.matmul(bank[c][:, 0:TOK], sel[0:HEADS, c, :], bias_sp[:, :], start=True, stop=False, skip_group_check=True)
                    for h2 in range(2):
                        g, lanes = 2 * c + h2, slice(64 * h2, 64 * h2 + 64)
                        for t in range(2):
                            pe.matmul(bank[c][lanes, t * P:(t + 1) * P], w_tok[:, t, g * 64:(g + 1) * 64], w_sp[:, g, :],
                                      start=False, stop=False, skip_group_check=True)
                        mm = pe.matmul(bank[c][lanes, SEQ:TOK], w_tok_s[:, g * 64:(g + 1) * 64],
                                       w_sps[:, g, :, :].rearrange("p b t -> p (b t)"),
                                       start=False, stop=h2 == 1, skip_group_check=True)
                    mm.then_inc(gm_mm.sem, 1)

            def batch_probabilities(L):
                pe.wait_ge(s_norm.sem, s_norm.at(L, 3))
                for g in range(2):
                    for n in range(PAGES):
                        pe.transpose(bank[6 + g][:, n * P:(n + 1) * P], prob_s[:, g, n * P:(n + 1) * P], ident)
                    pe.transpose(bank[6 + g][0:NS, PAST:PAST + P], prob_new[:, g, :, :].rearrange("p b t -> p (b t)"),
                                 ident).then_inc(s_tr.sem, 1)

            def batch_attention(L):
                for g in range(2):
                    pe.wait_ge(s_copied.sem, s_copied.at(L, 2 * g + 2))
                    pe.matmul(bank[2 + g][:, 0:GT * P], prob_nt[:, g, :], v_tok_s[:, :], start=True, stop=False, skip_group_check=True)
                    for b4 in range(4):
                        for n in range(PAGES):
                            mm = pe.matmul(bank[2 + g][32 * b4:32 * b4 + 32, 0:GT * P],
                                           prob_st[:, g, n * P + 32 * b4:n * P + 32 * b4 + 32],
                                           v_past[:, (4 * g + b4) * PAGES + n, :], start=False,
                                           stop=b4 == 3 and n == PAGES - 1, skip_group_check=True)
                    mm.then_inc(s_out.sem, 1)

            def batch_attention_transposes(L):
                pe.wait_ge(s_out_ok.sem, s_out_ok.at(L, 2))
                for c in range(GT):
                    for g in range(2):
                        mm = pe.transpose(bank[6][:, (2 * c + g) * P:(2 * c + g + 1) * P], out_s[:, g, c * P:(c + 1) * P], ident)
                mm.then_inc(s_out_tr.sem, 1)

            def pool_map(L):
                pe.wait_ge(s_out_ok.sem, s_out_ok.at(L, 2))
                pe.wait_ge(pool_step.sem, pool_step.at(L, pool_step.per))
                for c in range(GT):
                    pe.matmul(bank[(7, 3)[c]][:, 0:TOK], w_pool[:, c, :], pool_m[:, c, :], start=True, stop=True).then_inc(pool_mm.sem, 1)

            def conv_map(L):
                pe.wait_ge(mix_ok.sem, mix_ok.at(L, 2))
                pe.wait_ge(cv_act.sem, cv_act.at(L, 2))
                for m in range(GT):
                    for c in range(GT):
                        mm = pe.matmul(bank[4 + m][:, 0:TOK], w_pw[:, c, m * P:(m + 1) * P], conv_y[:, c, :], start=c == 0, stop=c == 1)
                    mm.then_inc(cv_pw.sem, 1)

            with pe.Fori(0, DEPTH) as L:
                gate_up(L, BASE_G1, T_G1, 0)
                down(L, BASE_D1, T_D1, 0)
                columns(L, BASE_I, T_I, 1, 0, first=True)
                columns(L, BASE_I, T_I, 1, 1)
                pe.wait_ge(small_in.sem, small_in.at(L, small_in.per))
                column(L, BASE_I, T_I, 1, 2, 0)
                column(L, BASE_I, T_I, 1, 2, 1)
                qk_sums(L)
                column(L, BASE_I, T_I, 1, 2, 2)
                column(L, BASE_I, T_I, 1, 2, 3)
                qk_spread(L)
                column(L, BASE_I, T_I, 1, 3, 0)
                prompt_scores(L)
                column(L, BASE_I, T_I, 1, 3, 1)
                batch_scores(L)
                gate_square_sum(L)
                conv_mean(L)
                column(L, BASE_I, T_I, 1, 3, 2)
                conv_variance(L)
                column(L, BASE_I, T_I, 1, 3, 3)
                prompt_attention_transposes(L)
                value_rows(L)
                gate_value_rows(L)
                prompt_attention(L)
                batch_probabilities(L)
                spatial_gates(L)
                batch_attention(L)
                pool_map(L)
                conv_map(L)
                batch_attention_transposes(L)
                with pe.Fori(0, IT_O) as i:
                    for j in range(4):
                        bank_free(L, i * 4 + (T_O + j))
                        counts = dict(MIX_ORDER)
                        ready = (lambda n, k: pe.wait_ge(mix_ok.sem, mix_ok.at(L, counts[k]))) if j == 0 else None
                        use_slot(L, BASE_O, i, j, bank[j][:, 0:TOK], [k for k, _ in MIX_ORDER], mix_hi, mix_lo, True, True, ready)
                gate_up(L, BASE_G2, T_G2, 2)
                down(L, BASE_D2, T_D2, 1)

        @block.scalar
        def _(act):
            act.sem_inc(states_out.sem, 16)

            def root_of_norm(L, n):
                act.wait_ge(norm_sum.sem, norm_sum.at(L, n + 1))
                act.activation(root[:, :], bank[6][:, 0:TOK], ACT.Sqrt, bias=eps_rms, scale=1.0 / D_MODEL).then_inc(norm_root.sem, 1)

            def norm_input(gain_col, d, e, xg_col):
                act.activation(xg_hi[:, bass.ds(d, 1), :].rearrange("p a t -> p (a t)"), x[:, bass.ds(d, 1), :].rearrange("p a t -> p (a t)"),
                               ACT.Identity, scale=gain[:, bass.ds(gain_col, 1)]).then_inc(xg_hi_ok.sem, 1)
                hold(act, summed.sem, xg_col)
                act.activation(square[:, e, :], x[:, bass.ds(d, 1), :].rearrange("p a t -> p (a t)"), ACT.Square).then_inc(squared.sem, 1)

            def round_slot(L, base, i, j, halves):
                buf, landed = ((raw_a, raw_a_in), (raw_b, raw_b_in))[j % 2]
                first, count = halves[j]
                if j < 2:
                    act.wait_ge(landed.sem, L * landed.per + (base + i) * 16 + 16)
                act.wait_ge(slots.sem, L * slots.per + (base + i) * 4 + j + 1)
                act.activation(w_hi[:, j, 0:count * P], buf[:, first * P:(first + count) * P], ACT.Copy).then_inc(split_hi.sem, 1)

            def silu(L, i, m, tile0):
                act.wait_ge(taken.sem, L * taken.per + i * 4 + (tile0 + 2 * m + 1 + taken.head))
                act.activation(tmp[:, 2 + m, :], tmp[:, m, :], ACT.Silu).then_inc(silu_ok.sem, 1)

            def round_h(L, i, m, ffn):
                hold(act, h_ok.sem, L * h_ok.per + i * 2 + (ffn * FT + m + 1))
                act.activation(h_hi[:, bass.ds(i * 2 + m, 1), :].rearrange("p a t -> p (a t)"), tmp[:, 6 + m, :],
                               ACT.Copy).then_inc(h_hi_ok.sem, 1)

            def gate_up(L, base, tile0, ffn):
                def step(i, base_next, i_next, halves):
                    for m in range(2):
                        round_slot(L, base_next, i_next, 2 * m, halves)
                        silu(L, i, m, tile0)
                        round_slot(L, base_next, i_next, 2 * m + 1, halves)
                        round_h(L, i, m, ffn)

                with act.Fori(0, IT_G - 1) as i:
                    step(i, base, i + 1, HALVES8)
                step(IT_G - 1, base + IT_G, 0, HALVES11)

            def norm_tile(L, tile0, norm, d, e):
                hold(act, taken.sem, L * taken.per + d + (tile0 + 1 + taken.head))
                norm_input(L * (3 * DT) + d + norm * DT, d, e, L * summed.per + d + norm * (DT + 1))

            def down(L, base, tile0, norm, last):
                def step(i, e):
                    for j in range(4):
                        round_slot(L, base, i + 1, j, HALVES11)
                    norm_tile(L, tile0, norm, i, e)

                with act.Fori(0, DT // 2 - 1) as i2:
                    for e in range(2):
                        step(i2 * 2 + e, e)
                step(DT - 2, 0)
                if not last:
                    for j in range(4):
                        round_slot(L, BASE_I, 0, j, HALVES8)
                norm_tile(L, tile0, norm, DT - 1, 1)

            eps_rms, eps_ln = stat[:, 60:61], stat[:, 61:62]
            act.wait_ge(zeros_ok.sem, 1)
            act.wait_ge(gain_in.sem, 16)
            act.wait_ge(x_in.sem, 32)
            with act.Fori(0, DT // 2) as i:
                for e in range(2):
                    d = i * 2 + e
                    norm_input(d, d, e, d + 1)

            with act.Fori(0, DEPTH) as L:
                for j in range(4):
                    round_slot(L, BASE_G1, 0, j, HALVES8)
                root_of_norm(L, 0)
                gate_up(L, BASE_G1, T_G1, 0)
                down(L, BASE_D1, T_D1, 1, False)
                root_of_norm(L, 1)
                for c in range(GT):
                    round_slot(L, BASE_I, 1, 2 * c, HALVES8)
                    round_slot(L, BASE_I, 1, 2 * c + 1, HALVES8)
                    act.wait_ge(taken.sem, taken.at(L, T_I + 2 * c + 2))
                    act.activation(z_g[:, c, :], z_g[:, c, :], ACT.Sigmoid).then_inc(glu_sig.sem, 1)
                for t in range(4):
                    round_slot(L, BASE_I, 2, t, HALVES8)
                    act.wait_ge(taken.sem, taken.at(L, T_I + 4 + t + 1))
                    act.activation(qk_square[:, t, :], qk[:, t, :], ACT.Square).then_inc(qk_sq.sem, 1)
                round_slot(L, BASE_I, 3, 0, HALVES8)
                round_slot(L, BASE_I, 3, 1, HALVES8)
                act.wait_ge(qk_sum.sem, qk_sum.at(L, 1))
                act.activation(qk_root, bank[4][0:8, 0:TOK], ACT.Sqrt, bias=eps_rms[0:8, :], scale=1.0 / HEAD).then_inc(qk_rt.sem, 1)
                round_slot(L, BASE_I, 3, 2, HALVES8)
                round_slot(L, BASE_I, 3, 3, HALVES8)

                def gelu(z, tile):
                    act.wait_ge(taken.sem, taken.at(L, tile + 1))
                    act.activation(z, z, ACT.Gelu_apprx_tanh).then_inc(gelu_ok.sem, 1)

                for c in range(GT):
                    gelu(z_w[:, c, :], T_I + 9 + 2 * c)
                for c in range(GT):
                    act.wait_ge(gelu_ok.sem, gelu_ok.at(L, c + 1))
                    act.activation(gm_sq[:, c, :], z_w[:, c, :], ACT.Square).then_inc(gm_sq_ok.sem, 1)
                round_slot(L, BASE_O, 0, 0, HALVES8)
                gelu(z_u[:, 0, :], T_I + 12)
                act.wait_ge(p_max.sem, p_max.at(L, 3))
                for t in range(2):
                    for h in range(HEADS):
                        cols = slice(t * P, t * P + (t + 1) * P)
                        act.activation(prob[:, h, cols], prob[:, h, cols], ACT.Exp, bias=stat[:, 8 + 4 * t + h:9 + 4 * t + h],
                                       scale=SCALE, accum_out=stat[:, 16 + 4 * t + h:17 + 4 * t + h]).then_inc(p_exp.sem, 1)
                round_slot(L, BASE_O, 0, 1, HALVES8)
                act.wait_ge(s_max.sem, s_max.at(L, 2))
                for g in range(2):
                    act.activation(prob_s[:, g, :], prob_s[:, g, :], ACT.Exp, bias=stat[:, 34 + g:35 + g], scale=SCALE,
                                   accum_out=stat[:, 36 + g:37 + g]).then_inc(s_exp.sem, 1)
                act.wait_ge(gm_sum.sem, gm_sum.at(L, 1))
                act.activation(gm_root[:, :], bank[6][:, 0:TOK], ACT.Sqrt, bias=eps_rms, scale=1.0 / (GT * P)).then_inc(gm_rt.sem, 1)
                for c in range(GT):
                    act.wait_ge(cv_cent.sem, cv_cent.at(L, c + 1))
                    act.activation(conv_sq[:, c, :], conv_y[:, c, :], ACT.Square).then_inc(cv_sq.sem, 1)
                round_slot(L, BASE_O, 0, 2, HALVES8)
                act.wait_ge(cv_var.sem, cv_var.at(L, 1))
                act.activation(conv_root[:, :], bank[7][:, 0:TOK], ACT.Sqrt, bias=eps_ln, scale=1.0 / (GT * P)).then_inc(cv_rt.sem, 1)
                gelu(z_u[:, 1, :], T_I + 14)
                round_slot(L, BASE_O, 0, 3, HALVES8)
                for h in range(HEADS):
                    act.wait_ge(p_tr.sem, p_tr.at(L, h + 1))
                    act.activation(prob_t[:, h, :], bank[4 + h][:, 0:3 * P], ACT.Copy).then_inc(p_copied.sem, 1)
                act.wait_ge(v_tr.sem, v_tr.at(L, 1))
                act.activation(v_tok[:, :, :].rearrange("p t n -> p (t n)"), bank[0][:, :], ACT.Copy).then_inc(v_copied.sem, 1)
                act.wait_ge(v_tr.sem, v_tr.at(L, 2))
                act.activation(v_tok_s[:, :], bank[1][0:NS, 0:GT * P], ACT.Copy).then_inc(v_copied.sem, 1)
                act.wait_ge(gm_tr.sem, gm_tr.at(L, 1))
                act.activation(w_tok[:, :, :].rearrange("p t n -> p (t n)"), bank[2][:, :], ACT.Copy).then_inc(gm_copied.sem, 1)
                act.wait_ge(gm_tr.sem, gm_tr.at(L, 2))
                act.activation(w_tok_s[:, :], bank[3][0:NS, 0:GT * P], ACT.Copy).then_inc(gm_copied.sem, 1)
                for c in range(GT):
                    act.wait_ge(p_att.sem, p_att.at(L, c + 1))
                    act.activation(mix_hi[:, c, 0:SEQ], bank[4 + c][:, 0:SEQ], ACT.Copy).then_inc(p_att_hi.sem, 1)
                for g in range(2):
                    act.wait_ge(s_tr.sem, s_tr.at(L, g + 1))
                    act.activation(prob_st[:, g, :], bank[6 + g][:, 0:PAST], ACT.Copy).then_inc(s_copied.sem, 1)
                    act.activation(prob_nt[:, g, :], bank[6 + g][0:NS, PAST:PAST + P], ACT.Copy).then_inc(s_copied.sem, 1)
                for c in range(GT):
                    hold(act, cv_ln.sem, cv_ln.at(L, c + 2))
                    act.activation(conv_y[:, c, :], conv_y[:, c, :], ACT.Silu, scale=vec[:, bass.ds(L * NV + (V_LG + c), 1)],
                                   bias=vec[:, bass.ds(L * NV + (V_LB + c), 1)]).then_inc(cv_act.sem, 1)
                for c in range(GT):
                    act.wait_ge(gm_ok.sem, gm_ok.at(L, c + 1))
                    act.activation(mix_hi[:, 6 + c, :], gated[:, c, :], ACT.Copy).then_inc(gm_hi.sem, 1)
                for g in range(2):
                    act.wait_ge(s_out.sem, s_out.at(L, g + 1))
                    act.activation(out_s[:, g, :], bank[2 + g][:, 0:GT * P], ACT.Copy).then_inc(s_out_ok.sem, 1)
                for c in range(GT):
                    hold(act, pool_mm.sem, pool_mm.at(L, c + 1))
                    act.activation(mix_hi[:, 2 + c, :], bank[(7, 3)[c]][:, 0:TOK], ACT.Identity,
                                   scale=vec[:, bass.ds(L * NV + (V_PS + c), 1)]).then_inc(pool_hi.sem, 1)
                for c in range(GT):
                    act.wait_ge(cv_pw.sem, cv_pw.at(L, c + 1))
                    act.activation(mix_hi[:, 4 + c, :], bank[4 + c][:, 0:TOK], ACT.Copy).then_inc(cv_hi.sem, 1)
                act.wait_ge(s_att.sem, s_att.at(L, 4))
                act.activation(mix_hi[:, 0:2, SEQ:TOK], att_s[:, :, :], ACT.Copy).then_inc(s_att_hi.sem, 1)
                for i in range(IT_O):
                    for j in range(4):
                        base_next, i_next = ((BASE_O, 1), (BASE_G2, 0))[i]
                        round_slot(L, base_next, i_next, j, HALVES8)
                        norm_tile(L, T_O, 2, 4 * i + j, j % 2)
                root_of_norm(L, 2)
                act.wait_ge(states_out.sem, states_out.at(L, states_out.per))
                gate_up(L, BASE_G2, T_G2, 1)
                down(L, BASE_D2, T_D2, 3, True)

        @block.vector
        def _(dve):
            dve.sem_inc(taken.sem, 4)
            for n, (ap, value) in enumerate(((stat[:, 60:61], RMS_EPS), (stat[:, 61:62], LN_EPS), (q_pad[:, :, :, :], 0.0),
                                             (conv_in[:, :, 0:CONV_HIST], 0.0), (pool_in[:, :, 0:POOL_HIST], 0.0))):
                last = dve.memset(ap, value)
            last.then_inc(zeros_ok.sem, 1)
            dve.memset(sumsq[:, :], 0.0).then_inc(summed.sem, 1)
            dve.wait_ge(gain_in.sem, 16)
            dve.wait_ge(x_in.sem, 32)

            def norm_input(gain_col, d, e, tile_count, sum_count):
                one = x[:, bass.ds(d, 1), :].rearrange("p a t -> p (a t)")
                dve.wait_ge(xg_hi_ok.sem, tile_count + 1)
                dve.scalar_tensor_tensor(out=xg_lo[:, bass.ds(d, 1), :].rearrange("p a t -> p (a t)"), in0=one,
                                         scalar=gain[:, bass.ds(gain_col, 1)],
                                         in1=xg_hi[:, bass.ds(d, 1), :].bitcast(F32).rearrange("p a t -> p (a t)"),
                                         op0=ALU.mult, op1=ALU.subtract).then_inc(xg_lo_ok.sem, 1)
                dve.wait_ge(squared.sem, tile_count + 1)
                dve.wait_ge(summed.sem, sum_count + 1)
                dve.tensor_tensor(sumsq[:, :], sumsq[:, :], square[:, e, :], ALU.add).then_inc(summed.sem, 1)

            def invert_norm(L, n):
                dve.wait_ge(norm_root.sem, norm_root.at(L, n + 1))
                dve.reciprocal(rms[:, :], root[:, :]).then_inc(norm_ok.sem, 1)
                dve.memset(sumsq[:, :], 0.0).then_inc(summed.sem, 1)
                hold(dve, norm_ok.sem, norm_ok.at(L, n + 1))

            def gate_up(L, base, tile0, ffn):
                with dve.Fori(0, IT_G) as i:
                    for m in range(2):
                        f = L * (2 * FT) + i * 2 + (ffn * FT + m + 1)
                        tiles = L * TILES + i * 4 + (tile0 + 2 * m + taken.head)
                        done = L * slots.per + i * 4 + (4 * base + 2 * m + slots.head)
                        dve.wait_ge(slots.sem, done + 1)
                        dve.tensor_tensor(tmp[:, m, :], bank[2 * m][:, 0:TOK], rms[:, :], ALU.mult).then_inc(taken.sem, 1)
                        dve.wait_ge(slots.sem, done + 2)
                        dve.tensor_tensor(tmp[:, 4 + m, :], bank[2 * m + 1][:, 0:TOK], rms[:, :], ALU.mult).then_inc(taken.sem, 1)
                        dve.wait_ge(silu_ok.sem, f)
                        dve.wait_ge(taken.sem, tiles + 2)
                        dve.tensor_tensor(tmp[:, 6 + m, :], tmp[:, 2 + m, :], tmp[:, 4 + m, :], ALU.mult).then_inc(h_ok.sem, 1)
                        dve.wait_ge(h_hi_ok.sem, f)
                        dve.tensor_tensor(h_lo[:, bass.ds(i * 2 + m, 1), :].rearrange("p a t -> p (a t)"), tmp[:, 6 + m, :],
                                          h_hi[:, bass.ds(i * 2 + m, 1), :].bitcast(F32).rearrange("p a t -> p (a t)"),
                                          ALU.subtract).then_inc(h_lo_ok.sem, 1)

            def residual(L, base, tile0, norm, factor, tiles_an_iteration, banks):
                n_banks = len(banks)
                with dve.Fori(0, DT // n_banks) as i:
                    for e in range(n_banks):
                        d = i * n_banks + e
                        slots_a_tile = 4 // tiles_an_iteration
                        dve.wait_ge(slots.sem, L * slots.per + d * slots_a_tile + (4 * base + slots_a_tile + slots.head))
                        one = x[:, bass.ds(d, 1), :].rearrange("p a t -> p (a t)")
                        dve.scalar_tensor_tensor(out=one, in0=bank[banks[e]][:, 0:TOK], scalar=factor, in1=one,
                                                 op0=ALU.mult, op1=ALU.add).then_inc(taken.sem, 1)
                        norm_input(L * (3 * DT) + d + norm * DT, d, e % 2, L * (3 * DT) + d + norm * DT,
                                   L * summed.per + d + norm * (DT + 1))

            with dve.Fori(0, DT // 2) as i:
                for e in range(2):
                    d = i * 2 + e
                    norm_input(d, d, e, d, d)

            def take(L, t, dst, b=None):
                dve.wait_ge(slots.sem, slots.at(L, 4 * BASE_I + t + 1))
                dve.tensor_tensor(dst, bank[t % 4][:, 0:TOK], rms[:, :], ALU.mult).then_inc(taken.sem, 1)

            def history(c):
                return split_tokens(conv_in[:, c, :], CONV_HIST + DEC_T, CONV_HIST)[1]

            def prompt_taps(L, k0, k1):
                if k0 == 0:
                    for c in range(GT):
                        dve.wait_ge(glu_ok.sem, glu_ok.at(L, 2 * c + 1))
                        dve.tensor_scalar(conv_y[:, c, 0:SEQ], conv_in[:, c, 0:SEQ], vec[:, bass.ds(L * NV + (V_CW + c), 1)],
                                          vec[:, bass.ds(L * NV + (V_CB + c), 1)], ALU.mult, ALU.add).then_inc(taps.sem, 1)
                    k0 = 1
                assert (k1 - k0) % 5 == 0
                with dve.Fori(0, (k1 - k0) // 5) as i:
                    for u in range(5):
                        for c in range(GT):
                            dve.wait_ge(taps.sem, L * taps.per + i * 10 + (2 * (k0 + u) + c - 1))
                            dve.scalar_tensor_tensor(out=conv_y[:, c, 0:SEQ], in0=conv_in[:, c, bass.ds(i * 5 + (k0 + u), SEQ)],
                                                     scalar=vec[:, bass.ds(L * NV + i * (5 * GT) + (V_CW + (k0 + u) * GT + c), 1)],
                                                     in1=conv_y[:, c, 0:SEQ], op0=ALU.mult, op1=ALU.add).then_inc(taps.sem, 1)

            def history_taps(L, k0, k1):
                if k0 == 0:
                    dve.wait_ge(small_in.sem, small_in.at(L, small_in.per))
                    for c in range(GT):
                        dve.tensor_scalar(batch(conv_y[:, c, SEQ:TOK]), history(c)[:, :, 0:DEC_T], vec[:, bass.ds(L * NV + (V_CW + c), 1)],
                                          vec[:, bass.ds(L * NV + (V_CB + c), 1)], ALU.mult, ALU.add).then_inc(batch_taps.sem, 1)
                    k0 = 1
                else:
                    hold(dve, glu_ok.sem, glu_ok.at(L, 4))
                assert (k1 - k0) % 2 == 0
                with dve.Fori(0, (k1 - k0) // 2) as i:
                    for u in range(2):
                        for c in range(GT):
                            dve.wait_ge(batch_taps.sem, L * batch_taps.per + i * 4 + (2 * (k0 + u) + c - 1))
                            y = batch(conv_y[:, c, SEQ:TOK])
                            dve.scalar_tensor_tensor(out=y, in0=history(c)[:, :, bass.ds(i * 2 + (k0 + u), DEC_T)],
                                                     scalar=vec[:, bass.ds(L * NV + i * (2 * GT) + (V_CW + (k0 + u) * GT + c), 1)],
                                                     in1=y, op0=ALU.mult, op1=ALU.add).then_inc(batch_taps.sem, 1)

            with dve.Fori(0, DEPTH) as L:
                invert_norm(L, 0)
                gate_up(L, BASE_G1, T_G1, 0)
                history_taps(L, 0, CONV_HIST - DEC_T + 1)
                dve.tensor_tensor(w_sp[:, :, :], w_sp[:, :, :], views["tril"].rearrange("p (g t) -> p g t", g=1).to_broadcast([P, HEADS, P]),
                                  ALU.mult).then_inc(sp_ok.sem, 1)
                dve.tensor_copy(bias_sp[:, 0:SEQ].rearrange("p (n t) -> p n t", n=2),
                                b_sp[:, :].rearrange("p (n t) -> p n t", n=1).to_broadcast([HEADS, 2, P])).then_inc(sp_ok.sem, 1)
                dve.tensor_copy(batch(bias_sp[:, SEQ:TOK]),
                                b_sp[:, 0:DEC_T].rearrange("p (n t) -> p n t", n=1).to_broadcast([HEADS, DEC_B, DEC_T])).then_inc(sp_ok.sem, 1)
                residual(L, BASE_D1, T_D1, 1, 0.5, 1, (4, 5))
                invert_norm(L, 1)
                for c in range(GT):
                    take(L, 2 * c, z_a[:, c, :])
                    take(L, 2 * c + 1, z_g[:, c, :])
                for c in range(GT):
                    dve.wait_ge(glu_sig.sem, glu_sig.at(L, c + 1))
                    dve.tensor_tensor(conv_in[:, c, CONV_HIST:CONV_HIST + SEQ], z_a[:, c, 0:SEQ], z_g[:, c, 0:SEQ], ALU.mult).then_inc(glu_ok.sem, 1)
                    dve.tensor_tensor(history(c)[:, :, CONV_HIST:], batch(z_a[:, c, SEQ:TOK]), batch(z_g[:, c, SEQ:TOK]), ALU.mult).then_inc(glu_ok.sem, 1)

                def take_pool(c):
                    dve.wait_ge(slots.sem, slots.at(L, 4 * BASE_I + 8 + 2 * c + 1))
                    dve.tensor_tensor(pool_in[:, c, POOL_HIST:POOL_HIST + SEQ], bank[2 * c][:, 0:SEQ], rms[:, 0:SEQ], ALU.mult)
                    _, rows = split_tokens(pool_in[:, c, :], POOL_HIST + DEC_T, POOL_HIST)
                    dve.tensor_tensor(rows[:, :, POOL_HIST:], batch(bank[2 * c][:, SEQ:TOK]), batch(rms[:, SEQ:TOK]), ALU.mult).then_inc(taken.sem, 1)

                prompt_taps(L, 0, 11)
                take(L, 4, qk[:, 0, :])
                take(L, 5, qk[:, 1, :])
                take(L, 6, qk[:, 2, :])
                prompt_taps(L, 11, 16)
                take(L, 7, qk[:, 3, :])
                prompt_taps(L, 16, 21)
                take_pool(0)
                take(L, 9, z_w[:, 0, :])
                dve.wait_ge(qk_rt.sem, qk_rt.at(L, 1))
                dve.reciprocal(qk_root, qk_root).then_inc(qk_inv.sem, 1)
                take_pool(1)
                take(L, 11, z_w[:, 1, :])
                for t in range(4):
                    dve.wait_ge(qk_rep.sem, qk_rep.at(L, t + 1))
                    dve.scalar_tensor_tensor(out=qk[:, t, :], in0=qk[:, t, :], scalar=vec[:, bass.ds(L * NV + (V_QG, V_KG)[t % 2], 1)],
                                             in1=bank[4 + t][:, 0:TOK], op0=ALU.mult, op1=ALU.mult).then_inc(qk_ok.sem, 1)
                dve.wait_ge(qk_ok.sem, qk_ok.at(L, 4))
                for c in range(GT):
                    for h2 in range(2):
                        lanes, h = slice(64 * h2, 64 * h2 + 64), 2 * c + h2
                        dve.tensor_copy(q_pad[lanes, c, :, h * DEC_T:(h + 1) * DEC_T], batch(qk[lanes, 2 * c, SEQ:TOK])).then_inc(pads.sem, 1)
                    dve.tensor_copy(k_all[:, c, :, PAST:KEYS], batch(qk[:, 2 * c + 1, SEQ:TOK])).then_inc(pads.sem, 1)
                prompt_taps(L, 21, CONV_W)
                history_taps(L, CONV_HIST - DEC_T + 1, CONV_W)
                take(L, 12, z_u[:, 0, :])
                for h in range(HEADS):
                    dve.wait_ge(p_scores.sem, p_scores.at(L, h + 1))
                    dve.scalar_tensor_tensor(out=prob[:, h, :], in0=views["dist"], scalar=2.0 ** (-8.0 * (h + 1) / HEADS) / SCALE,
                                             in1=bank[4 + h][:, 0:3 * P], op0=ALU.mult, op1=ALU.add).then_inc(p_biased.sem, 1)
                dve.wait_ge(p_biased.sem, p_biased.at(L, 4))
                dve.tensor_reduce(stat[:, 0:4], prob[:, :, 0:P], AX.X, ALU.max).then_inc(p_max.sem, 1)
                dve.tensor_reduce(stat[:, 4:8], prob[:, :, P:3 * P], AX.X, ALU.max).then_inc(p_max.sem, 1)
                dve.wait_ge(p_max.sem, p_max.at(L, 2))
                dve.tensor_scalar(stat[:, 8:16], stat[:, 0:8], -SCALE, None, ALU.mult).then_inc(p_max.sem, 1)
                take(L, 13, z_v[:, 0, :])
                for g in range(2):
                    dve.wait_ge(s_scores.sem, s_scores.at(L, g + 1))
                    dve.tensor_tensor(prob_s[:, g, :], bank[4 + g][:, 0:KEYS], views["alibi"], ALU.add).then_inc(s_biased.sem, 1)
                dve.wait_ge(s_biased.sem, s_biased.at(L, 2))
                dve.tensor_reduce(stat[:, 32:34], prob_s[:, :, :], AX.X, ALU.max).then_inc(s_max.sem, 1)
                dve.wait_ge(s_max.sem, s_max.at(L, 1))
                dve.tensor_scalar(stat[:, 34:36], stat[:, 32:34], -SCALE, None, ALU.mult).then_inc(s_max.sem, 1)
                dve.wait_ge(cv_mean.sem, cv_mean.at(L, 1))
                for c in range(GT):
                    dve.scalar_tensor_tensor(out=conv_y[:, c, :], in0=bank[7][:, 0:TOK], scalar=-1.0 / (GT * P), in1=conv_y[:, c, :],
                                             op0=ALU.mult, op1=ALU.add).then_inc(cv_cent.sem, 1)
                dve.wait_ge(p_exp.sem, p_exp.at(L, 8))
                dve.reciprocal(stat[:, 24:32], stat[:, 16:24]).then_inc(p_norm.sem, 1)
                dve.wait_ge(p_norm.sem, p_norm.at(L, 1))
                for t in range(2):
                    cols, n = slice(t * P, t * P + (t + 1) * P), (t + 1) * P
                    inv = stat[:, 24 + 4 * t:28 + 4 * t].rearrange("p (h n) -> p h n", n=1).to_broadcast([P, HEADS, n])
                    dve.tensor_tensor(prob[:, :, cols], prob[:, :, cols], inv, ALU.mult).then_inc(p_norm.sem, 1)
                take(L, 14, z_u[:, 1, :])
                dve.wait_ge(gm_rt.sem, gm_rt.at(L, 1))
                dve.reciprocal(gm_root[:, :], gm_root[:, :]).then_inc(gm_v.sem, 1)
                dve.wait_ge(gm_v.sem, gm_v.at(L, 1))
                for c in range(GT):
                    dve.scalar_tensor_tensor(out=z_w[:, c, :], in0=z_w[:, c, :], scalar=vec[:, bass.ds(L * NV + (V_GG + c), 1)],
                                             in1=gm_root[:, :], op0=ALU.mult, op1=ALU.mult).then_inc(gm_v.sem, 1)
                dve.wait_ge(s_exp.sem, s_exp.at(L, 2))
                dve.reciprocal(stat[:, 38:40], stat[:, 36:38]).then_inc(s_norm.sem, 1)
                dve.wait_ge(s_norm.sem, s_norm.at(L, 1))
                dve.tensor_tensor(prob_s[:, :, :], prob_s[:, :, :],
                                  stat[:, 38:40].rearrange("p (g n) -> p g n", n=1).to_broadcast([P, 2, KEYS]), ALU.mult).then_inc(s_norm.sem, 1)
                take(L, 15, z_v[:, 1, :])
                dve.wait_ge(s_norm.sem, s_norm.at(L, 2))
                dve.tensor_tensor(prob_new[:, :, :, :],
                                  prob_s[:, :, PAST:KEYS].rearrange("p g (b t) -> p g b t", b=1).to_broadcast([P, 2, DEC_B, DEC_T]),
                                  views["newm"].rearrange("p (g b t) -> p g b t", g=2, b=DEC_B), ALU.mult).then_inc(s_norm.sem, 1)
                dve.wait_ge(cv_rt.sem, cv_rt.at(L, 1))
                dve.reciprocal(conv_root[:, :], conv_root[:, :]).then_inc(cv_ln.sem, 1)
                dve.wait_ge(cv_ln.sem, cv_ln.at(L, 1))
                for c in range(GT):
                    dve.tensor_tensor(conv_y[:, c, :], conv_y[:, c, :], conv_root[:, :], ALU.mult).then_inc(cv_ln.sem, 1)
                dve.wait_ge(sp_rep.sem, sp_rep.at(L, 1))
                dve.wait_ge(v_copied.sem, v_copied.at(L, 2))
                dve.tensor_tensor(w_sps[:, :, :, :],
                                  bank[1][0:NS, 256:288].rearrange("p (g b t) -> p g b t", g=HEADS, b=1).to_broadcast([NS, HEADS, DEC_B, DEC_T]),
                                  views["bmask"][0:NS, :].rearrange("p (g b t) -> p g b t", g=1, b=DEC_B).to_broadcast([NS, HEADS, DEC_B, DEC_T]),
                                  ALU.mult).then_inc(sp_ok.sem, 1)

                def low_part(c, out_lo, src, out_hi):
                    dve.tensor_tensor(out_lo, src, out_hi.bitcast(F32), ALU.subtract).then_inc(mix_ok.sem, 1)

                for c in range(GT):
                    dve.wait_ge(p_att_hi.sem, p_att_hi.at(L, c + 1))
                    low_part(c, mix_lo[:, c, 0:SEQ], bank[4 + c][:, 0:SEQ], mix_hi[:, c, 0:SEQ])
                for c in range(GT):
                    dve.wait_ge(gm_mm.sem, gm_mm.at(L, c + 1))
                    dve.tensor_tensor(gated[:, c, :], z_u[:, c, :], bank[c][:, 0:TOK], ALU.mult).then_inc(gm_ok.sem, 1)
                for c in range(GT):
                    dve.wait_ge(gm_hi.sem, gm_hi.at(L, c + 1))
                    low_part(c, mix_lo[:, 6 + c, :], gated[:, c, :], mix_hi[:, 6 + c, :])
                for c in range(GT):
                    dve.wait_ge(pool_hi.sem, pool_hi.at(L, c + 1))
                    dve.scalar_tensor_tensor(out=mix_lo[:, 2 + c, :], in0=bank[(7, 3)[c]][:, 0:TOK],
                                             scalar=vec[:, bass.ds(L * NV + (V_PS + c), 1)], in1=mix_hi[:, 2 + c, :].bitcast(F32),
                                             op0=ALU.mult, op1=ALU.subtract).then_inc(mix_ok.sem, 1)
                for c in range(GT):
                    dve.wait_ge(cv_hi.sem, cv_hi.at(L, c + 1))
                    low_part(c, mix_lo[:, 4 + c, :], bank[4 + c][:, 0:TOK], mix_hi[:, 4 + c, :])
                dve.wait_ge(s_out_tr.sem, s_out_tr.at(L, 1))
                for c in range(GT):
                    for h2 in range(2):
                        lanes, h = slice(64 * h2, 64 * h2 + 64), 2 * c + h2
                        src = bank[6][lanes, 2 * c * P:2 * (c + 1) * P].rearrange("p (b n) -> p b n", b=DEC_B)[:, :, h * DEC_T:(h + 1) * DEC_T]
                        dve.tensor_copy(batch(att_s[lanes, c, :]), src).then_inc(s_att.sem, 1)
                dve.wait_ge(s_att_hi.sem, s_att_hi.at(L, 1))
                low_part(0, mix_lo[:, 0:2, SEQ:TOK], att_s[:, :, :], mix_hi[:, 0:2, SEQ:TOK])
                residual(L, BASE_O, T_O, 2, 1.0, 4, (0, 1, 2, 3))
                invert_norm(L, 2)
                hold(dve, states_out.sem, states_out.at(L, states_out.per))
                gate_up(L, BASE_G2, T_G2, 1)
                residual(L, BASE_D2, T_D2, 3, 0.5, 1, (4, 5))


def _constants(np):
    BIG = -1.0e30
    c = {}
    c["ones"] = np.ones((P, P))
    heads = np.kron(np.eye(8), np.ones((1, 64))).reshape(8, 4, P)
    c["hsum"] = heads.transpose(2, 1, 0) * (np.arange(8) // 2 == np.arange(4)[:, None])
    c["hsum"] = c["hsum"].reshape(P, -1)
    c["hrep"] = np.zeros((P, 4 * P))
    c["hrep"][:8] = heads.reshape(8, -1)
    c["ident"] = np.eye(P)
    q = np.arange(P)[:, None]
    first = np.where(q >= np.arange(P), np.arange(P) - q, BIG)
    second = np.where(q + P >= np.arange(2 * P), np.arange(2 * P) - (q + P), BIG)
    c["dist"] = np.concatenate([first, second], 1)
    row = np.arange(P)
    slope = 2.0 ** (-8.0 * ((row // 8) % 4 + 1) / HEADS) / SCALE
    pos = PAST + row % 8
    key = np.arange(KEYS)
    c["alibi"] = np.where(key <= pos[:, None], slope[:, None] * (key - pos[:, None]), BIG)
    b = np.arange(NS) // 8
    c["newm"] = np.concatenate([b[None, :] == (4 * g + row // 32)[:, None] for g in range(2)], 1)
    c["bmask"] = np.zeros((P, NS))
    c["bmask"][:NS] = b[:, None] == b[None, :]
    c["e8"] = np.zeros((P, NS))
    c["e8"][:8] = np.arange(8)[:, None] == (np.arange(NS) % 8)[None, :]
    gsel = np.zeros((P, GT, P))
    for g in range(HEADS):
        gsel[g, g // 2, 64 * (g % 2):64 * (g % 2) + 64] = 1
    c["gsel"] = gsel.reshape(P, -1)
    c["tril"] = np.arange(P)[:, None] <= np.arange(P)[None, :]
    first, window = np.zeros((P, GT, POOL_HIST + 1)), np.zeros((P, GT))
    for g, w in enumerate((2, 4, 8, 16)):
        lanes = slice(64 * (g % 2), 64 * (g % 2) + 64)
        first[lanes, g // 2] = 1.0 / np.minimum(np.arange(POOL_HIST + 1) + 1, w)
        window[lanes, g // 2] = 1.0 / w
    c["first"], c["window"] = first.reshape(P, -1), window
    return np.concatenate([np.asarray(c[n], np.float32) for n, _ in CONSTS], 1)


def kernel(**inputs):
    import numpy as np
    import concourse.bacc as bacc
    from concourse.bass_utils import run_bass_kernel_spmd as run

    a = {k: np.asarray(v) for k, v in inputs.items()}
    n_pool = a["cache_k"].shape[1]

    def cols(w):
        d, r, n = w.shape
        return w.reshape(d, r // P, P, n // P, P).transpose(0, 3, 2, 1, 4)

    def halves(first, second):
        both = np.stack([first, second], 2)
        d, it, ab, half = both.shape[:4]
        return both.transpose(0, 1, 2, 4, 3, 5, 6).reshape(d, it, ab, P, -1)

    def gate_up(g, u):
        g, u = cols(g), cols(u)
        pair = lambda w: w.reshape(DEPTH, FT // 2, 2, P, DT, P)
        return halves(pair(g), pair(u))

    def down(w):
        w = cols(w)
        return np.stack([w[:, :, :, :11], w[:, :, :, 11:]], 2).reshape(DEPTH, DT, 2, P, 11 * P)

    w_in = cols(a["w_in"])
    order_a = [8, 9, 0, 1, 6, 7, 12, 13]
    order_b = [10, 11, 2, 3, 14, 15, 4, 5]
    i8 = halves(w_in[:, order_a].reshape(DEPTH, 4, 2, P, DT, P), w_in[:, order_b].reshape(DEPTH, 4, 2, P, DT, P))
    w_out = cols(a["w_out"])[:, :, :, [6, 7, 2, 3, 4, 5, 0, 1]].reshape(DEPTH, 2, 2, 2, P, DT, P)
    o8 = halves(w_out[:, :, :, 0], w_out[:, :, :, 1])
    w8 = np.concatenate([gate_up(a["ffn1_w_gate"], a["ffn1_w_up"]), i8, o8, gate_up(a["ffn2_w_gate"], a["ffn2_w_up"])], 1)
    w11 = np.concatenate([down(a["ffn1_w_down"]), down(a["ffn2_w_down"])], 1)

    gains = np.stack([a["ffn1_norm"], a["mix_norm"], a["ffn2_norm"]], 1).reshape(3 * DEPTH, DT, P)
    gains = np.concatenate([gains, gains[:1]]).transpose(2, 0, 1).reshape(P, -1)
    two = lambda v: v.reshape(DEPTH, GT, P).transpose(2, 0, 1)
    twice = lambda v: np.concatenate([v, v], 1).T[:, :, None]
    conv_w = a["conv_w"].reshape(DEPTH, CONV_W * GT, P).transpose(2, 0, 1)
    vecs = np.concatenate([twice(a["q_norm"]), twice(a["k_norm"]), two(a["pool_scale"]), two(a["conv_b"]), two(a["conv_ln_g"]),
                           two(a["conv_ln_b"]), two(a["gate_norm"]), conv_w], 2).reshape(P, -1)
    pool_w = np.zeros((DEPTH, P, GT, P), np.float32)
    for g in range(4):
        lanes = slice(64 * (g % 2), 64 * (g % 2) + 64)
        pool_w[:, lanes, g // 2, lanes] = a["pool_w"][:, g]
    tok = np.concatenate([a["x_prompt"].reshape(SEQ, D_MODEL), a["x_sample"].reshape(NS, D_MODEL)])
    arrays = {
        "xT": tok.reshape(TOK, DT, P).transpose(2, 1, 0),
        "w8": w8.reshape(DEPTH * W8_ROWS, 2, P, N8),
        "w11": w11.reshape(DEPTH * W11_ROWS, 2, P, N11),
        "gains": gains,
        "vecs": vecs,
        "consts": _constants(np),
        "pool_w": pool_w,
        "conv_pw": a["conv_pw"].reshape(DEPTH, GT, P, GT * P).transpose(0, 2, 1, 3),
        "sp_wT": a["spatial_w"].transpose(0, 3, 1, 2),
        "sp_b": a["spatial_b"],
        "cache_kT": a["cache_k"].reshape(DEPTH, n_pool, PAGE, GT, P).transpose(0, 1, 4, 3, 2),
        "cache_v": a["cache_v"].reshape(DEPTH, n_pool, PAGE, GT * P),
        "conv_hist": a["state_conv"].reshape(DEPTH, DEC_B, CONV_HIST, GT, P).transpose(0, 3, 4, 1, 2),
        "pool_hist": a["state_pool"].reshape(DEPTH, DEC_B, POOL_HIST, GT, P).transpose(0, 3, 4, 1, 2),
        "pages": a["page_table"].reshape(1, DEC_B * PAGES),
    }
    outs = {"yT": [P, DT, TOK], "kT": [DEPTH, GT, P, TOK], "vT": [DEPTH, GT, P, TOK],
            "poolT": [DEPTH, GT, P, POOL_HIST], "pool_sT": [DEPTH, GT, P, DEC_B, POOL_HIST],
            "convT": [DEPTH, GT, P, CONV_HIST], "conv_sT": [DEPTH, GT, P, DEC_B, CONV_HIST],
            "gateT": [DEPTH, GT, P, NS]}
    nc = bacc.Bacc("TRN2", target_bir_lowering=False, num_devices=1)
    args, feed = [], {}
    for name, v in arrays.items():
        v = np.ascontiguousarray(v)
        feed[f"in_{name}"] = v
        args.append(nc.dram_tensor(f"in_{name}", v.shape, mybir.dt.from_np(v.dtype), kind="ExternalInput").ap())
    for name, shape in outs.items():
        args.append(nc.dram_tensor(f"out_{name}", shape, F32, kind="ExternalOutput").ap())
    hybrid_decoder(nc, *args)
    r = run(nc, [feed], core_ids=[0]).results[0]
    o = {name: np.asarray(r[f"out_{name}"]) for name in outs}

    y = o["yT"].transpose(2, 1, 0).reshape(TOK, D_MODEL)
    width = GT * P

    def rows(t):
        return np.ascontiguousarray(t.transpose(0, 3, 1, 2)).reshape(DEPTH, -1, width)

    def state(t):
        return np.ascontiguousarray(t.transpose(0, 3, 4, 1, 2)).reshape(DEPTH, DEC_B, -1, width)

    k, v = rows(o["kT"]), rows(o["vT"])
    prompt = lambda t: t[:, :SEQ].reshape(DEPTH, 1, SEQ, HEADS, HEAD)
    sample = lambda t: t[:, SEQ:].reshape(DEPTH, DEC_B, DEC_T, HEADS, HEAD)
    return (y[:SEQ].reshape(1, SEQ, D_MODEL), y[SEQ:].reshape(DEC_B, DEC_T, D_MODEL),
            prompt(k), prompt(v), sample(k), sample(v),
            rows(o["poolT"]).reshape(DEPTH, 1, POOL_HIST, width), state(o["pool_sT"]),
            rows(o["convT"]).reshape(DEPTH, 1, CONV_HIST, width), state(o["conv_sT"]),
            rows(o["gateT"]).reshape(DEPTH, DEC_B, DEC_T, width))
```

```python
from contextlib import ExitStack

import concourse.bass as bass
from concourse import mybir

F32 = mybir.dt.float32
F32R = mybir.dt.float32r
I32 = mybir.dt.int32
ALU = mybir.AluOpType
ACT = mybir.ActivationFunctionType
AX = mybir.AxisListType

P = 128
DEPTH, D_MODEL, FFN = 2, 1024, 2816
SEQ, DEC_B, DEC_T = 256, 8, 8
NS = DEC_B * DEC_T
TOK = SEQ + NS
PAST, PAGE = 256, 128
PAGES = PAST // PAGE
HEADS, HEAD = 4, 64
KEYS = PAST + DEC_T
POOL_HIST, CONV_W, CONV_HIST = 15, 31, 30
RMS_EPS, LN_EPS = 1e-6, 1e-5
SCALE = HEAD ** -0.5
DT = D_MODEL // P
FT = FFN // P
GT = 2

IT_G, IT_D, IT_I, IT_O = FT // 2, DT, 4, 2
BASE_G1 = 0
BASE_D1 = BASE_G1 + IT_G
BASE_I = BASE_D1 + IT_D
BASE_O = BASE_I + IT_I
BASE_G2 = BASE_O + IT_O
BASE_D2 = BASE_G2 + IT_G
ITS = BASE_D2 + IT_D
W8_G1, W8_I, W8_O, W8_G2, W8_ROWS = 0, IT_G, IT_G + IT_I, IT_G + IT_I + IT_O, 2 * IT_G + IT_I + IT_O
W11_ROWS = 2 * IT_D
N8, N11 = 16 * P, 11 * P
HALVES8 = ((0, 8), (0, 8), (8, 8), (8, 8))
HALVES11 = ((0, 6), (0, 6), (6, 5), (6, 5))
T_G1 = 0
T_D1 = T_G1 + 4 * IT_G
T_I = T_D1 + DT
T_O = T_I + 16
T_G2 = T_O + DT
T_D2 = T_G2 + 4 * IT_G
TILES = T_D2 + DT

V_QG, V_KG, V_PS, V_CB, V_LG, V_LB, V_GG, V_CW = 0, 1, 2, 4, 6, 8, 10, 12
NV = V_CW + CONV_W * GT
CONSTS = (("ident", P), ("dist", 3 * P), ("alibi", KEYS), ("newm", 2 * NS), ("bmask", NS),
          ("e8", NS), ("gsel", GT * P), ("tril", P), ("hsum", 4 * 8), ("hrep", 4 * P),
          ("first", GT * (POOL_HIST + 1)), ("window", GT))
NC_ = sum(n for _, n in CONSTS)
SMALLS = 8
STATES = 11


class Signal:

    def __init__(self, sem, per_layer, head=0):
        self.sem, self.per, self.head = sem, per_layer, head

    def at(self, layer, k):
        return layer * self.per + (k + self.head)


def hybrid_decoder(nc, xT, w8, w11, gains, vecs, consts, pool_w, conv_pw, sp_wT, sp_b,
                   cache_kT, cache_v, conv_hist, pool_hist, pages,
                   yT, kT, vT, poolT, pool_sT, convT, conv_sT, gateT):
    ctx = ExitStack()
    with ctx:
        place = [16512]

        def sb(name, shape, dt=F32, at=None):
            n = 4
            for s in shape[1:]:
                n *= s
            offset = place[0] if at is None else at[0]
            t = nc.alloc_sbuf_tensor_at(name, shape, dt, offset=offset)
            end = offset + (n + 31) // 32 * 32
            if at is None:
                place[0] = end
                assert end <= 229344, (name, end)
            else:
                at[0] = end
                assert end <= at[1], (name, end, at[1])
            return t

        raw = sb("raw", [P, 4, 8 * P])
        w_hi = sb("w_hi", [P, 4, 8 * P], F32R)
        w_lo = sb("w_lo", [P, 4, 8 * P], F32R)
        x = sb("x", [P, DT, TOK])
        mix_place = place[0]
        mix_hi = sb("mix_hi", [P, DT, TOK], F32R)
        mix_lo = sb("mix_lo", [P, DT, TOK], F32R)
        norm_region = [place[0], None]
        xg_hi = sb("xg_hi", [P, DT, TOK], F32R)
        xg_lo = sb("xg_lo", [P, DT, TOK], F32R)
        norm_region[1] = place[0]
        ffn_region = [place[0], None]
        h_hi = sb("h_hi", [P, FT, TOK], F32R)
        h_lo = sb("h_lo", [P, FT, TOK], F32R)
        ffn_region[1] = place[0]
        cst = sb("cst", [P, NC_])
        ones = sb("ones", [P, P])
        gain = sb("gain", [P, (3 * DEPTH + 1) * DT])
        vec = sb("vec", [P, DEPTH * NV])
        page_row = sb("page_row", [1, DEC_B * PAGES], I32)
        w_pool = sb("w_pool", [P, GT, P])
        w_pw = sb("w_pw", [P, GT, GT * P])
        w_sp = sb("w_sp", [P, HEADS, P])
        b_sp = sb("b_sp", [HEADS, P])
        bias_sp = sb("bias_sp", [HEADS, TOK])
        w_sps = sb("w_sps", [NS, HEADS, DEC_B, DEC_T])
        conv_in = sb("conv_in", [P, GT, CONV_HIST + SEQ + DEC_B * (CONV_HIST + DEC_T)])
        pool_in = sb("pool_in", [P, GT, POOL_HIST + SEQ + DEC_B * (POOL_HIST + DEC_T)])
        conv_y = sb("conv_y", [P, GT, TOK])
        rms = sb("rms", [P, TOK])
        root = sb("root", [P, TOK])
        sumsq = sb("sumsq", [P, TOK])
        square = sb("square", [P, 2, TOK])
        tmp = sb("tmp", [P, 8, TOK])
        q_pad = sb("q_pad", [P, GT, DEC_B, 32])
        stat = sb("stat", [P, 64])
        prob = sb("prob", [P, HEADS, 3 * P])
        prob_s = sb("prob_s", [P, 2, KEYS])

        k_all = sb("k_all", [P, GT, DEC_B, KEYS], at=ffn_region)
        v_past = sb("v_past", [P, DEC_B * PAGES, GT * P], at=ffn_region)
        qk = sb("qk", [P, 4, TOK], at=ffn_region)
        z_v = sb("z_v", [P, GT, TOK], at=ffn_region)
        z_u = sb("z_u", [P, GT, TOK], at=ffn_region)
        z_w = sb("z_w", [P, GT, TOK], at=ffn_region)
        v_tok = sb("v_tok", [P, 2, GT * P], at=ffn_region)
        v_tok_s = sb("v_tok_s", [NS, GT * P], at=ffn_region)
        w_tok = sb("w_tok", [P, 2, GT * P], at=ffn_region)
        w_tok_s = sb("w_tok_s", [NS, GT * P], at=ffn_region)
        prob_t = sb("prob_t", [P, HEADS, 3 * P], at=norm_region)
        prob_st = sb("prob_st", [P, 2, PAST], at=norm_region)
        prob_new = sb("prob_new", [P, 2, DEC_B, DEC_T], at=norm_region)
        prob_nt = sb("prob_nt", [NS, 2, P], at=norm_region)
        out_s = sb("out_s", [P, 2, GT * P], at=norm_region)
        att_s = sb("att_s", [P, GT, NS], at=norm_region)
        win1 = sb("win1", [P, GT, POOL_HIST + SEQ + DEC_B * (POOL_HIST + DEC_T)],
                  at=[mix_place + 2 * TOK * 4, mix_place + 5 * TOK * 4])
        win2 = sb("win2", [P, GT, POOL_HIST + SEQ + DEC_B * (POOL_HIST + DEC_T)],
                  at=[mix_place + (DT + 2) * TOK * 4, mix_place + (DT + 5) * TOK * 4])
        pool_m = tmp[:, 6:8, :]
        z_a = tmp[:, 0:2, :]
        z_g = tmp[:, 2:4, :]
        qk_square = tmp[:, 4:8, :]
        qk_root = tmp[0:8, 2, :]
        gm_sq = tmp[:, 0:2, :]
        gm_root = tmp[:, 2, :]
        gated = tmp[:, 4:6, :]
        conv_sq = tmp[:, 0:2, :]
        conv_root = tmp[:, 3, :]

        at, views = 0, {}
        for name, n in CONSTS:
            views[name] = cst[:, at:at + n]
            at += n
        ident = views["ident"]

        bank = [ctx.enter_context(nc.psum_tensor(f"bank{i}", [P, 512], F32)) for i in range(8)]

        def sig(name, per_layer, head=0):
            return Signal(ctx.enter_context(nc.semaphore(name)), per_layer, head)

        gain_in = sig("gain_in", 0)
        consts_in = sig("consts_in", 0)
        x_in = [sig(f"x{n}_in", 0) for n in range(2)]
        raw_in = [sig(f"raw{j}_in", 16 * ITS) for j in range(4)]
        small_in = sig("small_in", 16 * SMALLS)
        kv_in = sig("kv_in", 16 * 2 * DEC_B * PAGES)
        states_out = sig("states_out", 16 * STATES, 16)
        y_out = sig("y_out", 0)
        passed = sig("passed", 0)
        split_hi = sig("split_hi", 4 * ITS)
        split = sig("split", 4 * ITS, 4)
        slots = sig("slots", 4 * ITS, 4)
        taken = sig("taken", TILES, 4)
        xg_hi_ok = sig("xg_hi_ok", 3 * DT, DT)
        xg_lo_ok = sig("xg_lo_ok", 3 * DT, DT)
        squared = sig("squared", 3 * DT)
        squared_first = sig("squared_first", 0)
        squared_too = sig("squared_too", 0)
        summed = sig("summed", 3 * (DT + 1), DT + 1)
        norm_sum = sig("norm_sum", 3)
        norm_root = sig("norm_root", 3)
        norm_ok = sig("norm_ok", 3)
        silu_ok = sig("silu_ok", 2 * FT)
        h_ok = sig("h_ok", 2 * FT)
        h_hi_ok = sig("h_hi_ok", 2 * FT)
        h_lo_ok = sig("h_lo_ok", 2 * FT)
        filled = sig("filled", 0)
        glu_sig = sig("glu_sig", 2)
        glu_ok = sig("glu_ok", 4)
        taps = sig("taps", 2 * CONV_W)
        batch_taps = sig("batch_taps", 2 * (CONV_HIST - DEC_T + 1))
        late_taps = sig("late_taps", 2 * DEC_T)
        qk_sq = sig("qk_sq", 4)
        qk_sum = sig("qk_sum", 1)
        qk_rt = sig("qk_rt", 1)
        qk_inv = sig("qk_inv", 1)
        qk_rep = sig("qk_rep", 4)
        qk_ok = sig("qk_ok", 4)
        pads = sig("pads", 6)
        sp_ok = sig("sp_ok", 4)
        sp_rep = sig("sp_rep", 1)
        v_tr = sig("v_tr", 2)
        v_copied = sig("v_copied", 2)
        p_scores = sig("p_scores", 2 * HEADS)
        p_biased = sig("p_biased", 2 * HEADS)
        p_max = sig("p_max", 3)
        p_exp = sig("p_exp", 8)
        p_norm = sig("p_norm", 3)
        p_tr = sig("p_tr", 4)
        p_copied = sig("p_copied", 4)
        p_att = sig("p_att", 2)
        p_att_hi = sig("p_att_hi", 2)
        s_scores = sig("s_scores", 2)
        s_biased = sig("s_biased", 2)
        s_max = sig("s_max", 2)
        s_exp = sig("s_exp", 2)
        s_norm = sig("s_norm", 3)
        s_tr = sig("s_tr", 2)
        s_copied = sig("s_copied", 4)
        s_out = sig("s_out", 2)
        s_out_ok = sig("s_out_ok", 2)
        s_out_tr = sig("s_out_tr", 1)
        s_att = sig("s_att", 4)
        s_att_hi = sig("s_att_hi", 1)
        gelu_ok = sig("gelu_ok", 4)
        gm_sq_ok = sig("gm_sq_ok", 2)
        gm_sum = sig("gm_sum", 1)
        gm_rt = sig("gm_rt", 1)
        gm_v = sig("gm_v", 3)
        gm_tr = sig("gm_tr", 2)
        gm_copied = sig("gm_copied", 2)
        gm_mm = sig("gm_mm", 2)
        gm_ok = sig("gm_ok", 2)
        gm_hi = sig("gm_hi", 2)
        pool_step = sig("pool_step", 12)
        pool_mm = sig("pool_mm", 2)
        pool_hi = sig("pool_hi", 2)
        cv_mean = sig("cv_mean", 1)
        cv_cent = sig("cv_cent", 2)
        cv_sq = sig("cv_sq", 2)
        cv_var = sig("cv_var", 1)
        cv_rt = sig("cv_rt", 1)
        cv_ln = sig("cv_ln", 3)
        cv_act = sig("cv_act", 2)
        cv_pw = sig("cv_pw", 2)
        cv_hi = sig("cv_hi", 2)
        mix_ok = sig("mix_ok", 9)
        conv_sum = bank[7][:, :].rearrange("p (c t) -> p c t", c=GT)
        score = lambda t, h: bank[4][:, h * P:(h + 1) * P] if t == 0 else bank[5 + h % 2][:, h // 2 * 2 * P:(h // 2 + 1) * 2 * P]
        SCORE_ORDER = ((0, 0), (0, 2), (1, 1), (1, 3), (0, 1), (0, 3), (1, 0), (1, 2))
        QK_BANK = (4, 5, 6, 4)
        P_TR_BANK = (4, 5, 6, 0)
        MIX_ORDER = ((6, 3), (7, 4), (2, 5), (3, 6), (4, 7), (5, 8), (0, 9), (1, 9))

        def split_tokens(ap2d, width, hist):
            prompt = ap2d[:, 0:hist + SEQ]
            rows = ap2d[:, hist + SEQ:hist + SEQ + DEC_B * width].rearrange("p (b t) -> p b t", b=DEC_B)
            return prompt, rows

        def batch(ap2d):
            return ap2d.rearrange("p (b t) -> p b t", b=DEC_B)

        def hold(engine, sem, value):
            engine.wait_ge(sem, value)
            engine.sem_inc(passed.sem, 1)

        block = ctx.enter_context(nc.Block())

        @block.sync
        def _(sp):
            def load_slot(L, base, i, j, weights, row, halves):
                sp.wait_ge(split.sem, L * split.per + (base + i) * 4 + j + 1)
                first, count = halves[j]
                src = weights[bass.ds(row, 1), j % 2, :, first * P:(first + count) * P].rearrange("a p n -> (a p) n")
                sp.dma_start(raw[:, j, 0:count * P], src).then_inc(raw_in[j].sem, 16)

            def load(L, base, i, weights, row, halves):
                for j in range(4):
                    load_slot(L, base, i, j, weights, row, halves)

            def load_small(L):
                hold(sp, states_out.sem, states_out.at(L, 0))
                one = bass.ds(L, 1)
                for c in range(GT):
                    _, conv_rows = split_tokens(conv_in[:, c, :], CONV_HIST + DEC_T, CONV_HIST)
                    sp.dma_start(conv_rows[:, :, 0:CONV_HIST],
                                 conv_hist[one, c, :, :, :].rearrange("a p b t -> (a p) b t")).then_inc(small_in.sem, 16)
                    _, pool_rows = split_tokens(pool_in[:, c, :], POOL_HIST + DEC_T, POOL_HIST)
                    sp.dma_start(pool_rows[:, :, 0:POOL_HIST],
                                 pool_hist[one, c, :, :, :].rearrange("a p b t -> (a p) b t")).then_inc(small_in.sem, 16)
                for dst, src in ((w_pool, pool_w), (w_pw, conv_pw), (w_sp, sp_wT)):
                    sp.dma_start(dst[:, :, :], src[one, :, :, :].rearrange("a p c n -> (a p) c n")).then_inc(small_in.sem, 16)
                sp.dma_start(b_sp[:, :], sp_b[one, :, :].rearrange("a g t -> (a g) t")).then_inc(small_in.sem, 16)

            def load_past(L, b):
                one = bass.ds(L, 1)
                for n in range(PAGES):
                    page = sp.value_load(page_row[0:1, bass.ds(b * PAGES + n, 1)],
                                         min_val=0, max_val=cache_v.shape[1] - 1)
                    at_page = bass.ds(page, 1)
                    sp.dma_start(k_all[:, :, bass.ds(b, 1), n * PAGE:(n + 1) * PAGE].rearrange("p c b t -> p c (b t)"),
                                 cache_kT[one, at_page, :, :, :].rearrange("l a p c t -> (l a p) c t")).then_inc(kv_in.sem, 16)
                    sp.dma_start(v_past[:, bass.ds(b * PAGES + n, 1), :].rearrange("p b t -> p (b t)"),
                                 cache_v[one, at_page, :, :].rearrange("l a p n -> (l a p) n")).then_inc(kv_in.sem, 16)

            def store_states(L):
                layer = bass.ds(L, 1)
                sp.wait_ge(mix_ok.sem, mix_ok.at(L, mix_ok.per))
                sp.dma_start(kT[layer, :, :, :].rearrange("l c p t -> p (l c) t"), qk[:, 1:4:2, :]).then_inc(states_out.sem, 16)
                sp.dma_start(vT[layer, :, :, :].rearrange("l c p t -> p (l c) t"), z_v[:, :, :]).then_inc(states_out.sem, 16)
                sp.dma_start(poolT[layer, :, :, :].rearrange("l c p t -> p (l c) t"), pool_in[:, :, SEQ:SEQ + POOL_HIST]).then_inc(states_out.sem, 16)
                sp.dma_start(convT[layer, :, :, :].rearrange("l c p t -> p (l c) t"), conv_in[:, :, SEQ:SEQ + CONV_HIST]).then_inc(states_out.sem, 16)
                sp.dma_start(gateT[layer, :, :, :].rearrange("l c p t -> p (l c) t"), z_w[:, :, SEQ:TOK]).then_inc(states_out.sem, 16)
                for c in range(GT):
                    _, rows = split_tokens(pool_in[:, c, :], POOL_HIST + DEC_T, POOL_HIST)
                    sp.dma_start(pool_sT[layer, c, :, :, :].rearrange("l p b t -> (l p) b t"), rows[:, :, DEC_T:]).then_inc(states_out.sem, 16)
                    _, rows = split_tokens(conv_in[:, c, :], CONV_HIST + DEC_T, CONV_HIST)
                    for half in range(2):
                        sp.dma_start(conv_sT[layer, c, :, 4 * half:4 * half + 4, :].rearrange("l p b t -> (l p) b t"),
                                     rows[:, 4 * half:4 * half + 4, DEC_T:]).then_inc(states_out.sem, 16)

            sp.dma_start(gain[:, :], gains).then_inc(gain_in.sem, 16)
            load_slot(0, BASE_G1, 0, 0, w8, W8_G1, HALVES8)
            for n in range(2):
                half = slice(n * DT // 2, (n + 1) * DT // 2)
                sp.dma_start(x[:, half, :], xT[:, half, :]).then_inc(x_in[n].sem, 16)
            for j in range(1, 4):
                load_slot(0, BASE_G1, 0, j, w8, W8_G1, HALVES8)
            with sp.Fori(0, DEPTH) as L:
                load_small(L)
                with sp.Fori(1, IT_G) as i:
                    load(L, BASE_G1, i, w8, L * W8_ROWS + W8_G1 + i, HALVES8)
                with sp.Fori(0, IT_D) as i:
                    load(L, BASE_D1, i, w11, L * W11_ROWS + i, HALVES11)
                with sp.Fori(0, 2) as i:
                    load(L, BASE_I, i, w8, L * W8_ROWS + W8_I + i, HALVES8)
                hold(sp, slots.sem, slots.at(L, 4 * BASE_I))
                sp.wait_ge(consts_in.sem, 48)
                with sp.Fori(0, DEC_B // 4) as n:
                    for j in range(4):
                        load_slot(L, BASE_I, 2 + n, j, w8, L * W8_ROWS + (W8_I + 2) + n, HALVES8)
                        load_past(L, n * 4 + j)
                with sp.Fori(0, IT_O) as i:
                    load(L, BASE_O, i, w8, L * W8_ROWS + W8_O + i, HALVES8)
                store_states(L)
                with sp.Fori(0, IT_G) as i:
                    load(L, BASE_G2, i, w8, L * W8_ROWS + W8_G2 + i, HALVES8)
                with sp.Fori(0, IT_D) as i:
                    load(L, BASE_D2, i, w11, L * W11_ROWS + IT_D + i, HALVES11)
                load(L + 1, BASE_G1, 0, w8, L * W8_ROWS + (W8_ROWS + W8_G1), HALVES8)
            sp.wait_ge(taken.sem, taken.at(DEPTH - 1, T_D2 + DT - 2))
            sp.dma_start(yT[:, 0:DT - 2, :], x[:, 0:DT - 2, :]).then_inc(y_out.sem, 16)
            sp.wait_ge(taken.sem, taken.at(DEPTH, 0))
            sp.dma_start(yT[:, DT - 2:DT, :], x[:, DT - 2:DT, :]).then_inc(y_out.sem, 16)
            sp.wait_ge(y_out.sem, 32)
            sp.wait_ge(states_out.sem, states_out.at(DEPTH, 0))

        @block.gpsimd
        def _(pool):
            pool.sem_inc(split.sem, 4)

            def split_iteration(L, base, i, halves, which=range(4)):
                for j in which:
                    count = halves[j][1]
                    pool.wait_ge(split_hi.sem, L * split_hi.per + (base + i) * 4 + j + 1)
                    pool.tensor_tensor(w_lo[:, j, 0:count * P], raw[:, j, 0:count * P],
                                       w_hi[:, j, 0:count * P].bitcast(F32), ALU.subtract).then_inc(split.sem, 1)

            def late_history_taps(L):
                pool.wait_ge(qk_ok.sem, qk_ok.at(L, 4))
                pool.wait_ge(glu_ok.sem, glu_ok.at(L, 4))
                hold(pool, batch_taps.sem, batch_taps.at(L, batch_taps.per))
                rows = conv_in[:, :, CONV_HIST + SEQ:].rearrange("p c (b t) -> p c b t", b=DEC_B)
                sums = conv_y[:, :, SEQ:TOK].rearrange("p c (b t) -> p c b t", b=DEC_B)
                products = pool_m[:, :, SEQ:TOK].rearrange("p c (b t) -> p c b t", b=DEC_B)
                for n in range(DEC_T):
                    k = CONV_HIST - DEC_T + 1 + n
                    weights = vec[:, bass.ds(L * NV + (V_CW + k * GT), GT)].rearrange("p (c b t) -> p c b t", b=1, t=1)
                    if n:
                        hold(pool, late_taps.sem, late_taps.at(L, 2 * n))
                    pool.tensor_tensor(products, rows[:, :, :, k:k + DEC_T], weights.to_broadcast([P, GT, DEC_B, DEC_T]),
                                       ALU.mult).then_inc(late_taps.sem, 1)
                    pool.wait_ge(late_taps.sem, late_taps.at(L, 2 * n + 1))
                    pool.tensor_tensor(sums, sums, products, ALU.add).then_inc(late_taps.sem, 1)

            def window_sums(L):
                width = POOL_HIST + SEQ + DEC_B * (POOL_HIST + DEC_T)
                pool.wait_ge(taken.sem, taken.at(L, T_I + 11))
                pool.wait_ge(small_in.sem, small_in.at(L, 16 * SMALLS))
                steps = [0]

                def done(ins):
                    ins.then_inc(pool_step.sem, 1)
                    steps[0] += 1
                    hold(pool, pool_step.sem, pool_step.at(L, steps[0]))

                def add(dst, src, lanes, c, shift, lead):
                    done(pool.tensor_tensor(dst[lanes, c, lead:width], src[lanes, c, lead:width],
                                            src[lanes, c, lead - shift:width - shift], ALU.add))

                low, high, every = slice(0, 64), slice(64, P), slice(0, P)
                add(win1, pool_in, every, 0, 1, 1)
                add(win1, pool_in, every, 1, 1, 1)
                add(win2, pool_in, low, 0, 1, 1)
                add(win2, win1, high, 0, 2, 3)
                add(win2, win1, every, 1, 2, 3)
                add(win1, win2, every, 1, 4, 7)
                add(win2, win1, high, 1, 8, 15)
                done(pool.tensor_copy(win2[low, 1, 15:width], win1[low, 1, 15:width]))
                hold(pool, qk_ok.sem, qk_ok.at(L, 4))
                first = views["first"].rearrange("p (c t) -> p c t", c=GT)
                for c in range(GT):
                    _, mean_rows = split_tokens(win2[:, c, :], POOL_HIST + DEC_T, POOL_HIST)
                    scale = views["window"][:, c:c + 1]
                    pool.tensor_scalar(pool_m[:, c, 0:SEQ], win2[:, c, POOL_HIST:POOL_HIST + SEQ], scale, 1.0, ALU.mult, ALU.mult)
                    last = pool.tensor_scalar(batch(pool_m[:, c, SEQ:TOK]), mean_rows[:, :, POOL_HIST:], scale, 1.0, ALU.mult, ALU.mult)
                done(last)
                done(pool.tensor_tensor(pool_m[:, :, 0:POOL_HIST + 1], win2[:, :, POOL_HIST:2 * POOL_HIST + 1], first, ALU.mult))
                done(pool.tensor_tensor(pool_m[:, :, 0:SEQ], pool_m[:, :, 0:SEQ],
                                        pool_in[:, :, POOL_HIST:POOL_HIST + SEQ], ALU.subtract))
                for c in range(GT):
                    _, rows = split_tokens(pool_in[:, c, :], POOL_HIST + DEC_T, POOL_HIST)
                    last = pool.tensor_tensor(batch(pool_m[:, c, SEQ:TOK]), batch(pool_m[:, c, SEQ:TOK]),
                                              rows[:, :, POOL_HIST:], ALU.subtract)
                last.then_inc(pool_step.sem, 1)
                assert steps[0] + 1 == pool_step.per

            split_iteration(0, BASE_G1, 0, HALVES8, range(1))
            pool.wait_ge(x_in[1].sem, 16)
            for d in range(DT // 2, DT):
                pool.tensor_tensor(tmp[:, d, :], x[:, d, :], x[:, d, :], ALU.mult).then_inc(squared_too.sem, 1)
            split_iteration(0, BASE_G1, 0, HALVES8, range(1, 4))
            with pool.Fori(0, DEPTH) as L:
                with pool.Fori(1, IT_G) as i:
                    split_iteration(L, BASE_G1, i, HALVES8)
                with pool.Fori(0, IT_D) as i:
                    split_iteration(L, BASE_D1, i, HALVES11)
                with pool.Fori(0, IT_I) as i:
                    split_iteration(L, BASE_I, i, HALVES8)
                late_history_taps(L)
                window_sums(L)
                with pool.Fori(0, IT_O) as i:
                    split_iteration(L, BASE_O, i, HALVES8)
                with pool.Fori(0, IT_G) as i:
                    split_iteration(L, BASE_G2, i, HALVES8)
                with pool.Fori(0, IT_D) as i:
                    split_iteration(L, BASE_D2, i, HALVES11)
                split_iteration(L + 1, BASE_G1, 0, HALVES8)

        @block.tensor
        def _(pe):
            pe.sem_inc(slots.sem, 4)

            def use_slot(L, base, i, j, out, k_tiles, in_hi, in_lo, first, last, before_k=None):
                pe.wait_ge(split.sem, L * split.per + (base + i) * 4 + (j + 1 + split.head))
                for n, k in enumerate(k_tiles):
                    if before_k:
                        before_k(n, k)
                    hi, lo = w_hi[:, j, n * P:(n + 1) * P], w_lo[:, j, n * P:(n + 1) * P]
                    pe.matmul(out, hi, in_hi[:, k, :], start=first and n == 0, stop=False)
                    pe.matmul(out, hi, in_lo[:, k, :], start=False, stop=False)
                    end = n == len(k_tiles) - 1
                    mm = pe.matmul(out, lo, in_hi[:, k, :], start=False, stop=last and end)
                mm.then_inc(slots.sem, 1)

            def bank_free(L, tile):
                pe.wait_ge(taken.sem, L * taken.per + tile + 1)

            def sum_squares(L, n):
                pe.wait_ge(summed.sem, L * summed.per + (n + 1) * (DT + 1))
                pe.matmul(bank[6][:, 0:TOK], ones[:, :], sumsq[:, :], start=True, stop=True).then_inc(norm_sum.sem, 1)

            def column(L, base, tile0, norm, i, j, first=False):
                bank_free(L, i * 4 + (tile0 + j))
                ready = (lambda n, k: pe.wait_ge(xg_lo_ok.sem, L * xg_lo_ok.per + norm * DT + k + 1)) if first and j == 0 else None
                use_slot(L, base, i, j, bank[j][:, 0:TOK], range(8), xg_hi, xg_lo, True, True, ready)
                if first and j == (1 if norm == 0 else 0):
                    sum_squares(L, norm)

            def columns(L, base, tile0, norm, i, first=False):
                for j in range(4):
                    column(L, base, tile0, norm, i, j, first)

            def down(L, base, tile0, ffn):
                with pe.Fori(0, IT_D // 2) as i2:
                    for e in range(2):
                        i = i2 * 2 + e
                        pe.wait_ge(taken.sem, L * taken.per + i + (tile0 - 2 + 1 + 4))
                        for j, ks in enumerate((range(0, 6), range(11, 17), range(6, 11), range(17, 22))):
                            pe.wait_ge(h_lo_ok.sem, h_lo_ok.at(L, ffn * FT + ks[-1] + 1))
                            use_slot(L, base, i, j, bank[4 + e][:, 0:TOK], ks, h_hi, h_lo, j == 0, j == 3)

            def gate_up(L, base, tile0, norm):
                columns(L, base, tile0, norm, 0, first=True)
                with pe.Fori(1, IT_G) as i:
                    columns(L, base, tile0, norm, i)

            def qk_sums(L):
                pe.wait_ge(consts_in.sem, 48)
                pe.wait_ge(qk_sq.sem, qk_sq.at(L, 4))
                hsum = views["hsum"].rearrange("p (t n) -> p t n", t=4)
                for t in range(4):
                    mm = pe.matmul(bank[4][0:8, 0:TOK], hsum[:, t, :], qk_square[:, t, :], start=t == 0, stop=t == 3)
                mm.then_inc(qk_sum.sem, 1)

            def qk_spread(L):
                pe.wait_ge(qk_inv.sem, qk_inv.at(L, 1))
                hrep = views["hrep"].rearrange("p (t n) -> p t n", t=4)
                for t in range(4):
                    if t == 3:
                        pe.wait_ge(qk_ok.sem, qk_ok.at(L, 1))
                    pe.matmul(bank[QK_BANK[t]][:, 0:TOK], hrep[0:8, t, :], qk_root, start=True, stop=True).then_inc(qk_rep.sem, 1)

            def prompt_scores(L):
                pe.wait_ge(qk_ok.sem, qk_ok.at(L, 4))
                for n, (t, h) in enumerate(SCORE_ORDER):
                    c, lanes = h // 2, slice(64 * (h % 2), 64 * (h % 2) + 64)
                    if n == 4:
                        pe.wait_ge(p_scores.sem, p_scores.at(L, 2))
                    pe.matmul(score(t, h), qk[lanes, 2 * c, t * P:(t + 1) * P], qk[lanes, 2 * c + 1, 0:(t + 1) * P],
                              start=True, stop=True).then_inc(p_scores.sem, 1)

            def value_rows(L):
                pe.wait_ge(taken.sem, taken.at(L, T_O))
                for c in range(GT):
                    for t in range(2):
                        mm = pe.transpose(bank[3][:, t * 2 * P + c * P:t * 2 * P + (c + 1) * P], z_v[:, c, t * P:(t + 1) * P], ident)
                mm.then_inc(v_tr.sem, 1)
                pe.wait_ge(sp_ok.sem, sp_ok.at(L, 3))
                pe.matmul(bank[1][0:NS, 256:288].rearrange("p (g t) -> p g t", g=HEADS), views["e8"][0:8, :],
                          w_sp[0:8, :, 0:DEC_T], start=True, stop=True).then_inc(sp_rep.sem, 1)
                for c in range(GT):
                    mm = pe.transpose(bank[1][0:NS, c * P:(c + 1) * P], z_v[:, c, SEQ:TOK], ident)
                mm.then_inc(v_tr.sem, 1)

            def batch_scores(L):
                pe.wait_ge(pads.sem, pads.at(L, 6))
                pe.wait_ge(kv_in.sem, kv_in.at(L, kv_in.per))
                for g in range(2):
                    pe.wait_ge(p_biased.sem, p_biased.at(L, 6 + 2 * g))
                    for b4 in range(4):
                        b = 4 * g + b4
                        for c in range(GT):
                            mm = pe.matmul(bank[4 + g][32 * b4:32 * b4 + 32, 0:KEYS], q_pad[:, c, b, :], k_all[:, c, b, :],
                                           start=c == 0, stop=c == 1)
                    mm.then_inc(s_scores.sem, 1)

            def gate_square_sum(L):
                pe.wait_ge(gm_sq_ok.sem, gm_sq_ok.at(L, 2))
                pe.wait_ge(p_biased.sem, p_biased.at(L, 8))
                for c in range(GT):
                    mm = pe.matmul(bank[6][:, 0:TOK], ones[:, :], gm_sq[:, c, :], start=c == 0, stop=c == 1)
                mm.then_inc(gm_sum.sem, 1)

            def conv_mean(L):
                pe.wait_ge(taps.sem, taps.at(L, taps.per))
                pe.wait_ge(late_taps.sem, late_taps.at(L, late_taps.per))
                for c in range(GT):
                    mm = pe.matmul(bank[7][:, 0:TOK], ones[:, :], conv_y[:, c, :], start=c == 0, stop=c == 1)
                mm.then_inc(cv_mean.sem, 1)

            def conv_variance(L):
                pe.wait_ge(cv_sq.sem, cv_sq.at(L, 2))
                for c in range(GT):
                    mm = pe.matmul(bank[7][:, 0:TOK], ones[:, :], conv_sq[:, c, :], start=c == 0, stop=c == 1)
                mm.then_inc(cv_var.sem, 1)

            def prompt_attention_transposes(L):
                pe.wait_ge(p_norm.sem, p_norm.at(L, 3))
                pe.wait_ge(s_biased.sem, s_biased.at(L, 2))
                pe.wait_ge(gm_rt.sem, gm_rt.at(L, 1))
                for h in range(HEADS):
                    for n in range(3):
                        mm = pe.transpose(bank[P_TR_BANK[h]][:, n * P:(n + 1) * P], prob[:, h, n * P:(n + 1) * P], ident)
                    mm.then_inc(p_tr.sem, 1)

            def gate_value_rows(L):
                pe.wait_ge(p_copied.sem, p_copied.at(L, 3))
                pe.wait_ge(gm_v.sem, gm_v.at(L, 3))
                for c in range(GT):
                    for t in range(2):
                        mm = pe.transpose(bank[2][:, t * 2 * P + c * P:t * 2 * P + (c + 1) * P], z_w[:, c, t * P:(t + 1) * P], ident)
                mm.then_inc(gm_tr.sem, 1)
                for c in range(GT):
                    mm = pe.transpose(bank[6][0:NS, c * P:(c + 1) * P], z_w[:, c, SEQ:TOK], ident)
                mm.then_inc(gm_tr.sem, 1)

            def prompt_attention(L):
                pe.wait_ge(p_copied.sem, p_copied.at(L, 4))
                pe.wait_ge(v_copied.sem, v_copied.at(L, 1))
                for c in range(GT):
                    for h2 in range(2):
                        h, lanes = 2 * c + h2, slice(64 * h2, 64 * h2 + 64)
                        for t in range(2):
                            for kt in range(t + 1):
                                mm = pe.matmul(bank[4 + c][lanes, t * P:(t + 1) * P], v_tok[:, kt, h * 64:(h + 1) * 64],
                                               prob_t[:, h, (t + kt) * P:(t + kt + 1) * P], start=kt == 0, stop=kt == t)
                    mm.then_inc(p_att.sem, 1)

            def spatial_gates(L):
                pe.wait_ge(sp_ok.sem, sp_ok.at(L, 4))
                pe.wait_ge(v_copied.sem, v_copied.at(L, 2))
                pe.wait_ge(gm_copied.sem, gm_copied.at(L, 2))
                sel = views["gsel"].rearrange("p (c n) -> p c n", c=GT)
                for c in range(GT):
                    pe.matmul(bank[c][:, 0:TOK], sel[0:HEADS, c, :], bias_sp[:, :], start=True, stop=False, skip_group_check=True)
                    for h2 in range(2):
                        g, lanes = 2 * c + h2, slice(64 * h2, 64 * h2 + 64)
                        for t in range(2):
                            pe.matmul(bank[c][lanes, t * P:(t + 1) * P], w_tok[:, t, g * 64:(g + 1) * 64], w_sp[:, g, :],
                                      start=False, stop=False, skip_group_check=True)
                        mm = pe.matmul(bank[c][lanes, SEQ:TOK], w_tok_s[:, g * 64:(g + 1) * 64],
                                       w_sps[:, g, :, :].rearrange("p b t -> p (b t)"),
                                       start=False, stop=h2 == 1, skip_group_check=True)
                    mm.then_inc(gm_mm.sem, 1)

            def batch_probabilities(L):
                pe.wait_ge(s_norm.sem, s_norm.at(L, 3))
                pe.wait_ge(gm_copied.sem, gm_copied.at(L, 2))
                pe.wait_ge(cv_rt.sem, cv_rt.at(L, 1))
                for g in range(2):
                    for n in range(PAGES):
                        pe.transpose(bank[6 + g][:, n * P:(n + 1) * P], prob_s[:, g, n * P:(n + 1) * P], ident)
                    pe.transpose(bank[6 + g][0:NS, PAST:PAST + P], prob_new[:, g, :, :].rearrange("p b t -> p (b t)"),
                                 ident).then_inc(s_tr.sem, 1)

            def batch_attention(L):
                for g in range(2):
                    pe.wait_ge(s_copied.sem, s_copied.at(L, 2 * g + 2))
                    pe.matmul(bank[2 + g][:, 0:GT * P], prob_nt[:, g, :], v_tok_s[:, :], start=True, stop=False, skip_group_check=True)
                    for b4 in range(4):
                        for n in range(PAGES):
                            mm = pe.matmul(bank[2 + g][32 * b4:32 * b4 + 32, 0:GT * P],
                                           prob_st[:, g, n * P + 32 * b4:n * P + 32 * b4 + 32],
                                           v_past[:, (4 * g + b4) * PAGES + n, :], start=False,
                                           stop=b4 == 3 and n == PAGES - 1, skip_group_check=True)
                    mm.then_inc(s_out.sem, 1)

            def batch_attention_transposes(L):
                pe.wait_ge(s_out_ok.sem, s_out_ok.at(L, 2))
                for c in range(GT):
                    for g in range(2):
                        mm = pe.transpose(bank[6][:, (2 * c + g) * P:(2 * c + g + 1) * P], out_s[:, g, c * P:(c + 1) * P], ident)
                mm.then_inc(s_out_tr.sem, 1)

            def pool_map(L):
                pe.wait_ge(s_out_ok.sem, s_out_ok.at(L, 2))
                pe.wait_ge(pool_step.sem, pool_step.at(L, pool_step.per))
                for c in range(GT):
                    pe.matmul(bank[(7, 3)[c]][:, 0:TOK], w_pool[:, c, :], pool_m[:, c, :], start=True, stop=True).then_inc(pool_mm.sem, 1)

            def conv_map(L):
                pe.wait_ge(mix_ok.sem, mix_ok.at(L, 2))
                pe.wait_ge(cv_act.sem, cv_act.at(L, 2))
                for m in range(GT):
                    for c in range(GT):
                        mm = pe.matmul(bank[4 + m][:, 0:TOK], w_pw[:, c, m * P:(m + 1) * P], conv_y[:, c, :], start=c == 0, stop=c == 1)
                    mm.then_inc(cv_pw.sem, 1)

            with pe.Fori(0, DEPTH) as L:
                gate_up(L, BASE_G1, T_G1, 0)
                down(L, BASE_D1, T_D1, 0)
                columns(L, BASE_I, T_I, 1, 0, first=True)
                columns(L, BASE_I, T_I, 1, 1)
                pe.wait_ge(small_in.sem, small_in.at(L, small_in.per))
                column(L, BASE_I, T_I, 1, 2, 0)
                column(L, BASE_I, T_I, 1, 2, 1)
                qk_sums(L)
                column(L, BASE_I, T_I, 1, 2, 2)
                column(L, BASE_I, T_I, 1, 2, 3)
                qk_spread(L)
                column(L, BASE_I, T_I, 1, 3, 0)
                prompt_scores(L)
                column(L, BASE_I, T_I, 1, 3, 1)
                batch_scores(L)
                gate_square_sum(L)
                column(L, BASE_I, T_I, 1, 3, 2)
                conv_mean(L)
                column(L, BASE_I, T_I, 1, 3, 3)
                prompt_attention_transposes(L)
                value_rows(L)
                conv_variance(L)
                gate_value_rows(L)
                prompt_attention(L)
                batch_probabilities(L)
                spatial_gates(L)
                batch_attention(L)
                conv_map(L)
                pool_map(L)
                batch_attention_transposes(L)
                with pe.Fori(0, IT_O) as i:
                    for j in range(4):
                        bank_free(L, i * 4 + (T_O + j))
                        counts = dict(MIX_ORDER)
                        ready = (lambda n, k: pe.wait_ge(mix_ok.sem, mix_ok.at(L, counts[k]))) if j == 0 else None
                        use_slot(L, BASE_O, i, j, bank[j][:, 0:TOK], [k for k, _ in MIX_ORDER], mix_hi, mix_lo, True, True, ready)
                gate_up(L, BASE_G2, T_G2, 2)
                down(L, BASE_D2, T_D2, 1)

        @block.scalar
        def _(act):
            act.sem_inc(states_out.sem, 16)

            def root_of_norm(L, n):
                act.wait_ge(norm_sum.sem, norm_sum.at(L, n + 1))
                act.activation(root[:, :], bank[6][:, 0:TOK], ACT.Sqrt, bias=eps_rms, scale=1.0 / D_MODEL).then_inc(norm_root.sem, 1)

            def round_input(gain_col, d):
                act.activation(xg_hi[:, bass.ds(d, 1), :].rearrange("p a t -> p (a t)"), x[:, bass.ds(d, 1), :].rearrange("p a t -> p (a t)"),
                               ACT.Identity, scale=gain[:, bass.ds(gain_col, 1)]).then_inc(xg_hi_ok.sem, 1)

            def norm_input(gain_col, d, e, sum_count):
                round_input(gain_col, d)
                hold(act, summed.sem, sum_count)
                act.activation(square[:, e, :], x[:, bass.ds(d, 1), :].rearrange("p a t -> p (a t)"), ACT.Square).then_inc(squared.sem, 1)

            def round_slot(L, base, i, j, halves):
                count = halves[j][1]
                act.wait_ge(raw_in[j].sem, L * raw_in[j].per + (base + i) * 16 + 16)
                act.wait_ge(slots.sem, L * slots.per + (base + i) * 4 + j + 1)
                act.activation(w_hi[:, j, 0:count * P], raw[:, j, 0:count * P], ACT.Copy).then_inc(split_hi.sem, 1)

            def silu(L, i, m, tile0):
                act.wait_ge(taken.sem, L * taken.per + i * 4 + (tile0 + 2 * m + 1 + taken.head))
                act.activation(tmp[:, 2 + m, :], tmp[:, m, :], ACT.Silu).then_inc(silu_ok.sem, 1)

            def round_h(L, i, m, ffn):
                hold(act, h_ok.sem, L * h_ok.per + i * 2 + (ffn * FT + m + 1))
                act.activation(h_hi[:, bass.ds(i * 2 + m, 1), :].rearrange("p a t -> p (a t)"), tmp[:, 6 + m, :],
                               ACT.Copy).then_inc(h_hi_ok.sem, 1)

            def gate_up(L, base, tile0, ffn):
                def step(i, base_next, i_next, halves):
                    for m in range(2):
                        round_slot(L, base_next, i_next, 2 * m, halves)
                        silu(L, i, m, tile0)
                        round_slot(L, base_next, i_next, 2 * m + 1, halves)
                        round_h(L, i, m, ffn)

                act.preload_act_table(ACT.Silu)
                with act.Fori(0, IT_G - 1) as i:
                    step(i, base, i + 1, HALVES8)
                step(IT_G - 1, base + IT_G, 0, HALVES11)

            def norm_tile(L, tile0, norm, d, e):
                hold(act, taken.sem, L * taken.per + d + (tile0 + 1 + taken.head))
                norm_input(L * (3 * DT) + d + norm * DT, d, e, L * summed.per + d + norm * (DT + 1))

            def down(L, base, tile0, norm, last):
                def step(i, e):
                    for j in range(4):
                        round_slot(L, base, i + 1, j, HALVES11)
                    norm_tile(L, tile0, norm, i, e)

                act.preload_act_table(ACT.Sqrt)
                with act.Fori(0, DT // 2 - 1) as i2:
                    for e in range(2):
                        step(i2 * 2 + e, e)
                step(DT - 2, 0)
                for j in range(4):
                    if last:
                        round_slot(L + 1, BASE_G1, 0, j, HALVES8)
                    else:
                        round_slot(L, BASE_I, 0, j, HALVES8)
                norm_tile(L, tile0, norm, DT - 1, 1)

            eps_rms, eps_ln = stat[:, 60:61], stat[:, 61:62]
            act.wait_ge(filled.sem, 1)
            act.wait_ge(gain_in.sem, 16)
            act.preload_act_table(ACT.Sqrt)
            round_slot(0, BASE_G1, 0, 0, HALVES8)
            for d in range(DT):
                if d % (DT // 2) == 0:
                    act.wait_ge(x_in[d // (DT // 2)].sem, 16)
                round_input(d, d)
            for d in range(DT // 2):
                act.activation(tmp[:, d, :], x[:, d, :], ACT.Square).then_inc(squared_first.sem, 1)
            act.dma_start(cst[:, :], consts).then_inc(consts_in.sem, 16)
            act.dma_start(vec[:, :], vecs).then_inc(consts_in.sem, 16)
            act.dma_start(page_row[:, :], pages).then_inc(consts_in.sem, 16)
            for j in range(1, 4):
                round_slot(0, BASE_G1, 0, j, HALVES8)

            with act.Fori(0, DEPTH) as L:
                root_of_norm(L, 0)
                gate_up(L, BASE_G1, T_G1, 0)
                down(L, BASE_D1, T_D1, 1, False)
                root_of_norm(L, 1)
                def sigmoid(c):
                    act.wait_ge(taken.sem, taken.at(L, T_I + 2 * c + 2))
                    act.activation(z_g[:, c, :], z_g[:, c, :], ACT.Sigmoid).then_inc(glu_sig.sem, 1)

                round_slot(L, BASE_I, 1, 0, HALVES8)
                round_slot(L, BASE_I, 1, 1, HALVES8)
                sigmoid(0)
                round_slot(L, BASE_I, 1, 2, HALVES8)
                sigmoid(1)
                round_slot(L, BASE_I, 1, 3, HALVES8)
                for t in range(4):
                    round_slot(L, BASE_I, 2, t, HALVES8)
                    act.wait_ge(taken.sem, taken.at(L, T_I + 4 + t + 1))
                    act.activation(qk_square[:, t, :], qk[:, t, :], ACT.Square).then_inc(qk_sq.sem, 1)
                round_slot(L, BASE_I, 3, 0, HALVES8)
                round_slot(L, BASE_I, 3, 1, HALVES8)
                act.wait_ge(qk_sum.sem, qk_sum.at(L, 1))
                act.activation(qk_root, bank[4][0:8, 0:TOK], ACT.Sqrt, bias=eps_rms[0:8, :], scale=1.0 / HEAD).then_inc(qk_rt.sem, 1)
                round_slot(L, BASE_I, 3, 2, HALVES8)
                round_slot(L, BASE_I, 3, 3, HALVES8)

                def gelu(z, tile):
                    act.wait_ge(taken.sem, taken.at(L, tile + 1))
                    act.activation(z, z, ACT.Gelu_apprx_tanh).then_inc(gelu_ok.sem, 1)

                for c in range(GT):
                    gelu(z_w[:, c, :], T_I + 9 + 2 * c)
                for c in range(GT):
                    act.wait_ge(gelu_ok.sem, gelu_ok.at(L, c + 1))
                    act.activation(gm_sq[:, c, :], z_w[:, c, :], ACT.Square).then_inc(gm_sq_ok.sem, 1)
                round_slot(L, BASE_O, 0, 0, HALVES8)
                gelu(z_u[:, 0, :], T_I + 12)
                act.wait_ge(p_max.sem, p_max.at(L, 3))
                for t in range(2):
                    for h in range(HEADS):
                        cols = slice(t * P, t * P + (t + 1) * P)
                        act.activation(prob[:, h, cols], prob[:, h, cols], ACT.Exp, bias=stat[:, 8 + 4 * t + h:9 + 4 * t + h],
                                       scale=SCALE, accum_out=stat[:, 16 + 4 * t + h:17 + 4 * t + h]).then_inc(p_exp.sem, 1)
                round_slot(L, BASE_O, 0, 1, HALVES8)
                act.wait_ge(s_max.sem, s_max.at(L, 2))
                for g in range(2):
                    act.activation(prob_s[:, g, :], prob_s[:, g, :], ACT.Exp, bias=stat[:, 34 + g:35 + g], scale=SCALE,
                                   accum_out=stat[:, 36 + g:37 + g]).then_inc(s_exp.sem, 1)
                act.wait_ge(gm_sum.sem, gm_sum.at(L, 1))
                act.activation(gm_root[:, :], bank[6][:, 0:TOK], ACT.Sqrt, bias=eps_rms, scale=1.0 / (GT * P)).then_inc(gm_rt.sem, 1)
                round_slot(L, BASE_O, 0, 2, HALVES8)
                for c in range(GT):
                    act.wait_ge(cv_cent.sem, cv_cent.at(L, c + 1))
                    act.activation(conv_sq[:, c, :], conv_y[:, c, :], ACT.Square).then_inc(cv_sq.sem, 1)
                for h in range(HEADS):
                    act.wait_ge(p_tr.sem, p_tr.at(L, h + 1))
                    act.activation(prob_t[:, h, :], bank[P_TR_BANK[h]][:, 0:3 * P], ACT.Copy).then_inc(p_copied.sem, 1)
                act.wait_ge(v_tr.sem, v_tr.at(L, 1))
                act.activation(v_tok[:, :, :].rearrange("p t n -> p (t n)"), bank[3][:, :], ACT.Copy).then_inc(v_copied.sem, 1)
                act.wait_ge(v_tr.sem, v_tr.at(L, 2))
                act.activation(v_tok_s[:, :], bank[1][0:NS, 0:GT * P], ACT.Copy).then_inc(v_copied.sem, 1)
                act.wait_ge(cv_var.sem, cv_var.at(L, 1))
                act.activation(conv_root[:, :], bank[7][:, 0:TOK], ACT.Sqrt, bias=eps_ln, scale=1.0 / (GT * P)).then_inc(cv_rt.sem, 1)
                act.wait_ge(gm_tr.sem, gm_tr.at(L, 1))
                act.activation(w_tok[:, :, :].rearrange("p t n -> p (t n)"), bank[2][:, :], ACT.Copy).then_inc(gm_copied.sem, 1)
                act.wait_ge(gm_tr.sem, gm_tr.at(L, 2))
                act.activation(w_tok_s[:, :], bank[6][0:NS, 0:GT * P], ACT.Copy).then_inc(gm_copied.sem, 1)
                round_slot(L, BASE_O, 0, 3, HALVES8)
                for c in range(GT):
                    act.wait_ge(p_att.sem, p_att.at(L, c + 1))
                    act.activation(mix_hi[:, c, 0:SEQ], bank[4 + c][:, 0:SEQ], ACT.Copy).then_inc(p_att_hi.sem, 1)
                for g in range(2):
                    act.wait_ge(s_tr.sem, s_tr.at(L, g + 1))
                    act.activation(prob_st[:, g, :], bank[6 + g][:, 0:PAST], ACT.Copy).then_inc(s_copied.sem, 1)
                    act.activation(prob_nt[:, g, :], bank[6 + g][0:NS, PAST:PAST + P], ACT.Copy).then_inc(s_copied.sem, 1)
                gelu(z_u[:, 1, :], T_I + 14)
                for c in range(GT):
                    hold(act, cv_ln.sem, cv_ln.at(L, c + 2))
                    act.activation(conv_y[:, c, :], conv_y[:, c, :], ACT.Silu, scale=vec[:, bass.ds(L * NV + (V_LG + c), 1)],
                                   bias=vec[:, bass.ds(L * NV + (V_LB + c), 1)]).then_inc(cv_act.sem, 1)
                for c in range(GT):
                    act.wait_ge(gm_ok.sem, gm_ok.at(L, c + 1))
                    act.activation(mix_hi[:, 6 + c, :], gated[:, c, :], ACT.Copy).then_inc(gm_hi.sem, 1)
                for g in range(2):
                    act.wait_ge(s_out.sem, s_out.at(L, g + 1))
                    act.activation(out_s[:, g, :], bank[2 + g][:, 0:GT * P], ACT.Copy).then_inc(s_out_ok.sem, 1)
                for c in range(GT):
                    hold(act, pool_mm.sem, pool_mm.at(L, c + 1))
                    act.activation(mix_hi[:, 2 + c, :], bank[(7, 3)[c]][:, 0:TOK], ACT.Identity,
                                   scale=vec[:, bass.ds(L * NV + (V_PS + c), 1)]).then_inc(pool_hi.sem, 1)
                for c in range(GT):
                    act.wait_ge(cv_pw.sem, cv_pw.at(L, c + 1))
                    act.activation(mix_hi[:, 4 + c, :], bank[4 + c][:, 0:TOK], ACT.Copy).then_inc(cv_hi.sem, 1)
                act.wait_ge(s_att.sem, s_att.at(L, 4))
                act.activation(mix_hi[:, 0:2, SEQ:TOK], att_s[:, :, :], ACT.Copy).then_inc(s_att_hi.sem, 1)
                for i in range(IT_O):
                    for j in range(4):
                        base_next, i_next = ((BASE_O, 1), (BASE_G2, 0))[i]
                        round_slot(L, base_next, i_next, j, HALVES8)
                        norm_tile(L, T_O, 2, 4 * i + j, j % 2)
                root_of_norm(L, 2)
                hold(act, states_out.sem, states_out.at(L, states_out.per))
                gate_up(L, BASE_G2, T_G2, 1)
                down(L, BASE_D2, T_D2, 3, True)

        @block.vector
        def _(dve):
            dve.sem_inc(taken.sem, 4)
            for n, (ap, value) in enumerate(((stat[:, 60:61], RMS_EPS), (stat[:, 61:62], LN_EPS), (ones[:, :], 1.0), (q_pad[:, :, :, :], 0.0),
                                             (conv_in[:, :, 0:CONV_HIST], 0.0), (pool_in[:, :, 0:POOL_HIST], 0.0))):
                last = dve.memset(ap, value)
            last.then_inc(filled.sem, 1)
            dve.memset(sumsq[:, :], 0.0).then_inc(summed.sem, 1)
            dve.wait_ge(gain_in.sem, 16)
            for n in range(2):
                dve.wait_ge(x_in[n].sem, 16)

            def input_rest(gain_col, d, tile_count):
                one = x[:, bass.ds(d, 1), :].rearrange("p a t -> p (a t)")
                dve.wait_ge(xg_hi_ok.sem, tile_count + 1)
                dve.scalar_tensor_tensor(out=xg_lo[:, bass.ds(d, 1), :].rearrange("p a t -> p (a t)"), in0=one,
                                         scalar=gain[:, bass.ds(gain_col, 1)],
                                         in1=xg_hi[:, bass.ds(d, 1), :].bitcast(F32).rearrange("p a t -> p (a t)"),
                                         op0=ALU.mult, op1=ALU.subtract).then_inc(xg_lo_ok.sem, 1)

            def add_square(squares, signal, tile_count, sum_count):
                dve.wait_ge(signal.sem, tile_count + 1)
                dve.wait_ge(summed.sem, sum_count + 1)
                dve.tensor_tensor(sumsq[:, :], sumsq[:, :], squares, ALU.add).then_inc(summed.sem, 1)

            def invert_norm(L, n):
                dve.wait_ge(norm_root.sem, norm_root.at(L, n + 1))
                dve.reciprocal(rms[:, :], root[:, :]).then_inc(norm_ok.sem, 1)
                dve.memset(sumsq[:, :], 0.0).then_inc(summed.sem, 1)
                hold(dve, norm_ok.sem, norm_ok.at(L, n + 1))

            def gate_up_step(L, base, tile0, ffn, i):
                for m in range(2):
                    f = L * (2 * FT) + i * 2 + (ffn * FT + m + 1)
                    tiles = L * TILES + i * 4 + (tile0 + 2 * m + taken.head)
                    done = L * slots.per + i * 4 + (4 * base + 2 * m + slots.head)
                    dve.wait_ge(slots.sem, done + 1)
                    dve.tensor_tensor(tmp[:, m, :], bank[2 * m][:, 0:TOK], rms[:, :], ALU.mult).then_inc(taken.sem, 1)
                    dve.wait_ge(slots.sem, done + 2)
                    dve.tensor_tensor(tmp[:, 4 + m, :], bank[2 * m + 1][:, 0:TOK], rms[:, :], ALU.mult).then_inc(taken.sem, 1)
                    dve.wait_ge(silu_ok.sem, f)
                    dve.wait_ge(taken.sem, tiles + 2)
                    dve.tensor_tensor(tmp[:, 6 + m, :], tmp[:, 2 + m, :], tmp[:, 4 + m, :], ALU.mult).then_inc(h_ok.sem, 1)
                    dve.wait_ge(h_hi_ok.sem, f)
                    dve.tensor_tensor(h_lo[:, bass.ds(i * 2 + m, 1), :].rearrange("p a t -> p (a t)"), tmp[:, 6 + m, :],
                                      h_hi[:, bass.ds(i * 2 + m, 1), :].bitcast(F32).rearrange("p a t -> p (a t)"),
                                      ALU.subtract).then_inc(h_lo_ok.sem, 1)

            def gate_up(L, base, tile0, ffn):
                with dve.Fori(0, IT_G) as i:
                    gate_up_step(L, base, tile0, ffn, i)

            def residual(L, base, tile0, norm, factor, tiles_an_iteration, banks):
                n_banks = len(banks)
                with dve.Fori(0, DT // n_banks) as i:
                    for e in range(n_banks):
                        d = i * n_banks + e
                        slots_a_tile = 4 // tiles_an_iteration
                        dve.wait_ge(slots.sem, L * slots.per + d * slots_a_tile + (4 * base + slots_a_tile + slots.head))
                        one = x[:, bass.ds(d, 1), :].rearrange("p a t -> p (a t)")
                        dve.scalar_tensor_tensor(out=one, in0=bank[banks[e]][:, 0:TOK], scalar=factor, in1=one,
                                                 op0=ALU.mult, op1=ALU.add).then_inc(taken.sem, 1)
                        input_rest(L * (3 * DT) + d + norm * DT, d, L * (3 * DT) + d + norm * DT)
                        add_square(square[:, e % 2, :], squared, L * (3 * DT) + d + (norm - 1) * DT, L * summed.per + d + norm * (DT + 1))

            for d in range(DT):
                input_rest(d, d, d)
            for d in range(DT):
                signal, first = (squared_first, 0) if d < DT // 2 else (squared_too, DT // 2)
                add_square(tmp[:, d, :], signal, d - first, d)

            def take(L, t, dst, b=None):
                dve.wait_ge(slots.sem, slots.at(L, 4 * BASE_I + t + 1))
                dve.tensor_tensor(dst, bank[t % 4][:, 0:TOK], rms[:, :], ALU.mult).then_inc(taken.sem, 1)

            def history(c):
                return split_tokens(conv_in[:, c, :], CONV_HIST + DEC_T, CONV_HIST)[1]

            def prompt_tap(L, k, c):
                dve.wait_ge(taps.sem, L * taps.per + k * GT + (c - 1))
                out = conv_y[:, c, 0:SEQ] if isinstance(k, int) and k == CONV_W - 1 else conv_sum[:, c, :]
                dve.scalar_tensor_tensor(out=out, in0=conv_in[:, c, bass.ds(k, SEQ)],
                                         scalar=vec[:, bass.ds(L * NV + k * GT + (V_CW + c), 1)],
                                         in1=conv_sum[:, c, :], op0=ALU.mult, op1=ALU.add).then_inc(taps.sem, 1)

            def prompt_taps(L, k0, k1):
                if k0 == 0:
                    for c in range(GT):
                        dve.wait_ge(glu_ok.sem, glu_ok.at(L, 2 * c + 1))
                        dve.tensor_scalar(conv_sum[:, c, :], conv_in[:, c, 0:SEQ], vec[:, bass.ds(L * NV + (V_CW + c), 1)],
                                          vec[:, bass.ds(L * NV + (V_CB + c), 1)], ALU.mult, ALU.add).then_inc(taps.sem, 1)
                    k0 = 1
                assert (k1 - k0) % 5 == 0
                with dve.Fori(0, (k1 - k0) // 5) as i:
                    for u in range(5):
                        for c in range(GT):
                            prompt_tap(L, i * 5 + (k0 + u), c)

            def history_tap(L, k, c):
                y = batch(conv_y[:, c, SEQ:TOK])
                weight = vec[:, bass.ds(L * NV + k * GT + (V_CW + c), 1)]
                window = history(c)[:, :, bass.ds(k, DEC_T)]
                if isinstance(k, int) and k == 0:
                    dve.tensor_scalar(y, window, weight, vec[:, bass.ds(L * NV + (V_CB + c), 1)], ALU.mult, ALU.add).then_inc(batch_taps.sem, 1)
                else:
                    dve.wait_ge(batch_taps.sem, L * batch_taps.per + k * GT + (c - 1))
                    dve.scalar_tensor_tensor(out=y, in0=window, scalar=weight, in1=y, op0=ALU.mult, op1=ALU.add).then_inc(batch_taps.sem, 1)

            def gate_up_and_history(L, base, tile0, ffn):
                gate_up_step(L, base, tile0, ffn, 0)
                dve.wait_ge(small_in.sem, small_in.at(L, small_in.per))
                dve.wait_ge(consts_in.sem, 48)
                for c in range(GT):
                    history_tap(L, 0, c)
                with dve.Fori(1, IT_G) as i:
                    gate_up_step(L, base, tile0, ffn, i)
                    for u in range(2):
                        for c in range(GT):
                            history_tap(L, i * 2 + (u - 1), c)
                for k in range(2 * IT_G - 1, CONV_HIST - DEC_T + 1):
                    for c in range(GT):
                        history_tap(L, k, c)

            with dve.Fori(0, DEPTH) as L:
                invert_norm(L, 0)
                gate_up_and_history(L, BASE_G1, T_G1, 0)
                dve.tensor_tensor(w_sp[:, :, :], w_sp[:, :, :], views["tril"].rearrange("p (g t) -> p g t", g=1).to_broadcast([P, HEADS, P]),
                                  ALU.mult).then_inc(sp_ok.sem, 1)
                dve.tensor_copy(bias_sp[:, 0:SEQ].rearrange("p (n t) -> p n t", n=2),
                                b_sp[:, :].rearrange("p (n t) -> p n t", n=1).to_broadcast([HEADS, 2, P])).then_inc(sp_ok.sem, 1)
                dve.tensor_copy(batch(bias_sp[:, SEQ:TOK]),
                                b_sp[:, 0:DEC_T].rearrange("p (n t) -> p n t", n=1).to_broadcast([HEADS, DEC_B, DEC_T])).then_inc(sp_ok.sem, 1)
                residual(L, BASE_D1, T_D1, 1, 0.5, 1, (4, 5))
                invert_norm(L, 1)
                for c in range(GT):
                    take(L, 2 * c, z_a[:, c, :])
                    take(L, 2 * c + 1, z_g[:, c, :])
                for c in range(GT):
                    dve.wait_ge(glu_sig.sem, glu_sig.at(L, c + 1))
                    dve.tensor_tensor(conv_in[:, c, CONV_HIST:CONV_HIST + SEQ], z_a[:, c, 0:SEQ], z_g[:, c, 0:SEQ], ALU.mult).then_inc(glu_ok.sem, 1)
                    dve.tensor_tensor(history(c)[:, :, CONV_HIST:], batch(z_a[:, c, SEQ:TOK]), batch(z_g[:, c, SEQ:TOK]), ALU.mult).then_inc(glu_ok.sem, 1)

                def take_pool(c):
                    dve.wait_ge(slots.sem, slots.at(L, 4 * BASE_I + 8 + 2 * c + 1))
                    dve.tensor_tensor(pool_in[:, c, POOL_HIST:POOL_HIST + SEQ], bank[2 * c][:, 0:SEQ], rms[:, 0:SEQ], ALU.mult)
                    _, rows = split_tokens(pool_in[:, c, :], POOL_HIST + DEC_T, POOL_HIST)
                    dve.tensor_tensor(rows[:, :, POOL_HIST:], batch(bank[2 * c][:, SEQ:TOK]), batch(rms[:, SEQ:TOK]), ALU.mult).then_inc(taken.sem, 1)

                prompt_taps(L, 0, 11)
                take(L, 4, qk[:, 0, :])
                take(L, 5, qk[:, 1, :])
                take(L, 6, qk[:, 2, :])
                prompt_taps(L, 11, 16)
                take(L, 7, qk[:, 3, :])
                prompt_taps(L, 16, 21)
                take_pool(0)
                take(L, 9, z_w[:, 0, :])
                dve.wait_ge(qk_rt.sem, qk_rt.at(L, 1))
                dve.reciprocal(qk_root, qk_root).then_inc(qk_inv.sem, 1)
                take_pool(1)
                take(L, 11, z_w[:, 1, :])
                for t in range(4):
                    dve.wait_ge(qk_rep.sem, qk_rep.at(L, t + 1))
                    dve.scalar_tensor_tensor(out=qk[:, t, :], in0=qk[:, t, :], scalar=vec[:, bass.ds(L * NV + (V_QG, V_KG)[t % 2], 1)],
                                             in1=bank[QK_BANK[t]][:, 0:TOK], op0=ALU.mult, op1=ALU.mult).then_inc(qk_ok.sem, 1)
                dve.wait_ge(qk_ok.sem, qk_ok.at(L, 4))
                for c in range(GT):
                    for h2 in range(2):
                        lanes, h = slice(64 * h2, 64 * h2 + 64), 2 * c + h2
                        dve.tensor_copy(q_pad[lanes, c, :, h * DEC_T:(h + 1) * DEC_T], batch(qk[lanes, 2 * c, SEQ:TOK])).then_inc(pads.sem, 1)
                    dve.tensor_copy(k_all[:, c, :, PAST:KEYS], batch(qk[:, 2 * c + 1, SEQ:TOK])).then_inc(pads.sem, 1)
                prompt_taps(L, 21, 26)
                take(L, 12, z_u[:, 0, :])
                for t, h, done in ((1, 1, 4), (1, 3, 4), (0, 0, 6), (0, 1, 6), (0, 2, 6), (0, 3, 6), (1, 0, 8), (1, 2, 8)):
                    cols = slice(t * P, t * P + (t + 1) * P)
                    dve.wait_ge(p_scores.sem, p_scores.at(L, done))
                    dve.scalar_tensor_tensor(out=prob[:, h, cols], in0=views["dist"][:, cols], scalar=2.0 ** (-8.0 * (h + 1) / HEADS) / SCALE,
                                             in1=score(t, h), op0=ALU.mult, op1=ALU.add).then_inc(p_biased.sem, 1)
                dve.wait_ge(p_biased.sem, p_biased.at(L, 8))
                dve.tensor_reduce(stat[:, 0:4], prob[:, :, 0:P], AX.X, ALU.max).then_inc(p_max.sem, 1)
                dve.tensor_reduce(stat[:, 4:8], prob[:, :, P:3 * P], AX.X, ALU.max).then_inc(p_max.sem, 1)
                dve.wait_ge(p_max.sem, p_max.at(L, 2))
                dve.tensor_scalar(stat[:, 8:16], stat[:, 0:8], -SCALE, None, ALU.mult).then_inc(p_max.sem, 1)
                take(L, 13, z_v[:, 0, :])
                for k in range(26, CONV_W):
                    for c in range(GT):
                        prompt_tap(L, k, c)
                for g in range(2):
                    dve.wait_ge(s_scores.sem, s_scores.at(L, g + 1))
                    dve.tensor_tensor(prob_s[:, g, :], bank[4 + g][:, 0:KEYS], views["alibi"], ALU.add).then_inc(s_biased.sem, 1)
                dve.wait_ge(s_biased.sem, s_biased.at(L, 2))
                dve.tensor_reduce(stat[:, 32:34], prob_s[:, :, :], AX.X, ALU.max).then_inc(s_max.sem, 1)
                dve.wait_ge(s_max.sem, s_max.at(L, 1))
                dve.tensor_scalar(stat[:, 34:36], stat[:, 32:34], -SCALE, None, ALU.mult).then_inc(s_max.sem, 1)
                dve.wait_ge(p_exp.sem, p_exp.at(L, 8))
                dve.reciprocal(stat[:, 24:32], stat[:, 16:24]).then_inc(p_norm.sem, 1)
                dve.wait_ge(p_norm.sem, p_norm.at(L, 1))
                for t in range(2):
                    cols, n = slice(t * P, t * P + (t + 1) * P), (t + 1) * P
                    inv = stat[:, 24 + 4 * t:28 + 4 * t].rearrange("p (h n) -> p h n", n=1).to_broadcast([P, HEADS, n])
                    dve.tensor_tensor(prob[:, :, cols], prob[:, :, cols], inv, ALU.mult).then_inc(p_norm.sem, 1)
                take(L, 14, z_u[:, 1, :])
                dve.wait_ge(cv_mean.sem, cv_mean.at(L, 1))
                for c in range(GT):
                    dve.scalar_tensor_tensor(out=conv_y[:, c, :], in0=bank[7][:, 0:TOK], scalar=-1.0 / (GT * P), in1=conv_y[:, c, :],
                                             op0=ALU.mult, op1=ALU.add).then_inc(cv_cent.sem, 1)
                dve.wait_ge(gm_rt.sem, gm_rt.at(L, 1))
                dve.reciprocal(gm_root[:, :], gm_root[:, :]).then_inc(gm_v.sem, 1)
                take(L, 15, z_v[:, 1, :])
                dve.wait_ge(gm_v.sem, gm_v.at(L, 1))
                for c in range(GT):
                    dve.scalar_tensor_tensor(out=z_w[:, c, :], in0=z_w[:, c, :], scalar=vec[:, bass.ds(L * NV + (V_GG + c), 1)],
                                             in1=gm_root[:, :], op0=ALU.mult, op1=ALU.mult).then_inc(gm_v.sem, 1)
                dve.wait_ge(s_exp.sem, s_exp.at(L, 2))
                dve.reciprocal(stat[:, 38:40], stat[:, 36:38]).then_inc(s_norm.sem, 1)
                dve.wait_ge(s_norm.sem, s_norm.at(L, 1))
                dve.tensor_tensor(prob_s[:, :, :], prob_s[:, :, :],
                                  stat[:, 38:40].rearrange("p (g n) -> p g n", n=1).to_broadcast([P, 2, KEYS]), ALU.mult).then_inc(s_norm.sem, 1)
                dve.wait_ge(s_norm.sem, s_norm.at(L, 2))
                dve.tensor_tensor(prob_new[:, :, :, :],
                                  prob_s[:, :, PAST:KEYS].rearrange("p g (b t) -> p g b t", b=1).to_broadcast([P, 2, DEC_B, DEC_T]),
                                  views["newm"].rearrange("p (g b t) -> p g b t", g=2, b=DEC_B), ALU.mult).then_inc(s_norm.sem, 1)
                dve.wait_ge(sp_rep.sem, sp_rep.at(L, 1))
                dve.wait_ge(v_copied.sem, v_copied.at(L, 2))
                dve.tensor_tensor(w_sps[:, :, :, :],
                                  bank[1][0:NS, 256:288].rearrange("p (g b t) -> p g b t", g=HEADS, b=1).to_broadcast([NS, HEADS, DEC_B, DEC_T]),
                                  views["bmask"][0:NS, :].rearrange("p (g b t) -> p g b t", g=1, b=DEC_B).to_broadcast([NS, HEADS, DEC_B, DEC_T]),
                                  ALU.mult).then_inc(sp_ok.sem, 1)
                dve.wait_ge(cv_rt.sem, cv_rt.at(L, 1))
                dve.reciprocal(conv_root[:, :], conv_root[:, :]).then_inc(cv_ln.sem, 1)
                dve.wait_ge(cv_ln.sem, cv_ln.at(L, 1))
                for c in range(GT):
                    dve.tensor_tensor(conv_y[:, c, :], conv_y[:, c, :], conv_root[:, :], ALU.mult).then_inc(cv_ln.sem, 1)
                def low_part(c, out_lo, src, out_hi):
                    dve.tensor_tensor(out_lo, src, out_hi.bitcast(F32), ALU.subtract).then_inc(mix_ok.sem, 1)

                for c in range(GT):
                    dve.wait_ge(p_att_hi.sem, p_att_hi.at(L, c + 1))
                    low_part(c, mix_lo[:, c, 0:SEQ], bank[4 + c][:, 0:SEQ], mix_hi[:, c, 0:SEQ])
                dve.wait_ge(gelu_ok.sem, gelu_ok.at(L, 4))
                for c in range(GT):
                    dve.wait_ge(gm_mm.sem, gm_mm.at(L, c + 1))
                    dve.tensor_tensor(gated[:, c, :], z_u[:, c, :], bank[c][:, 0:TOK], ALU.mult).then_inc(gm_ok.sem, 1)
                for c in range(GT):
                    dve.wait_ge(gm_hi.sem, gm_hi.at(L, c + 1))
                    low_part(c, mix_lo[:, 6 + c, :], gated[:, c, :], mix_hi[:, 6 + c, :])
                for c in range(GT):
                    dve.wait_ge(pool_hi.sem, pool_hi.at(L, c + 1))
                    dve.scalar_tensor_tensor(out=mix_lo[:, 2 + c, :], in0=bank[(7, 3)[c]][:, 0:TOK],
                                             scalar=vec[:, bass.ds(L * NV + (V_PS + c), 1)], in1=mix_hi[:, 2 + c, :].bitcast(F32),
                                             op0=ALU.mult, op1=ALU.subtract).then_inc(mix_ok.sem, 1)
                for c in range(GT):
                    dve.wait_ge(cv_hi.sem, cv_hi.at(L, c + 1))
                    low_part(c, mix_lo[:, 4 + c, :], bank[4 + c][:, 0:TOK], mix_hi[:, 4 + c, :])
                dve.wait_ge(s_out_tr.sem, s_out_tr.at(L, 1))
                for c in range(GT):
                    for h2 in range(2):
                        lanes, h = slice(64 * h2, 64 * h2 + 64), 2 * c + h2
                        src = bank[6][lanes, 2 * c * P:2 * (c + 1) * P].rearrange("p (b n) -> p b n", b=DEC_B)[:, :, h * DEC_T:(h + 1) * DEC_T]
                        dve.tensor_copy(batch(att_s[lanes, c, :]), src).then_inc(s_att.sem, 1)
                dve.wait_ge(s_att_hi.sem, s_att_hi.at(L, 1))
                low_part(0, mix_lo[:, 0:2, SEQ:TOK], att_s[:, :, :], mix_hi[:, 0:2, SEQ:TOK])
                residual(L, BASE_O, T_O, 2, 1.0, 4, (0, 1, 2, 3))
                invert_norm(L, 2)
                hold(dve, states_out.sem, states_out.at(L, states_out.per))
                gate_up(L, BASE_G2, T_G2, 1)
                residual(L, BASE_D2, T_D2, 3, 0.5, 1, (4, 5))


def _constants(np):
    BIG = -1.0e30
    c = {}
    heads = np.kron(np.eye(8), np.ones((1, 64))).reshape(8, 4, P)
    c["hsum"] = heads.transpose(2, 1, 0) * (np.arange(8) // 2 == np.arange(4)[:, None])
    c["hsum"] = c["hsum"].reshape(P, -1)
    c["hrep"] = np.zeros((P, 4 * P))
    c["hrep"][:8] = heads.reshape(8, -1)
    c["ident"] = np.eye(P)
    q = np.arange(P)[:, None]
    first = np.where(q >= np.arange(P), np.arange(P) - q, BIG)
    second = np.where(q + P >= np.arange(2 * P), np.arange(2 * P) - (q + P), BIG)
    c["dist"] = np.concatenate([first, second], 1)
    row = np.arange(P)
    slope = 2.0 ** (-8.0 * ((row // 8) % 4 + 1) / HEADS) / SCALE
    pos = PAST + row % 8
    key = np.arange(KEYS)
    c["alibi"] = np.where(key <= pos[:, None], slope[:, None] * (key - pos[:, None]), BIG)
    b = np.arange(NS) // 8
    c["newm"] = np.concatenate([b[None, :] == (4 * g + row // 32)[:, None] for g in range(2)], 1)
    c["bmask"] = np.zeros((P, NS))
    c["bmask"][:NS] = b[:, None] == b[None, :]
    c["e8"] = np.zeros((P, NS))
    c["e8"][:8] = np.arange(8)[:, None] == (np.arange(NS) % 8)[None, :]
    gsel = np.zeros((P, GT, P))
    for g in range(HEADS):
        gsel[g, g // 2, 64 * (g % 2):64 * (g % 2) + 64] = 1
    c["gsel"] = gsel.reshape(P, -1)
    c["tril"] = np.arange(P)[:, None] <= np.arange(P)[None, :]
    first, window = np.zeros((P, GT, POOL_HIST + 1)), np.zeros((P, GT))
    for g, w in enumerate((2, 4, 8, 16)):
        lanes = slice(64 * (g % 2), 64 * (g % 2) + 64)
        first[lanes, g // 2] = 1.0 / np.minimum(np.arange(POOL_HIST + 1) + 1, w)
        window[lanes, g // 2] = 1.0 / w
    c["first"], c["window"] = first.reshape(P, -1), window
    return np.concatenate([np.asarray(c[n], np.float32) for n, _ in CONSTS], 1)


def kernel(**inputs):
    import numpy as np
    import concourse.bacc as bacc
    from concourse.bass_utils import run_bass_kernel_spmd as run

    a = {k: np.asarray(v) for k, v in inputs.items()}
    n_pool = a["cache_k"].shape[1]

    def cols(w):
        d, r, n = w.shape
        return w.reshape(d, r // P, P, n // P, P).transpose(0, 3, 2, 1, 4)

    def halves(first, second):
        both = np.stack([first, second], 2)
        d, it, ab, half = both.shape[:4]
        return both.transpose(0, 1, 2, 4, 3, 5, 6).reshape(d, it, ab, P, -1)

    def gate_up(g, u):
        g, u = cols(g), cols(u)
        pair = lambda w: w.reshape(DEPTH, FT // 2, 2, P, DT, P)
        return halves(pair(g), pair(u))

    def down(w):
        w = cols(w)
        return np.stack([w[:, :, :, :11], w[:, :, :, 11:]], 2).reshape(DEPTH, DT, 2, P, 11 * P)

    w_in = cols(a["w_in"])
    order_a = [8, 9, 0, 1, 6, 7, 12, 13]
    order_b = [10, 11, 2, 3, 14, 15, 4, 5]
    i8 = halves(w_in[:, order_a].reshape(DEPTH, 4, 2, P, DT, P), w_in[:, order_b].reshape(DEPTH, 4, 2, P, DT, P))
    w_out = cols(a["w_out"])[:, :, :, [6, 7, 2, 3, 4, 5, 0, 1]].reshape(DEPTH, 2, 2, 2, P, DT, P)
    o8 = halves(w_out[:, :, :, 0], w_out[:, :, :, 1])
    w8 = np.concatenate([gate_up(a["ffn1_w_gate"], a["ffn1_w_up"]), i8, o8, gate_up(a["ffn2_w_gate"], a["ffn2_w_up"])], 1)
    w11 = np.concatenate([down(a["ffn1_w_down"]), down(a["ffn2_w_down"])], 1)

    gains = np.stack([a["ffn1_norm"], a["mix_norm"], a["ffn2_norm"]], 1).reshape(3 * DEPTH, DT, P)
    gains = np.concatenate([gains, gains[:1]]).transpose(2, 0, 1).reshape(P, -1)
    two = lambda v: v.reshape(DEPTH, GT, P).transpose(2, 0, 1)
    twice = lambda v: np.concatenate([v, v], 1).T[:, :, None]
    conv_w = a["conv_w"].reshape(DEPTH, CONV_W * GT, P).transpose(2, 0, 1)
    vecs = np.concatenate([twice(a["q_norm"]), twice(a["k_norm"]), two(a["pool_scale"]), two(a["conv_b"]), two(a["conv_ln_g"]),
                           two(a["conv_ln_b"]), two(a["gate_norm"]), conv_w], 2).reshape(P, -1)
    pool_w = np.zeros((DEPTH, P, GT, P), np.float32)
    for g in range(4):
        lanes = slice(64 * (g % 2), 64 * (g % 2) + 64)
        pool_w[:, lanes, g // 2, lanes] = a["pool_w"][:, g]
    tok = np.concatenate([a["x_prompt"].reshape(SEQ, D_MODEL), a["x_sample"].reshape(NS, D_MODEL)])
    arrays = {
        "xT": tok.reshape(TOK, DT, P).transpose(2, 1, 0),
        "w8": np.concatenate([w8.reshape(DEPTH * W8_ROWS, 2, P, N8), np.zeros((1, 2, P, N8), np.float32)]),
        "w11": w11.reshape(DEPTH * W11_ROWS, 2, P, N11),
        "gains": gains,
        "vecs": vecs,
        "consts": _constants(np),
        "pool_w": pool_w,
        "conv_pw": a["conv_pw"].reshape(DEPTH, GT, P, GT * P).transpose(0, 2, 1, 3),
        "sp_wT": a["spatial_w"].transpose(0, 3, 1, 2),
        "sp_b": a["spatial_b"],
        "cache_kT": a["cache_k"].reshape(DEPTH, n_pool, PAGE, GT, P).transpose(0, 1, 4, 3, 2),
        "cache_v": a["cache_v"].reshape(DEPTH, n_pool, PAGE, GT * P),
        "conv_hist": a["state_conv"].reshape(DEPTH, DEC_B, CONV_HIST, GT, P).transpose(0, 3, 4, 1, 2),
        "pool_hist": a["state_pool"].reshape(DEPTH, DEC_B, POOL_HIST, GT, P).transpose(0, 3, 4, 1, 2),
        "pages": a["page_table"].reshape(1, DEC_B * PAGES),
    }
    outs = {"yT": [P, DT, TOK], "kT": [DEPTH, GT, P, TOK], "vT": [DEPTH, GT, P, TOK],
            "poolT": [DEPTH, GT, P, POOL_HIST], "pool_sT": [DEPTH, GT, P, DEC_B, POOL_HIST],
            "convT": [DEPTH, GT, P, CONV_HIST], "conv_sT": [DEPTH, GT, P, DEC_B, CONV_HIST],
            "gateT": [DEPTH, GT, P, NS]}
    nc = bacc.Bacc("TRN2", target_bir_lowering=False, num_devices=1)
    args, feed = [], {}
    for name, v in arrays.items():
        v = np.ascontiguousarray(v)
        feed[f"in_{name}"] = v
        args.append(nc.dram_tensor(f"in_{name}", v.shape, mybir.dt.from_np(v.dtype), kind="ExternalInput").ap())
    for name, shape in outs.items():
        args.append(nc.dram_tensor(f"out_{name}", shape, F32, kind="ExternalOutput").ap())
    hybrid_decoder(nc, *args)
    r = run(nc, [feed], core_ids=[0]).results[0]
    o = {name: np.asarray(r[f"out_{name}"]) for name in outs}

    y = o["yT"].transpose(2, 1, 0).reshape(TOK, D_MODEL)
    width = GT * P

    def rows(t):
        return np.ascontiguousarray(t.transpose(0, 3, 1, 2)).reshape(DEPTH, -1, width)

    def state(t):
        return np.ascontiguousarray(t.transpose(0, 3, 4, 1, 2)).reshape(DEPTH, DEC_B, -1, width)

    k, v = rows(o["kT"]), rows(o["vT"])
    prompt = lambda t: t[:, :SEQ].reshape(DEPTH, 1, SEQ, HEADS, HEAD)
    sample = lambda t: t[:, SEQ:].reshape(DEPTH, DEC_B, DEC_T, HEADS, HEAD)
    return (y[:SEQ].reshape(1, SEQ, D_MODEL), y[SEQ:].reshape(DEC_B, DEC_T, D_MODEL),
            prompt(k), prompt(v), sample(k), sample(v),
            rows(o["poolT"]).reshape(DEPTH, 1, POOL_HIST, width), state(o["pool_sT"]),
            rows(o["convT"]).reshape(DEPTH, 1, CONV_HIST, width), state(o["conv_sT"]),
            rows(o["gateT"]).reshape(DEPTH, DEC_B, DEC_T, width))
```
